# Optimizing a Trainium2 kernel written in Bass

```python
import math
import jax, jax.numpy as jnp
from jax import lax
import numpy as np

D_MODEL = 1024
BATCH = 1
SEQ = 256
DEPTH = 1
DEC_BATCH = 8
DEC_SEQ = 1
PAST_LEN = 2048
PAGE_SIZE = 128

N_META = 16
DN_HEADS = 4
DN_DK = 128
DN_DV = 128
DN_QK_W = DN_HEADS * DN_DK
DN_V_W = DN_HEADS * DN_DV
DN_CONV = 4
DN_CHUNK = 64
RW_HEADS = 8
RW_N = 64
RW_W = RW_HEADS * RW_N
RW_W_RANK = 64
RW_A_RANK = 64
RW_G_RANK = 128
PEER_HEADS = 8
PEER_NKEYS = 128
PEER_N = PEER_NKEYS * PEER_NKEYS
PEER_QDIM = 256
PEER_HALF = PEER_QDIM // 2
PEER_TOPK = 16
PEER_BLOCK = 256
NORM_EPS = 1e-6
GN_EPS = 64e-5

N_QKV = 2 * DN_QK_W + DN_V_W
O_Z = N_QKV
O_BETA = O_Z + DN_V_W
O_ALPHA = O_BETA + DN_HEADS
O_RW = O_ALPHA + DN_HEADS
N_RW = 3 * RW_W + RW_W_RANK + RW_A_RANK + RW_G_RANK
O_GATE = O_RW + N_RW
N_IN = O_GATE + 2 * D_MODEL

kernel_name = 'hybrid_deltanet_rwkv7_peer_meta_step'

def rmsnorm(x, g):
    xf = x.astype(jnp.float32)
    y = xf * lax.rsqrt(jnp.mean(xf * xf, -1, keepdims=True) + NORM_EPS) * g.astype(jnp.float32)
    return y.astype(x.dtype)

def l2norm(x):
    xf = x.astype(jnp.float32)
    return xf * lax.rsqrt(jnp.sum(xf * xf, -1, keepdims=True) + 1e-6)

def short_conv(u, buf, w):
    T = u.shape[1]
    up = jnp.concatenate([buf.astype(u.dtype), u], axis=1)
    y = up[:, 0:T] * w[0]
    for j in range(1, DN_CONV):
        y = y + up[:, j:j + T] * w[j]
    return jax.nn.silu(y), up[:, T:]

def dn_step(S, inp):
    q, k, v, g, beta = inp
    S = S * jnp.exp(g)[..., None, None]
    kv = jnp.einsum('bhkv,bhk->bhv', S, k)
    delta = (v - kv) * beta[..., None]
    S = S + k[..., :, None] * delta[..., None, :]
    return S, jnp.einsum('bhkv,bhk->bhv', S, q)

def dn_chunk(S, q, k, v, g, beta):
    L = q.shape[2]
    G = jnp.cumsum(g, -1)
    tri = jnp.tril(jnp.ones((L, L), bool))
    strict = jnp.tril(jnp.ones((L, L), bool), -1)
    decay = jnp.exp(jnp.where(tri, G[..., :, None] - G[..., None, :], -jnp.inf))
    kb = k * beta[..., None]
    A = jnp.where(strict, jnp.einsum('bhik,bhjk->bhij', kb, k) * decay, 0.0) + jnp.eye(L, dtype=q.dtype)
    rhs = jnp.concatenate([v * beta[..., None], kb * jnp.exp(G)[..., None]], -1)
    sol = lax.linalg.triangular_solve(A, rhs, left_side=True, lower=True, unit_diagonal=True)
    u, w = sol[..., :DN_DV], sol[..., DN_DV:]
    v_new = u - jnp.einsum('bhlk,bhkv->bhlv', w, S)
    qk = jnp.where(tri, jnp.einsum('bhik,bhjk->bhij', q, k) * decay, 0.0)
    o = jnp.einsum('bhlk,bhkv->bhlv', q * jnp.exp(G)[..., None], S) + jnp.einsum('bhij,bhjv->bhiv', qk, v_new)
    G_last = G[..., -1:]
    S = S * jnp.exp(G_last)[..., None] + jnp.einsum('bhlk,bhlv->bhkv', k * jnp.exp(G_last - G)[..., None], v_new)
    return S, o

def dn_chunked(S, q, k, v, g, beta, lead):
    B, H, T = g.shape
    S, o_lead = dn_chunk(S, q[:, :, :lead], k[:, :, :lead], v[:, :, :lead], g[:, :, :lead], beta[:, :, :lead])
    nc = (T - lead) // DN_CHUNK

    def split(a):
        a = a[:, :, lead:]
        return jnp.moveaxis(a.reshape((B, H, nc, DN_CHUNK) + a.shape[3:]), 2, 0)

    S, o_rest = lax.scan(lambda s, c: dn_chunk(s, *c), S, tuple(split(a) for a in (q, k, v, g, beta)))
    o_rest = jnp.moveaxis(o_rest, 0, 2).reshape(B, H, nc * DN_CHUNK, DN_DV)
    return S, jnp.concatenate([o_lead, o_rest], axis=2)

def rw_step(S, inp):
    r, w, k, v, a, b = inp
    sa = jnp.einsum('bhvk,bhk->bhv', S, a)
    S = S * w[:, :, None, :] + sa[..., :, None] * b[..., None, :] + v[..., :, None] * k[..., None, :]
    return S, jnp.einsum('bhvk,bhk->bhv', S, r)

def token_mixer(xn, conv_buf, s_dn, shift_buf, s_rw, p, lead):
    B, T, _ = xn.shape
    f32 = jnp.float32
    P = xn @ p['w_in']
    qkv, conv_new = short_conv(P[..., :N_QKV], conv_buf, p['dn_conv_w'])
    q = l2norm(qkv[..., :DN_QK_W].reshape(B, T, DN_HEADS, DN_DK)) * (DN_DK ** -0.5)
    k = l2norm(qkv[..., DN_QK_W:2 * DN_QK_W].reshape(B, T, DN_HEADS, DN_DK))
    v = qkv[..., 2 * DN_QK_W:].reshape(B, T, DN_HEADS, DN_DV).astype(f32)
    beta = jax.nn.sigmoid(P[..., O_BETA:O_ALPHA].astype(f32))
    g = -jnp.exp(p['dn_a_log'].astype(f32)) * jax.nn.softplus(P[..., O_ALPHA:O_RW].astype(f32) + p['dn_dt_bias'])
    S0 = s_dn.astype(f32)
    if lead is None:
        tm = lambda a: jnp.moveaxis(a, 1, 0)
        s_dn_new, o = lax.scan(dn_step, S0, (tm(q), tm(k), tm(v), tm(g), tm(beta)))
        o = jnp.moveaxis(o, 0, 1)
    else:
        hm = lambda a: jnp.moveaxis(a, 2, 1)
        s_dn_new, o = dn_chunked(S0, hm(q), hm(k), hm(v), hm(g), hm(beta), lead)
        o = jnp.moveaxis(o, 1, 2)
    z = P[..., O_Z:O_BETA].reshape(B, T, DN_HEADS, DN_DV).astype(f32)
    o_dn = (rmsnorm(o, p['dn_norm_w']) * jax.nn.silu(z)).reshape(B, T, DN_V_W).astype(xn.dtype)
    prw = P[..., O_RW:O_GATE]
    prev = jnp.concatenate([shift_buf.astype(prw.dtype), prw[:, :-1]], axis=1)
    mix = (prw + (prev - prw) * p['rw_mu']).astype(f32)
    shift_new = prw[:, -1:]
    c0 = 3 * RW_W
    r = mix[..., :RW_W]
    kr = mix[..., RW_W:2 * RW_W]
    vr = mix[..., 2 * RW_W:c0]
    wl = mix[..., c0:c0 + RW_W_RANK]
    al = mix[..., c0 + RW_W_RANK:c0 + RW_W_RANK + RW_A_RANK]
    gl = mix[..., c0 + RW_W_RANK + RW_A_RANK:]
    w_log = -jax.nn.softplus(-(p['rw_w0'] + jnp.tanh(wl) @ p['rw_w2'])) - 0.5
    decay = jnp.exp(-jnp.exp(w_log))
    a = jax.nn.sigmoid(p['rw_a0'] + al @ p['rw_a2'])
    gate = jax.nn.sigmoid(gl) @ p['rw_g2']
    hs = lambda t: t.reshape(B, T, RW_HEADS, RW_N)
    kk = l2norm(hs(kr * p['rw_k_k']))
    kr = kr * (1.0 + (a - 1.0) * p['rw_k_a'])
    r_h, k_h, v_h, a_h, w_h = hs(r), hs(kr), hs(vr), hs(a), hs(decay)
    tm = lambda t: jnp.moveaxis(t, 1, 0)
    s_rw_new, y = lax.scan(rw_step, s_rw.astype(f32), (tm(r_h), tm(w_h), tm(k_h), tm(v_h), tm(-kk), tm(kk * a_h)))
    y = jnp.moveaxis(y, 0, 1)
    mu = jnp.mean(y, -1, keepdims=True)
    var = jnp.mean(jnp.square(y - mu), -1, keepdims=True)
    y = ((y - mu) * lax.rsqrt(var + GN_EPS)).reshape(B, T, RW_W) * p['rw_gn_w'] + p['rw_gn_b']
    bonus = (jnp.sum(r_h * k_h * p['rw_r_k'], -1, keepdims=True) * v_h).reshape(B, T, RW_W)
    o_rw = ((y + bonus) * gate).astype(xn.dtype)
    ga = jax.nn.sigmoid(P[..., O_GATE:O_GATE + D_MODEL])
    gb = jax.nn.sigmoid(P[..., O_GATE + D_MODEL:])
    m = ga * (o_dn @ p['w_up_dn']) + gb * (o_rw @ p['w_up_rw'])
    out = m @ p['w_out']
    return out, (conv_new, s_dn_new.astype(s_dn.dtype), shift_new, s_rw_new.astype(s_rw.dtype))

def peer_ffn(x, wq, keys, u_tab, v_tab):
    M, D = x.shape
    nb = -(-M // PEER_BLOCK)
    xp = jnp.pad(x, ((0, nb * PEER_BLOCK - M), (0, 0))).reshape(nb, PEER_BLOCK, D)
    K = PEER_TOPK

    def block(xb):
        q = (xb @ wq).reshape(PEER_BLOCK, PEER_HEADS, 2, PEER_HALF)
        s = jnp.einsum('thpc,hpnc->thpn', q, keys)
        sv, si = lax.top_k(s, K)
        cand = (sv[:, :, 0, :, None] + sv[:, :, 1, None, :]).reshape(PEER_BLOCK, PEER_HEADS, K * K)
        cidx = (si[:, :, 0, :, None] * PEER_NKEYS + si[:, :, 1, None, :]).reshape(PEER_BLOCK, PEER_HEADS, K * K)
        cv, ci = lax.top_k(cand, K)
        eidx = jnp.take_along_axis(cidx, ci, -1)
        gates = jax.nn.softmax(cv.astype(jnp.float32), -1)
        h = jax.nn.gelu(jnp.einsum('thkd,td->thk', u_tab[eidx], xb).astype(jnp.float32))
        return jnp.einsum('thk,thkd->td', (gates * h).astype(xb.dtype), v_tab[eidx])

    return lax.map(block, xp).reshape(nb * PEER_BLOCK, D)[:M]

def layer(h, states, p, lead):
    conv_buf, s_dn, shift_buf, s_rw = states
    mix, new = token_mixer(rmsnorm(h, p['ln1']), conv_buf, s_dn, shift_buf, s_rw, p, lead)
    h = h + mix.astype(h.dtype)
    B, T, D = h.shape
    f = peer_ffn(rmsnorm(h, p['ln2']).reshape(B * T, D), p['peer_wq'], p['peer_keys'], p['peer_u'], p['peer_v'])
    return h + f.reshape(B, T, D).astype(h.dtype), new

def setup_inputs(seed: int = 0) -> dict:
    key = jax.random.key(seed)
    ks = iter(jax.random.split(key, 48))
    nrm = lambda shape, scale: jax.random.normal(next(ks), shape, jnp.float32) * scale
    L = DEPTH
    d = {}
    d['x_prompt'] = nrm((BATCH, SEQ, D_MODEL), 1.0)
    d['x_sample'] = nrm((DEC_BATCH, DEC_SEQ, D_MODEL), 1.0)
    d['cache_dn_conv'] = nrm((L, DEC_BATCH, DN_CONV - 1, N_QKV), 1.0)
    d['state_dn'] = nrm((L, DEC_BATCH, DN_HEADS, DN_DK, DN_DV), 0.3)
    d['cache_rw_shift'] = nrm((L, DEC_BATCH, 1, N_RW), 1.0)
    d['state_rw'] = nrm((L, DEC_BATCH, RW_HEADS, RW_N, RW_N), 1.0)
    d['meta_tokens'] = nrm((N_META, D_MODEL), 1.0)
    d['ln1'] = 1.0 + nrm((L, D_MODEL), 0.02)
    d['w_in'] = nrm((L, D_MODEL, N_IN), D_MODEL ** -0.5)
    d['dn_conv_w'] = nrm((L, DN_CONV, N_QKV), DN_CONV ** -0.5)
    d['dn_a_log'] = jnp.log(jax.random.uniform(next(ks), (L, DN_HEADS), jnp.float32, 1.0, 16.0))
    dt = jnp.exp(jax.random.uniform(next(ks), (L, DN_HEADS), jnp.float32, math.log(1e-3), math.log(1e-1)))
    d['dn_dt_bias'] = dt + jnp.log(-jnp.expm1(-dt))
    d['dn_norm_w'] = 1.0 + nrm((L, DN_DV), 0.02)
    d['rw_mu'] = jax.random.uniform(next(ks), (L, N_RW), jnp.float32, 0.0, 1.0)
    d['rw_w0'] = jax.random.uniform(next(ks), (L, RW_W), jnp.float32, -6.0, 1.0)
    d['rw_w2'] = nrm((L, RW_W_RANK, RW_W), 0.5 * RW_W_RANK ** -0.5)
    d['rw_a0'] = nrm((L, RW_W), 0.1)
    d['rw_a2'] = nrm((L, RW_A_RANK, RW_W), RW_A_RANK ** -0.5)
    d['rw_g2'] = nrm((L, RW_G_RANK, RW_W), RW_G_RANK ** -0.5)
    d['rw_k_k'] = 0.85 + nrm((L, RW_W), 0.02)
    d['rw_k_a'] = 1.0 + nrm((L, RW_W), 0.02)
    d['rw_r_k'] = nrm((L, RW_HEADS, RW_N), 0.1)
    d['rw_gn_w'] = 1.0 + nrm((L, RW_W), 0.02)
    d['rw_gn_b'] = nrm((L, RW_W), 0.02)
    d['w_up_dn'] = nrm((L, DN_V_W, D_MODEL), DN_V_W ** -0.5)
    d['w_up_rw'] = nrm((L, RW_W, D_MODEL), RW_W ** -0.5)
    d['w_out'] = nrm((L, D_MODEL, D_MODEL), D_MODEL ** -0.5)
    d['ln2'] = 1.0 + nrm((L, D_MODEL), 0.02)
    d['peer_wq'] = nrm((L, D_MODEL, PEER_HEADS * PEER_QDIM), D_MODEL ** -0.5)
    d['peer_keys'] = nrm((L, PEER_HEADS, 2, PEER_NKEYS, PEER_HALF), PEER_HALF ** -0.5)
    d['peer_u'] = nrm((L, PEER_N, D_MODEL), D_MODEL ** -0.5)
    d['peer_v'] = nrm((L, PEER_N, D_MODEL), PEER_HEADS ** -0.5)
    d['ln_f'] = 1.0 + nrm((D_MODEL,), 0.02)
    return d

def reference(x_prompt, x_sample, cache_dn_conv, state_dn, cache_rw_shift, state_rw, meta_tokens, ln1, w_in, dn_conv_w, dn_a_log, dn_dt_bias, dn_norm_w, rw_mu, rw_w0, rw_w2, rw_a0, rw_a2, rw_g2, rw_k_k, rw_k_a, rw_r_k, rw_gn_w, rw_gn_b, w_up_dn, w_up_rw, w_out, ln2, peer_wq, peer_keys, peer_u, peer_v, ln_f):
    Bp = x_prompt.shape[0]
    dt = x_prompt.dtype
    hp = jnp.concatenate([jnp.broadcast_to(meta_tokens.astype(dt), (Bp, N_META, D_MODEL)), x_prompt], axis=1)
    hs = x_sample
    zero_states = (jnp.zeros((Bp, DN_CONV - 1, N_QKV), dt), jnp.zeros((Bp, DN_HEADS, DN_DK, DN_DV), dt),
                   jnp.zeros((Bp, 1, N_RW), dt), jnp.zeros((Bp, RW_HEADS, RW_N, RW_N), dt))
    new_p, new_s = [], []
    for l in range(DEPTH):
        p = dict(ln1=ln1[l], w_in=w_in[l], dn_conv_w=dn_conv_w[l], dn_a_log=dn_a_log[l], dn_dt_bias=dn_dt_bias[l],
                 dn_norm_w=dn_norm_w[l], rw_mu=rw_mu[l], rw_w0=rw_w0[l], rw_w2=rw_w2[l], rw_a0=rw_a0[l],
                 rw_a2=rw_a2[l], rw_g2=rw_g2[l], rw_k_k=rw_k_k[l], rw_k_a=rw_k_a[l], rw_r_k=rw_r_k[l],
                 rw_gn_w=rw_gn_w[l], rw_gn_b=rw_gn_b[l], w_up_dn=w_up_dn[l], w_up_rw=w_up_rw[l], w_out=w_out[l],
                 ln2=ln2[l], peer_wq=peer_wq[l], peer_keys=peer_keys[l], peer_u=peer_u[l], peer_v=peer_v[l])
        hp, st_p = layer(hp, zero_states, p, N_META)
        hs, st_s = layer(hs, (cache_dn_conv[l], state_dn[l], cache_rw_shift[l], state_rw[l]), p, None)
        new_p.append(st_p)
        new_s.append(st_s)
    y_prompt = rmsnorm(hp[:, N_META:], ln_f)
    y_sample = rmsnorm(hs, ln_f)
    p_conv, p_dn, p_shift, p_rw = [jnp.stack(t) for t in zip(*new_p)]
    s_conv, s_dn, s_shift, s_rw = [jnp.stack(t) for t in zip(*new_s)]
    return (y_prompt, y_sample, p_conv, p_dn, p_shift, p_rw, s_conv, s_dn, s_shift, s_rw)


_drawn_inputs = setup_inputs


def setup_inputs(seed=0):
    import zlib

    import numpy as np

    out = dict(_drawn_inputs(seed))
    spreads = {}
    factors = {'rw_k_k': 10.953,
     'rw_k_a': 2.756,
     'rw_gn_w': 3.953,
     'rw_gn_b': 11.059,
     'ln_f': 7.367,
     'dn_norm_w': 6.673,
     'ln2': 3.34}
    for name, (base, spread) in spreads.items():
        noise = np.random.default_rng([zlib.crc32(name.encode()), seed]).standard_normal(out[name].shape)
        drawn = base * np.exp(spread * noise) if base else spread * noise
        out[name] = __import__('jax').numpy.asarray(drawn.astype(out[name].dtype))
    for name, factor in factors.items():
        out[name] = (out[name] * factor).astype(out[name].dtype)
    return out
```

```python
from contextlib import ExitStack

import concourse.bass as bass
from concourse import mybir

F32 = mybir.dt.float32
U32 = mybir.dt.uint32
ALU = mybir.AluOpType
ACT = mybir.ActivationFunctionType
AX = mybir.AxisListType.X

D = 1024
KT = D // 128
SEQ, META, NS = 256, 16, 8
PAD = 16
TC, NCH = 96, 3
NP = TC * NCH
NC = NP + NS
T0 = PAD + META
NX = NC - T0
DH, DK = 4, 128
RH, RN = 8, 64
NQKV, OZ, OBETA, ORW, NRW = 1536, 1536, 2048, 2056, 1792
OGATE = ORW + NRW
PH, PK, PT = 8, 128, 16
SLOT = 4096
NCAND = 54
PAIRS = [(0, 1, 16), (1, 1, 8), (2, 2, 5), (4, 4, 3), (8, 8, 1)]
LEVELS = 6
EDEC = float(2.718281828459045 ** -0.5)
GELU_C = 0.7978845608028654
NEG = -3.0e38

PAR = [("ln1", 8), ("conv", 48), ("mu", 14), ("w0", 4), ("a0", 4), ("k_k", 4), ("k_a", 4), ("r_k", 4),
       ("gn_w", 4), ("gn_b", 4), ("dn_norm", 1)]
PAR_AT = {name: sum(n for _, n in PAR[:i]) for i, (name, _) in enumerate(PAR)}
PAR_ROWS = sum(n for _, n in PAR)


class Steps:

    def __init__(self, eng, sem, base=0):
        self.eng, self.sem, self.n, self.base = eng, sem, 0, base

    def __call__(self, instruction):
        instruction.then_inc(self.sem, 1)
        self.n += 1

    def sync(self, lag=0):
        if self.n > lag:
            self.eng.wait_ge(self.sem, self.base + self.n - lag)


class Signal:

    def __init__(self, sem, before):
        self.sem, self.before = sem, before

    def at(self, n):
        return self.before + n


def series(sem, *counts):
    return [Signal(sem, sum(counts[:i])) for i in range(len(counts))]


def hybrid_step(nc, x_prompt, x_sample, cache_dn_conv, state_dn, cache_rw_shift, state_rw, meta_tokens, ln1, w_in,
                dn_conv_w, dn_a_log, dn_dt_bias, dn_norm_w, rw_mu, rw_w0, rw_w2, rw_a0, rw_a2, rw_g2, rw_k_k,
                rw_k_a, rw_r_k, rw_gn_w, rw_gn_b, w_up_dn, w_up_rw, w_out, ln2, peer_wq, peer_keys, peer_u,
                peer_v, ln_f, y_prompt, y_sample, p_conv, p_dn, p_shift, p_rw, s_conv, s_dn, s_shift, s_rw):
    with ExitStack() as ctx:
        sb_all = ctx.enter_context(nc.sbuf_tensor("sb_all", [128, 52900], F32))
        bank = [ctx.enter_context(nc.psum_tensor(f"bank{i}", [128, 512], F32)) for i in range(8)]

        def sem(name):
            return ctx.enter_context(nc.semaphore(name))

        def view(at, *shape):
            n = 1
            for s in shape:
                n *= s
            v = sb_all[:, at:at + n]
            if len(shape) == 2:
                v = v.rearrange("p (a b) -> p a b", a=shape[0])
            if len(shape) == 3:
                v = v.rearrange("p (a b c) -> p a b c", a=shape[0], b=shape[1])
            return v

        def psv(b, n, *shape, at=0):
            size = 1
            for s in shape:
                size *= s
            v = bank[b][0:n, at:at + size]
            if len(shape) == 2:
                v = v.rearrange("p (a b) -> p a b", a=shape[0])
            if len(shape) == 3:
                v = v.rearrange("p (a b c) -> p a b c", a=shape[0], b=shape[1])
            return v

        def row(v, n, *shape):
            return v.unsqueeze(len(v.shape)).broadcast_to([n, *shape])

        at = [0]

        def take(n):
            at[0] += n
            return at[0] - n

        W = take(3 * SLOT)
        wslot = [view(W + i * SLOT, KT, 512) for i in range(3)]
        ident = view(take(128), 128)
        ones = view(take(128), 128)
        halves = view(take(128), 128)
        incl = view(take(TC), TC)
        strict = view(take(TC), TC)
        level = view(take((LEVELS + 1) * TC), LEVELS + 1, TC)
        reset = view(take(NP), NP)
        par = view(take(PAR_ROWS), PAR_ROWS)
        omu = view(take(14), 14)
        omka = view(take(4), 4)
        eps = view(take(4), 4)
        ss = view(take(4), 4)
        rs = view(take(4), 4)
        ba = view(take(32), 4, 8)
        bt = view(take(16), 4, 4)
        gt = view(take(16), 4, 4)
        gtmp = view(take(16), 4, 4)
        dtb = view(take(4), 4)
        alog = view(take(4), 4)
        gcum = view(take(12), 3, 4)
        gend = view(take(12), 3, 4)
        gout = view(take(12), 3, 4)
        gtot = view(take(12), 3, 4)
        wc = view(take(12), 4, 3)
        stat = view(take(64), 64)
        sd = view(take(96), 12, 8)
        sdv = view(take(8 * 32), 8, 32)
        sv = view(take(192), 6, 4, 8)
        wba = view(take(64), 8, 8)
        XN = take(KT * NC)
        xnT = view(XN, KT, NC)
        R = take(0)
        A, B, C, E, G, H = take(3588), take(4158), take(4144), take(4736), take(4608), take(2368)
        I1, I2, I3, I4, T = take(2304), take(1536), take(1536), take(1152), take(4608)
        assert at[0] <= 52900, at[0]

        xtok = view(C, 3, D)
        xs = view(E, 3, D)
        parrow = view(I1, 128)
        pre = view(A, 12, 3 + NC)
        prw = view(B, 14, 1 + NC)
        mix = view(C, 14, NC)
        cconv = view(T, NQKV)
        cshift = view(T + 1536, NRW)
        lora = view(T + 3328, 512)
        g2w = view(T + 3840, 512)
        cconvT = view(I2, 12, 24)
        cshiftT = view(I2 + 288, 14, 8)
        cst = view(I2 + 400, 12, 8)
        dmix = view(I2 + 500, 14, 8)
        shift_out = view(G, NRW)
        conv_out = view(I1, NQKV)
        ld, aa, kk, cum = (view(E + i * 4 * NC, 4, NC) for i in range(4))
        t0, t1, t2 = (view(B + i * 4 * NC, 4, NC) for i in range(3))
        gate, bonus = view(H, 4, NC), view(H + 4 * NC, 4, NC)
        ar = view(G, 4, 2, NP)
        bb = view(G + 8 * NP, 4, NP)
        kb = view(G + 12 * NP, 4, NP)
        v_rw, b_rw, k_rw = view(T, 3, 512), view(T + 1536, 3, 512), view(T + 3072, 3, 512)
        qkv = view(C, 12, NC)
        sqb = view(B, 8, NC)
        rnb = view(E, 8, NC)
        gbc = view(I3, 12, 128)
        dec, edec, dst = view(A, 12, TC), view(A + 1152, 12, TC), view(A + 2304, 12, TC)
        qkh = view(I1, 8, NP)
        k_dn, v_dn = view(I2, 3, 512), view(I3, 3, 512)
        qkd = view(I4, 12, TC)
        bT = view(E, 12, TC)
        xx = view(E + 1152, 12, TC)
        yy = view(E + 2304, 12, TC)
        xT = view(B, 36, TC)
        akT, rbT, rkT = (view(W + SLOT + i * 2304, 24, TC) for i in range(3))
        s_dn_p = view(A, 512)
        s_rw_p = view(A + 512, 4, 64)
        r_buf, u_buf, o_buf = view(A + 768, 512), view(A + 1280, 512), view(A + 1792, 512)
        r_bufw, u_bufw = view(A + 2304, 512), view(A + 2816, 512)
        odn, orw = view(C, 4, NC), view(C + 4 * NC, 4, NC)
        sq_o, on_o = view(C + 8 * NC, 512), view(C + 8 * NC + 512, 512)
        yw_o, sqw_o = view(E + 3456, 512), view(E + 3968, 512)

        items = []

        def item(name, source, slot, width=512):
            use = sum(1 for i in items if i[2] == slot)
            items.append((name, source, slot, width, use))

        def wcols(w, lo, n):
            return w[0].rearrange("(k p) n -> p k n", p=128)[:, :, lo:lo + n]

        for name, lo, n, slot in (("r", ORW, 512, 0), ("kr", ORW + 512, 512, 1), ("vr", ORW + 1024, 512, 2),
                                  ("wag", ORW + 1536, 256, 0), ("q", 0, 512, 1), ("k", 512, 512, 2),
                                  ("v", 1024, 512, 0), ("z", OZ, 512, 0), ("g0", OGATE, 512, 1),
                                  ("g1", OGATE + 512, 512, 2), ("g2", OGATE + 1024, 512, 0),
                                  ("g3", OGATE + 1536, 512, 1)):
            item(name, wcols(w_in, lo, n), slot, n)
        item("updn", w_up_dn[0].rearrange("(k p) n -> p k n", p=128), 2)
        item("uprw", w_up_rw[0].rearrange("(k p) n -> p k n", p=128), 0)
        item("out0", wcols(w_out, 0, 512), 1)
        item("out1", wcols(w_out, 512, 512), 2)
        for i in range(4):
            item(f"wq{i}", wcols(peer_wq, 512 * i, 512), i % 3)
        place = {i[0]: i for i in items}

        w_landed = [sem(f"w_landed{i}") for i in range(3)]
        x_in = sem("x_in")
        small_in = sem("small_in")
        par_in = sem("par_in")
        consts = sem("consts")
        pool_step = sem("pool_step")
        vec_step = sem("vec_step")
        act_step = sem("act_step")
        rs_ready = sem("rs_ready")
        xs_ready = sem("xs_ready")
        xT_t = sem("xT_t")
        xT_done = sem("xT_done")
        par2_ready = sem("par2_ready")
        proj_ready = sem("proj_ready")
        proj_used = sem("proj_used")
        out_dma = sem("out_dma")
        shift_sent = sem("shift_sent")
        conv_sent = sem("conv_sent")
        mix_ready = sem("mix_ready")
        kk0_ready = sem("kk0_ready")
        bonus_in = sem("bonus_in")
        bonus_done = sem("bonus_done")
        cum_ready = sem("cum_ready")
        rw_vec_ready = sem("rw_vec_ready")
        conv_done = sem("conv_done")
        qk_done = sem("qk_done")
        ln_done = sem("ln_done")
        g_ready = sem("g_ready")
        gb_in = sem("gb_in")
        dec_in = sem("dec_in")
        dec_ready = sem("dec_ready")
        kq_used = sem("kq_used")
        rwm_used = sem("rwm_used")
        inv_y = sem("inv_y")
        inv_y_used = sem("inv_y_used")
        inv_z = sem("inv_z")
        inv_z_used = sem("inv_z_used")
        inv_x = sem("inv_x")
        inv_x_used = sem("inv_x_used")
        inv_first = sem("inv_first")
        inv_c = sem("inv_c")
        rwb_ready = sem("rwb_ready")
        rwb_used = sem("rwb_used")
        dn_r = sem("dn_r")
        dn_r_done = sem("dn_r_done")
        dn_u = sem("dn_u")
        dn_u_done = sem("dn_u_done")
        dn_o = sem("dn_o")
        dn_o_used = sem("dn_o_used")
        dn_s = sem("dn_s")
        dn_s_done = sem("dn_s_done")
        dn_ss = sem("dn_ss")
        dn_root = sem("dn_root")
        dn_on = sem("dn_on")
        dn_ot = sem("dn_ot")
        dn_ot_used = sem("dn_ot_used")
        rw_r = sem("rw_r")
        rw_r_done = sem("rw_r_done")
        rw_u = sem("rw_u")
        rw_u_done = sem("rw_u_done")
        rw_y = sem("rw_y")
        rw_s = sem("rw_s")
        rw_s_done = sem("rw_s_done")
        rw_c = sem("rw_c")
        rw_sq = sem("rw_sq")
        rw_var = sem("rw_var")
        rw_root = sem("rw_root")
        rw_yn = sem("rw_yn")
        rw_yt = sem("rw_yt")
        rw_yt_used = sem("rw_yt_used")
        up_ready = sem("up_ready")
        h_ready = sem("h_ready")
        query_ready = sem("query_ready")
        state_sent = sem("state_sent")
        st_in = sem("st_in")
        strw_in = sem("strw_in")
        strw_sent = sem("strw_sent")
        st_sent = sem("st_sent")
        svp_in = sem("svp_in")
        ytok_in = sem("ytok_in")
        x_again = sem("x_again")
        rows_in = sem("rows_in")
        keys_in = sem("keys_in")
        sc_sent = sem("sc_sent")
        y_sent = sem("y_sent")
        pst_t = sem("pst_t")
        svt_t = sem("svt_t")
        gbs_ready = sem("gbs_ready")
        gbs_sum = sem("gbs_sum")
        yv_ready = sem("yv_ready")
        syt_ready = sem("syt_ready")
        syt_t = sem("syt_t")
        kqp_ready = sem("kqp_ready")
        sdn_mv = sem("sdn_mv")
        delta_ready = sem("delta_ready")
        osq_sum = sem("osq_sum")
        tokd_t = sem("tokd_t")
        spread_ready = sem("spread_ready")
        outer = sem("outer")
        outer_used = sem("outer_used")
        ssq_ready = sem("ssq_ready")
        branches_ready = sem("branches_ready")
        up_used = sem("up_used")
        merged = sem("merged")
        h_used = sem("h_used")
        hsq = sem("hsq")
        hroot = sem("hroot")
        xn2_ready = sem("xn2_ready")
        xn2_t = sem("xn2_t")
        keys_t = sem("keys_t")
        score = sem("score")
        score_used = sem("score_used")
        u_free = sem("u_free")
        v_free = sem("v_free")
        idx_ready = sem("idx_ready")
        topk_step = sem("topk_step")
        cv_ready = sem("cv_ready")
        gexp_ready = sem("gexp_ready")
        gelu_step = sem("gelu_step")
        gelu_in = sem("gelu_in")
        tanh_ready = sem("tanh_ready")
        w_ready = sem("w_ready")
        held_steps = sem("held_steps")
        diag_ready = sem("diag_ready")
        peer_done = sem("peer_done")
        fsq = sem("fsq")
        froot = sem("froot")
        y_ready = sem("y_ready")
        u_in = [sem(f"u_in{i}") for i in range(8)]
        v_in = [sem(f"v_in{i}") for i in range(8)]
        (par_ready, cache_ready, ba_used, mix_part, shift_ready, wag_act, lora_used, kksq_ready, norm_used,
            exp_ready, conv_ready, vtok_ready, tap_ready, silu_done, qk_sq, qk_root, gexp_done, dec_exp,
            tok_ready, prw_ready) = series(sem("act_signals"), 1, 2, 1, 14, 4, 2, 12, 1, 4, 4, 3, 3, 12, 3, 1,
            8, 1, 6, 6, 6)
        (pst_ready, svt_ready, egb_ready, oroot, tokd_ready, sroot, syt_used, keys_ready, xn2T_ready, score_free,
            query_used) = series(sem("act_signals2"), 1, 6, 1, 1, 1, 1, 1, 4, 6, 1, 16)
        (par_t, cache_t, ba_ready, shift_t, lora_ready, norm_ready, bonus_sum, conv_t, vtok_t, qk_sum,
            gsum_ready, gb_ready, kq_ready, tok_t, prw_t, rwm_ready) = series(sem("pe_signals"), 1, 1, 1, 4, 12,
            4, 4, 3, 3, 8, 1, 3, 6, 6, 6, 12)
        ct = view(E + 3456, 12, TC)

        svt = view(T, RH, 6, RN)
        prwo = view(T + 3072, 8, 64)
        svp = view(T + 3584, 6, 64)
        vhalf, sa, yv = view(T + 3968, 32), view(T + 4000, 32), view(T + 4032, 32)
        ytok = view(T + 4064, 512)
        st = view(E, 32, 128)
        strw, prod = view(B, 32, 64), view(B + 2048, 32, 64)
        gbs = view(I1, 8, 128)
        stok = view(I3, 2, 512)
        spread = view(I1, 8, 128)
        zs = view(I4, 4, NX)
        gates = view(G, 16, NX)
        mm_ = view(A + 768, KT, NX)
        htok = view(T, 3, D)
        xn2 = view(C + 512, 3, D)
        xn2T = view(H, KT, NX)
        scratch = view(G, D)
        qT = view(G, 2, 4, NX)
        keysT = view(XN, 16, 128)
        ssc = view(I1, 2048)
        ln2row, lnfrow, xsrep = view(I2, D), view(I2 + D, D), view(I2 + 2 * D, D)
        zero512 = view(I4, 512)
        sc_all = view(E, 17, 256)
        uring = view(A, 8, D)
        vring = view(W + SLOT, 8, D)
        ttr_out = view(G, D)
        diag = view(G + 8 * NX, 8, 128)
        onehot = view(G + 8 * NX + D, PT, NCAND)
        small = [T + 3072]

        def tiny(*shape):
            n = 1
            for s in shape:
                n *= s
            small[0] += n
            assert small[0] <= T + 4608
            return view(small[0] - n, *shape)

        cur, curm = tiny(2, 128), tiny(2, 128)
        best = tiny(2, PT)
        keyf = tiny(2, PT)
        cand, candm, cidx = tiny(NCAND), tiny(NCAND), tiny(NCAND)
        cv, posf, eidf, ncv0 = tiny(PT), tiny(PT), tiny(PT), tiny(1)
        iota = tiny(NCAND)
        gexp, gsum, hdot, wgt = tiny(2, PT), tiny(2, 1), tiny(2, PT), tiny(2, PT)
        g1, g2 = tiny(PT), tiny(PT)
        selh, sel = tiny(8, 8), tiny(8)
        key_i = ctx.enter_context(nc.sbuf_tensor("key_i", [128, 2 * PT], U32))
        pos_i = ctx.enter_context(nc.sbuf_tensor("pos_i", [128, PT], U32))
        idx = ctx.enter_context(nc.sbuf_tensor("idx", [128, 2 * PT], U32))


        def emit_state_outputs(sp):
            sp.wait_ge(rw_yt_used, NCH)
            sp.wait_ge(dn_ot_used, NCH)
            for h in range(DH):
                sp.dma_start(st[:, 8 * h:8 * h + 8, :], state_dn[0, :, h].rearrange("b k v -> k b v")).then_inc(st_in, 16)
            for half in range(2):
                sp.dma_start(strw[64 * half:64 * half + 64],
                             state_rw[0].rearrange("b h v k -> (b h) v k")[:, 32 * half:32 * half + 32, :]
                             ).then_inc(strw_in, 16)
            sp.wait_ge(svt_ready.sem, svt_ready.at(6))
            for b in range(NS):
                for half in range(2):
                    p = 64 * half + 8 * b
                    sp.dma_start(svp[p:p + 8].rearrange("p x n -> p (x n)"),
                                 svt[b:b + 1].rearrange("p h x n -> p h (x n)")).then_inc(svp_in, 16)
            sp.wait_ge(dn_s_done, NCH)
            sp.dma_start(p_dn[0, 0].rearrange("h k v -> k h v"),
                         s_dn_p.rearrange("p (h v) -> p h v", h=4)).then_inc(state_sent, 16)
            sp.wait_ge(pst_ready.sem, pst_ready.at(1))
            sp.dma_start(p_rw[0, 0].rearrange("h v k -> v h k"), prwo[0:64]).then_inc(state_sent, 16)

        def emit_sample_outputs(sp):
            sp.wait_ge(yv_ready, 1)
            for b in range(NS):
                for half in range(2):
                    p = 64 * half + 8 * b
                    sp.dma_start(ytok[b:b + 1].rearrange("p (h n) -> p h n", n=RN)[:, :, 32 * half:32 * half + 32],
                                 yv[p:p + 8]).then_inc(ytok_in, 16)
            for half in range(2):
                sp.dma_start(s_rw[0].rearrange("b h v k -> (b h) v k")[:, 32 * half:32 * half + 32, :],
                             strw[64 * half:64 * half + 64]).then_inc(strw_sent, 16)
            sp.wait_ge(svp_in, 16 * 16)
            for i in range(2):
                sp.dma_start(htok[:, i, :], x_prompt[0, 128 * i:128 * i + 128]).then_inc(x_again, 16)
            sp.dma_start(htok[0:NS, 2, :], x_sample[:, 0]).then_inc(x_again, 16)
            for h in range(DH):
                sp.wait_ge(outer_used, 2 * h + 2)
                sp.dma_start(s_dn[0, :, h].rearrange("b k v -> k b v"), st[:, 8 * h:8 * h + 8, :]).then_inc(st_sent, 16)

        def emit_norm_rows(sp):
            sp.wait_ge(branches_ready, 1)
            sp.dma_start(ln2row, ln2.broadcast_to([128, D])).then_inc(rows_in, 16)
            sp.dma_start(lnfrow, ln_f.rearrange("(a d) -> a d", a=1).broadcast_to([128, D])).then_inc(rows_in, 16)

        def emit_peer_io(sp):
            sp.wait_ge(xn2_ready, 3)
            for h in range(PH):
                sp.dma_start(xsrep[NS * h:NS * h + NS], xn2[0:NS, 2, :]).then_inc(sc_sent, 16)
            sp.wait_ge(score_used, 12)
            sp.wait_ge(score_free.sem, score_free.at(1))
            for h in range(PH):
                sp.dma_start(sc_all[NS * h:NS * h + NS, 16, :], ssc[0:NS, 256 * h:256 * h + 256]).then_inc(sc_sent, 16)
            for i in range(3):
                sp.wait_ge(y_ready, i + 1)
                sp.dma_start(y_prompt[0, 128 * i:128 * i + 128] if i < 2 else y_sample[:, 0],
                             xn2[0:128 if i < 2 else NS, i, :]).then_inc(y_sent, 16)
            sp.wait_ge(y_sent, 48)
            for s, n in ((out_dma, 16), (shift_sent, 32), (conv_sent, 32), (state_sent, 32), (strw_sent, 32), (st_sent, 64)):
                sp.wait_ge(s, n)

        def held(eng, s, value):
            eng.wait_ge(s, value)
            eng.sem_inc(held_steps, 1)

        def gather(pool, ring, landed, table, p, j, n):
            pool.indirect_dma_start(ring[0:n, j % 8, :], None, table[0],
                                    bass.IndirectOffsetOnAxis(ap=idx[0:n, PT * p + j:PT * p + j + 1], axis=0)
                                    ).then_inc(landed[j % 8], 16)

        def pool_unit(pool, u, p, n=128):
            pool.wait_ge(idx_ready, u + 1)
            pool.sem_inc(held_steps, 1)
            for ring, landed, table, free in ((uring, u_in, peer_u, u_free), (vring, v_in, peer_v, v_free)):
                for j in range(PT):
                    held(pool, free, 16 * u + (j + 1))
                    gather(pool, ring, landed, table, p, j, n)

        def pool_peer(pool, step):
            pool.wait_ge(h_used, 6)
            step(nc.gpsimd.iota(iota, [[1, NCAND]], base=0, channel_multiplier=0, allow_small_or_imprecise_dtypes=True))
            step(nc.gpsimd.memset(selh, 0.0))
            step(nc.gpsimd.memset(zero512, 0.0))
            step.sync()
            nc.gpsimd.affine_select(out=selh, in_=selh, pattern=[[-8, 8], [-1, 8]], compare_op=ALU.not_equal, fill=1.0,
                                    base=0, channel_multiplier=1).then_inc(consts, 1)
            for t in range(2):
                with pool.Fori(0, 4) as i:
                    for p in range(2):
                        pool_unit(pool, i * 2 + (8 * t + p), p)
            pool_unit(pool, 16, 0, NS * PH)

        def pe_rest(pe, mm):
            tile = [26]

            def project(name):
                slot = wait_w(pe, name)
                for f in range(place[name][3] // 128):
                    pe.wait_ge(proj_used, tile[0] - 3)
                    for k in range(KT):
                        ins = mm(psv(tile[0] % 4, 128, NX), wslot[slot][:, k, f * 128:(f + 1) * 128],
                                 xnT[:, k, T0:NC], start=k == 0, stop=k == KT - 1)
                    ins.then_inc(proj_ready, 1)
                    tile[0] += 1

            pe.wait_ge(rw_s_done, NCH)
            pe.wait_ge(dn_s_done, NCH)
            pe.wait_ge(rw_yt_used, NCH)
            pe.wait_ge(dn_ot_used, NCH)
            for f in range(4):
                ins = nc.tensor.transpose(psv(7, 64, 128, at=128 * f), s_rw_p[:, f, :], ident)
            ins.then_inc(pst_t, 1)
            for x in range(6):
                if x >= 2:
                    pe.wait_ge(svt_ready.sem, svt_ready.at(x - 1))
                for f in range(4):
                    ins = nc.tensor.transpose(psv(4 + x % 2, NS, 128, at=128 * f), sv[:, x, f, :], ident)
                ins.then_inc(svt_t, 1)
            pe.wait_ge(gbs_ready, 1)
            for i in range(8):
                ins = mm(psv(6, 128, NS, at=NS * i), gbs[0:NS, i, :], ident[0:NS, 0:NS])
            ins.then_inc(gbs_sum, 1)
            project("z")
            project("g0")
            pe.wait_ge(svt_ready.sem, svt_ready.at(6))
            pe.wait_ge(kqp_ready, 1)
            mm(psv(7, 128, 32), ones, sdv[:, 2, :])
            for h in range(DH):
                pe.wait_ge(st_in, 64)
                for b in range(NS):
                    ins = mm(psv(5, 128, 2, at=2 * (8 * h + b)), st[:, 8 * h + b, :], sd[:, h:h + 5:4, b])
            ins.then_inc(sdn_mv, 1)
            project("g1")
            pe.wait_ge(delta_ready, 1)
            mm(psv(6, 128, 32), ones, sdv[:, 5, :]).then_inc(osq_sum, 1)
            for h in range(DH):
                nc.tensor.transpose(psv(4, NS, 128, at=128 * h), sdv[:, 3, 8 * h:8 * h + 8], ident)
            for h in range(DH):
                ins = nc.tensor.transpose(psv(5, NS, 128, at=128 * h), sd[:, 4 + h, :], ident)
            ins.then_inc(tokd_t, 1)
            project("g2")
            pe.wait_ge(oroot.sem, oroot.at(1))
            for n in range(8):
                h, half = n // 2, n % 2
                pe.wait_ge(spread_ready, h + 1)
                if n >= 4:
                    pe.wait_ge(outer_used, n - 3)
                mm(psv(4 + n % 4, 128, 4, 128), stok[0:NS, 1, 128 * h:128 * h + 128],
                   spread[0:NS, 4 * half:4 * half + 4, :]).then_inc(outer, 1)
            project("g3")
            pe.wait_ge(syt_ready, 1)
            pe.wait_ge(outer_used, 8)
            for f in range(4):
                ins = nc.tensor.transpose(psv(4, 128, NS, at=NS * f), ytok[0:NS, 128 * f:128 * f + 128],
                                          ident[0:NS, 0:NS])
            ins.then_inc(syt_t, 1)
            pe.wait_ge(proj_used, 46)
            pe.wait_ge(branches_ready, 1)
            for n in range(16):
                name, src = (("updn", odn), ("uprw", orw))[n // 8]
                if n % 8 == 0:
                    slot = wait_w(pe, name)
                    w = wslot[slot].rearrange("p k n -> p (k n)").rearrange("p (k n) -> p k n", k=4)
                if n >= 4:
                    pe.wait_ge(up_used, n - 3)
                f = n % 8
                for k in range(4):
                    ins = mm(psv(n % 4, 128, NX), w[:, k, f * 128:f * 128 + 128], src[:, k, T0:NC], start=k == 0, stop=k == 3)
                ins.then_inc(up_ready, 1)
            pe.wait_ge(keys_in, 16)
            pe.wait_ge(syt_used.sem, syt_used.at(1))
            for n in range(4):
                for q in range(4):
                    ins = nc.tensor.transpose(psv(4 + n, 128, 128, at=128 * q), keysT[:, 4 * n + q, :], ident)
                ins.then_inc(keys_t, 1)
            pe.wait_ge(up_used, 16)
            pe.wait_ge(merged, 8)
            pe.wait_ge(keys_ready.sem, keys_ready.at(4))
            for n in range(6):
                half, i = n // 3, n % 3
                if i == 0:
                    slot = wait_w(pe, f"out{half}")
                rows, cols = (128, slice(128 * i, 128 * i + 128)) if i < 2 else (NS, slice(SEQ, SEQ + NS))
                for k in range(KT):
                    ins = mm(psv(n, rows, 512), mm_[:, k, cols], wslot[slot][:, k, :], start=k == 0, stop=k == KT - 1)
                ins.then_inc(h_ready, 1)
            pe.wait_ge(h_used, 6)
            for i, n in enumerate((128, 128, NS)):
                pe.wait_ge(xn2_ready, i + 1)
                for half in range(2):
                    for q in range(4):
                        k = 4 * half + q
                        ins = nc.tensor.transpose(psv(2 * i + half, 128, 4, 128)[:, q, 0:n],
                                                  xn2[0:n, i, k * 128:(k + 1) * 128], ident[0:n, 0:n])
                    ins.then_inc(xn2_t, 1)
            pe.wait_ge(xn2T_ready.sem, xn2T_ready.at(6))
            for hp in range(4):
                slot = wait_w(pe, f"wq{hp}")
                for q in range(4):
                    n = 4 * hp + q
                    if n >= 4:
                        pe.wait_ge(query_used.sem, query_used.at(n - 3))
                    for k in range(KT):
                        ins = mm(psv(q, 128, NX), wslot[slot][:, k, 128 * q:128 * q + 128], xn2T[:, k, :],
                                 start=k == 0, stop=k == KT - 1)
                    ins.then_inc(query_ready, 1)
                if hp == 2:
                    pe.wait_ge(query_ready, 12)
                    pe.sem_inc(v_free, 8)
                pe.wait_ge(query_used.sem, query_used.at(4 * hp + 4))
                for i in range(3):
                    n = 3 * hp + i
                    if n >= 4:
                        pe.wait_ge(score_used, n - 3)
                    rows, cols = (128, slice(128 * i, 128 * i + 128)) if i < 2 else (NS, slice(SEQ, SEQ + NS))
                    for q in range(4):
                        ins = mm(psv(4 + n % 4, rows, 128, at=128 * q), qT[:, hp % 2, q, cols], keysT[:, 4 * hp + q, :])
                    ins.then_inc(score, 1)
            pe.wait_ge(score_used, 12)
            pe.wait_ge(consts, 2)

            def weigh(t, lhsT, rows, out_rows, j, start=False, stop=False):
                for half in range(2):
                    ins = mm(psv(2 * t + half, out_rows, 512), lhsT, vring[0:rows, j % 8, 512 * half:512 * half + 512],
                             start=start, stop=stop)
                return ins

            for t in range(2):
                for half in range(2):
                    mm(psv(2 * t + half, 128, 512), ident, zero512, stop=False)
                with pe.Fori(0, 4) as i:
                    for p in range(2):
                        u = i * 2 + (8 * t + p)
                        for j in range(PT):
                            pe.wait_ge(v_in[j % 8], 32 * u + 16 * (j // 8 + 1))
                            pe.wait_ge(diag_ready, 16 * u + (j + 1))
                            weigh(t, diag[:, j % 8, :], 128, 128, j).then_inc(v_free, 1)
                for half in range(2):
                    ins = mm(psv(2 * t + half, 128, 512), ident, zero512, start=False)
                ins.then_inc(peer_done, 1)
            for j in range(PT):
                pe.wait_ge(v_in[j % 8], 32 * 16 + 16 * (j // 8 + 1))
                pe.wait_ge(diag_ready, 16 * 16 + j + 1)
                ins = weigh(2, diag[0:NS * PH, j % 8, 0:NS], NS * PH, NS, j, start=j == 0, stop=j == PT - 1)
                ins.then_inc(v_free if j < PT - 1 else peer_done, 1)

        def act_rest(act, step, fn, evacuate):
            act.wait_ge(pst_t, 1)
            fn(prwo[0:64].rearrange("p h k -> p (h k)"), psv(7, 64, 512)).then_inc(pst_ready.sem, 1)
            for x in range(6):
                act.wait_ge(svt_t, x + 1)
                fn(svt[0:NS, :, x, :], psv(4 + x % 2, NS, RH, RN)).then_inc(svt_ready.sem, 1)
            act.wait_ge(gbs_sum, 1)
            step(fn(sdv[:, 1, :], psv(6, 128, 32, at=32)))
            fn(sdv[:, 0, :], psv(6, 128, 32), ACT.Exp).then_inc(egb_ready.sem, 1)
            evacuate([zs[:, f, :] for f in range(4)], ACT.Silu, NX)
            evacuate([gates[:, f, :] for f in range(8)], ACT.Sigmoid, NX)
            act.wait_ge(osq_sum, 1)
            fn(sdv[:, 6, :], psv(6, 128, 32), ACT.Sqrt, scale=1.0 / DK, bias=eps[:, 0:1]).then_inc(oroot.sem, 1)
            act.wait_ge(tokd_t, 1)
            step(fn(stok[0:NS, 0, :], psv(4, NS, 512)))
            fn(stok[0:NS, 1, :], psv(5, NS, 512)).then_inc(tokd_ready.sem, 1)
            act.wait_ge(ssq_ready, 1)
            fn(stat[0:NS, 40:48], stat[0:NS, 32:40], ACT.Sqrt, scale=1.0 / RN, bias=eps[0:NS, 2:3]).then_inc(sroot.sem, 1)
            evacuate([gates[:, 8 + f, :] for f in range(8)], ACT.Sigmoid, NX)
            act.wait_ge(syt_t, 1)
            fn(orw[:, :, NP:NC], psv(4, 128, 4, NS)).then_inc(syt_used.sem, 1)
            for n in range(4):
                act.wait_ge(keys_t, 4)
                fn(keysT[:, 4 * n:4 * n + 4, :], psv(4 + n, 128, 4, 128)).then_inc(keys_ready.sem, 1)
            for i, n in enumerate((128, 128, NS)):
                act.wait_ge(h_used, 6)
                fn(scratch[0:n], htok[0:n, i, :], ACT.Square, accum_out=ss[0:n, i:i + 1]).then_inc(hsq, 1)
                act.wait_ge(hsq, i + 1)
                fn(rs[0:n, i:i + 1], ss[0:n, i:i + 1], ACT.Sqrt, scale=1.0 / D, bias=eps[0:n, 0:1]).then_inc(hroot, 1)
            for i, n in enumerate((128, 128, NS)):
                for half in range(2):
                    act.wait_ge(xn2_t, 2 * i + half + 1)
                    fn(xn2T[:, 4 * half:4 * half + 4, 128 * i:128 * i + n],
                       psv(2 * i + half, 128, 4, 128)[:, :, 0:n]).then_inc(xn2T_ready.sem, 1)
            act.wait_ge(consts, 2)
            act.wait_ge(st_sent, 64)
            act.wait_ge(state_sent, 32)
            fn(sc_all[:, 16, :], zero512[:, 0:256]).then_inc(score_free.sem, 1)
            for hp in range(4):
                for q in range(4):
                    n = 4 * hp + q
                    if hp >= 2:
                        act.wait_ge(score, 3 * hp - 3)
                    act.wait_ge(query_ready, n + 1)
                    fn(qT[:, hp % 2, q, :], psv(q, 128, NX)).then_inc(query_used.sem, 1)
                for i in range(3):
                    n = 3 * hp + i
                    act.wait_ge(score, n + 1)
                    if i < 2:
                        dst = sc_all[:, 8 * i + 2 * hp:8 * i + 2 * hp + 2, :].rearrange("p u n -> p (u n)")
                    else:
                        dst = ssc[0:NS, 512 * hp:512 * hp + 512]
                    fn(dst, psv(4 + n % 4, 128 if i < 2 else NS, 512)).then_inc(score_used, 1)

            def softmax_exp(u, p):
                act.wait_ge(cv_ready, u + 1)
                fn(gexp[:, p, :], cv, ACT.Exp, bias=ncv0, accum_out=gsum[:, p, :]).then_inc(gexp_ready, 1)

            def act_unit(u, p, n=128, last=False):
                act.wait_ge(gelu_in, u + 1)
                fn(g2[0:n], g1[0:n], ACT.Tanh, scale=GELU_C).then_inc(tanh_ready, 1)
                act.wait_ge(w_ready, u + 1)
                for j in range(PT):
                    act.wait_ge(v_free, 16 * u + (j + 1))
                    out, src = (diag[:, j % 8, :], ident) if n == 128 else (diag[0:n, j % 8, 0:NS], sel[0:n])
                    fn(out, src, scale=wgt[0:n, p, j:j + 1]).then_inc(diag_ready, 1)
                if not last:
                    softmax_exp(u + 1, 1 - p)

            softmax_exp(0, 0)
            for t in range(2):
                with act.Fori(0, 4) as i:
                    for p in range(2):
                        act_unit(i * 2 + (8 * t + p), p)
            act_unit(16, 0, NS * PH, True)
            for i, n in enumerate((128, 128, NS)):
                act.wait_ge(fsq, i + 1)
                step(fn(ttr_out[0:n], htok[0:n, i, :], ACT.Square, accum_out=ss[0:n, i:i + 1]))
                step.sync()
                fn(rs[0:n, i:i + 1], ss[0:n, i:i + 1], ACT.Sqrt, scale=1.0 / D, bias=eps[0:n, 0:1]).then_inc(froot, 1)

        def vec_rest(dve, step, v, tt, ts, stt, pc):
            dve.wait_ge(dn_o, NCH)
            step(v.tensor_copy(gbs[0:NS, 0:4, :], row(gt[0:NS, 3, :], NS, 4, 128)))
            v.tensor_copy(gbs[0:NS, 4:8, :], row(bt[0:NS, 3, :], NS, 4, 128)).then_inc(gbs_ready, 1)
            s32 = [sdv[:, i, :] for i in range(8)]
            s48 = [sdv[:, i, :].rearrange("p (h b) -> p h b", h=4) for i in range(8)]
            tt(s48[2], sd[:, 0:4, :], sd[:, 4:8, :], ALU.mult).then_inc(kqp_ready, 1)
            dve.wait_ge(svp_in, 16 * 16)
            dve.wait_ge(strw_in, 32)

            def over_v(x):
                return svp[:, x, :].unsqueeze(1).broadcast_to([128, 32, 64])

            def over_k(x):
                return row(x, 128, 32, 64)

            step(v.tensor_copy(vhalf[0:64], svp[0:64, 3, 0:32]))
            step(v.tensor_copy(vhalf[64:128], svp[64:128, 3, 32:64]))
            step(tt(prod, strw, over_v(4), ALU.mult))
            step.sync()
            step(v.tensor_reduce(sa, prod, AX, ALU.add))
            step(tt(strw, strw, over_v(1), ALU.mult))
            step.sync()
            step(tt(prod, over_v(5), over_k(sa), ALU.mult))
            step.sync()
            step(tt(strw, strw, prod, ALU.subtract))
            step.sync()
            step(tt(prod, over_v(2), over_k(vhalf), ALU.mult))
            step.sync()
            step(tt(strw, strw, prod, ALU.add))
            step.sync()
            step(tt(prod, strw, over_v(0), ALU.mult))
            step.sync()
            v.tensor_reduce(yv, prod, AX, ALU.add).then_inc(yv_ready, 1)
            dve.wait_ge(sdn_mv, 1)
            dve.wait_ge(egb_ready.sem, egb_ready.at(1))
            p2 = psv(5, 128, 32, 2)
            step(tt(s32[3], p2[:, :, 1], s32[0], ALU.mult))
            step(tt(s32[4], p2[:, :, 0], s32[0], ALU.mult))
            step.sync()
            step(tt(s48[3], sd[:, 8:12, :], s48[3], ALU.subtract))
            step.sync()
            step(tt(s32[3], s32[3], s32[1], ALU.mult))
            step.sync()
            step(tt(s32[7], s32[3], psv(7, 128, 32), ALU.mult))
            step.sync()
            step(tt(s32[4], s32[4], s32[7], ALU.add))
            step.sync()
            tt(s32[5], s32[4], s32[4], ALU.mult).then_inc(delta_ready, 1)
            dve.wait_ge(oroot.sem, oroot.at(1))
            step(v.reciprocal(s32[6], s32[6]))
            step.sync()
            step(tt(odn[:, :, NP:NC], s48[4], s48[6], ALU.mult))
            dve.wait_ge(ytok_in, 16 * 16)
            y8 = ytok[0:NS].rearrange("p (h v) -> p h v", h=8)
            sq8 = prod[0:NS].rearrange("p a b -> p (a b)")[:, 0:512].rearrange("p (h v) -> p h v", h=8)
            step(v.tensor_reduce(stat[0:NS, 32:40], y8, AX, ALU.add))
            step.sync()
            step(ts(stat[0:NS, 32:40], stat[0:NS, 32:40], 1.0 / RN, None, ALU.mult))
            step.sync()
            step(tt(y8, y8, row(stat[0:NS, 32:40], NS, 8, 64), ALU.subtract))
            step.sync()
            step(tt(sq8, y8, y8, ALU.mult))
            step.sync()
            v.tensor_reduce(stat[0:NS, 32:40], sq8, AX, ALU.add).then_inc(ssq_ready, 1)
            dve.wait_ge(tokd_ready.sem, tokd_ready.at(1))
            for n in range(8):
                h, half = n // 2, n % 2
                if half == 0:
                    if h > 0:
                        dve.wait_ge(outer, n)
                    tt(spread[0:NS], stok[0:NS, 0, 128 * h:128 * h + 128].unsqueeze(1).broadcast_to([NS, NS, 128]),
                       row(ident[0:NS, 0:NS], NS, NS, 128), ALU.mult).then_inc(spread_ready, 1)
                dve.wait_ge(outer, n + 1)
                for b in range(4):
                    m = 8 * h + 4 * half + b
                    ins = stt(st[:, m, :], st[:, m, :], s32[0][:, m:m + 1], psv(4 + n % 4, 128, 128, at=128 * b),
                              ALU.mult, ALU.add)
                    if b < 3:
                        step(ins)
                ins.then_inc(outer_used, 1)
            dve.wait_ge(sroot.sem, sroot.at(1))
            step(v.reciprocal(stat[0:NS, 40:48], stat[0:NS, 40:48]))
            step.sync()
            tt(y8, y8, row(stat[0:NS, 40:48], NS, 8, 64), ALU.mult).then_inc(syt_ready, 1)
            dve.wait_ge(proj_used, 30)
            for h in range(DH):
                step(stt(odn[:, h, T0:NC], odn[:, h, T0:NC], pc("dn_norm"), zs[:, h, :], ALU.mult, ALU.mult))
            dve.wait_ge(syt_used.sem, syt_used.at(1))
            for f in range(4):
                step(ts(orw[:, f, T0:NC], orw[:, f, T0:NC], pc("gn_w", f), pc("gn_b", f), ALU.mult, ALU.add))
            step.sync()
            step(tt(orw[:, :, T0:NC], orw[:, :, T0:NC], bonus[:, :, T0:NC], ALU.add))
            step.sync()
            tt(orw[:, :, T0:NC], orw[:, :, T0:NC], gate[:, :, T0:NC], ALU.mult).then_inc(branches_ready, 1)
            dve.wait_ge(proj_used, 46)
            for n in range(16):
                dve.wait_ge(up_ready, n + 1)
                f, p = n % 8, psv(n % 4, 128, NX)
                if n < 8:
                    tt(mm_[:, f, :], p, gates[:, f, :], ALU.mult).then_inc(up_used, 1)
                else:
                    tt(gates[:, n, :], p, gates[:, n, :], ALU.mult).then_inc(up_used, 1)
                    dve.wait_ge(up_used, n + 1)
                    tt(mm_[:, f, :], mm_[:, f, :], gates[:, n, :], ALU.add).then_inc(merged, 1)
            dve.wait_ge(x_again, 48)
            for n in range(6):
                half, i = n // 3, n % 3
                rows = 128 if i < 2 else NS
                dve.wait_ge(h_ready, n + 1)
                h_ = htok[0:rows, i, 512 * half:512 * half + 512]
                tt(h_, h_, psv(n, rows, 512), ALU.add).then_inc(h_used, 1)
            dve.wait_ge(rows_in, 32)
            for i, n in enumerate((128, 128, NS)):
                dve.wait_ge(hroot, i + 1)
                step(v.reciprocal(rs[0:n, i:i + 1], rs[0:n, i:i + 1]))
                step.sync()
                stt(xn2[0:n, i, :], htok[0:n, i, :], rs[0:n, i:i + 1], ln2row[0:n], ALU.mult, ALU.mult).then_inc(xn2_ready, 1)
            dve.wait_ge(consts, 2)
            step(v.tensor_reduce(sel, selh.rearrange("p h b -> p b h"), AX, ALU.add))
            dve.wait_ge(strw_sent, 32)
            dve.sem_inc(u_free, 8)
            dve.wait_ge(score_used, 1)
            NTOP = 32

            def topk(u, p, src, first=False):
                k = Steps(dve, topk_step, u * NTOP)

                def sync():
                    held(dve, topk_step, k.base + k.n)

                if not first:
                    dve.wait_ge(score_used, 12)
                    dve.wait_ge(v_free, 16 * u - 8)
                    dve.wait_ge(gexp_ready, u)
                k(v.tensor_copy(cur, src))
                sync()
                for x in range(2):
                    k(v.max(best[:, x, 0:8], cur[:, x, :]))
                sync()
                for x in range(2):
                    k(v.match_replace(curm[:, x, :], best[:, x, 0:8], cur[:, x, :], NEG))
                    k(v.max_index(key_i[:, PT * x:PT * x + 8], best[:, x, 0:8], cur[:, x, :]))
                sync()
                for x in range(2):
                    k(v.max(best[:, x, 8:16], curm[:, x, :]))
                sync()
                for x in range(2):
                    k(v.max_index(key_i[:, PT * x + 8:PT * x + 16], best[:, x, 8:16], curm[:, x, :]))
                at_ = 0
                for a, na, nb in PAIRS:
                    o = cand[:, at_:at_ + na * nb].rearrange("p (a b) -> p a b", a=na)
                    k(tt(o, row(best[:, 0, a:a + na], 128, na, nb),
                         best[:, 1, 0:nb].unsqueeze(1).broadcast_to([128, na, nb]), ALU.add))
                    at_ += na * nb
                sync()
                k(v.max(cv[:, 0:8], cand))
                k(ts(keyf[:, 0, :], key_i[:, 0:PT], float(PK), None, ALU.mult))
                k(ts(keyf[:, 1, :], key_i[:, PT:2 * PT], 1.0, None, ALU.mult))
                sync()
                k(v.match_replace(candm, cv[:, 0:8], cand, NEG))
                k(v.max_index(pos_i[:, 0:8], cv[:, 0:8], cand))
                at_ = 0
                for a, na, nb in PAIRS:
                    o = cidx[:, at_:at_ + na * nb].rearrange("p (a b) -> p a b", a=na)
                    k(tt(o, row(keyf[:, 0, a:a + na], 128, na, nb),
                         keyf[:, 1, 0:nb].unsqueeze(1).broadcast_to([128, na, nb]), ALU.add))
                    at_ += na * nb
                sync()
                k(v.max(cv[:, 8:16], candm))
                sync()
                k(v.max_index(pos_i[:, 8:16], cv[:, 8:16], candm))
                ts(ncv0, cv[:, 0:1], -1.0, None, ALU.mult).then_inc(cv_ready, 1)
                k.sync()
                k(v.tensor_copy(posf, pos_i[:, :]))
                k.sync()
                k(tt(onehot, iota.unsqueeze(1).broadcast_to([128, PT, NCAND]), row(posf, 128, PT, NCAND), ALU.is_equal))
                k.sync()
                k(tt(onehot, onehot, cidx.unsqueeze(1).broadcast_to([128, PT, NCAND]), ALU.mult))
                k.sync()
                k(v.tensor_reduce(eidf, onehot, AX, ALU.add))
                assert k.n == NTOP, k.n
                k.sync()
                v.tensor_copy(idx[:, PT * p:PT * p + PT], eidf).then_inc(idx_ready, 1)

            NGELU = 5

            def experts(u, p, x, n=128):
                for j in range(PT):
                    dve.wait_ge(u_in[j % 8], 32 * u + 16 * (j // 8 + 1))
                    v.tensor_tensor_reduce(uring[0:n, j % 8, :], uring[0:n, j % 8, :], x, 1.0, 0.0, ALU.mult, ALU.add,
                                           hdot[0:n, p, j:j + 1]).then_inc(u_free, 1)
                h = hdot[0:n, p, :]
                a, b = g1[0:n], g2[0:n]
                k = Steps(dve, gelu_step, u * NGELU)
                dve.wait_ge(u_free, 16 * u + (PT + 8))
                k(tt(a, h, h, ALU.mult))
                k.sync()
                k(ts(a, a, 0.044715, 1.0, ALU.mult, ALU.add))
                k.sync()
                tt(a, a, h, ALU.mult).then_inc(gelu_in, 1)
                dve.wait_ge(gexp_ready, u + 1)
                k(v.reciprocal(gsum[0:n, p, :], gsum[0:n, p, :]))
                dve.wait_ge(tanh_ready, u + 1)
                k(stt(b, b, 1.0, h, ALU.add, ALU.mult))
                k.sync()
                k(tt(b, b, gexp[0:n, p, :], ALU.mult))
                k.sync()
                ts(wgt[0:n, p, :], b, gsum[0:n, p, :], 0.5, ALU.mult, ALU.mult).then_inc(w_ready, 1)
                assert k.n == NGELU

            topk(0, 0, sc_all[:, 0, :].rearrange("p (x n) -> p x n", x=2), True)
            flat = sc_all.rearrange("p u n -> p (u n)")
            for t in range(2):
                if t == 1:
                    dve.wait_ge(sc_sent, 16 * 16)
                with dve.Fori(0, 4) as i:
                    for p in range(2):
                        u = i * 2 + (8 * t + p)
                        experts(u, p, xn2[:, t, :])
                        src = flat[:, bass.ds(i * 512 + (8 * t + p + 1) * 256, 256)].rearrange("p (x n) -> p x n", x=2)
                        topk(u + 1, 1 - p, src)
            experts(16, 0, xsrep[0:NS * PH], NS * PH)
            for i, n in enumerate((128, 128, NS)):
                dve.wait_ge(peer_done, i + 1)
                for half in range(2):
                    h_ = htok[0:n, i, 512 * half:512 * half + 512]
                    ins = tt(h_, h_, psv(2 * i + half, n, 512), ALU.add)
                    if half == 0:
                        step(ins)
                ins.then_inc(fsq, 1)
            for i, n in enumerate((128, 128, NS)):
                dve.wait_ge(froot, i + 1)
                step(v.reciprocal(rs[0:n, i:i + 1], rs[0:n, i:i + 1]))
                step.sync()
                stt(xn2[0:n, i, :], htok[0:n, i, :], rs[0:n, i:i + 1], lnfrow[0:n], ALU.mult, ALU.mult).then_inc(y_ready, 1)

        TILE_ROWS = [128, 128, NS + META]

        def ccols(c):
            return slice(c * TC, (c + 1) * TC)

        def wait_w(eng, name):
            _, _, slot, _, use = place[name]
            eng.wait_ge(w_landed[slot], 16 * (use + 1))
            return slot

        freed, tiles = {}, 0
        for name, _, _, width, _ in items:
            if name == "updn":
                break
            tiles += width // 128
            freed[name] = (proj_ready, tiles)
        freed.update(updn=(up_ready, 8), uprw=(up_ready, 16), out0=(h_ready, 3), out1=(h_ready, 6),
                     wq0=(query_ready, 4), wq1=(query_ready, 8), wq2=(query_ready, 12))

        block = ctx.enter_context(nc.Block())

        @block.sync
        def _(sp):
            sp.dma_start(xtok[:, 0, :], x_prompt[0, 0:128]).then_inc(x_in, 16)
            sp.dma_start(xtok[:, 1, :], x_prompt[0, 128:256]).then_inc(x_in, 16)
            sp.dma_start(xtok[0:NS, 2, :], x_sample[:, 0]).then_inc(x_in, 16)
            sp.dma_start(xtok[NS:NS + META, 2, :], meta_tokens).then_inc(x_in, 16)
            srcs = {"ln1": ln1, "mu": rw_mu, "w0": rw_w0, "a0": rw_a0, "k_k": rw_k_k, "k_a": rw_k_a, "gn_w": rw_gn_w,
                    "gn_b": rw_gn_b, "dn_norm": dn_norm_w}
            for name, n in PAR:
                if name == "conv":
                    src = dn_conv_w[0].rearrange("j (f p) -> (j f) p", p=128)
                elif name == "r_k":
                    src = rw_r_k[0].rearrange("(f a) n -> f (a n)", a=2)
                else:
                    src = srcs[name][0].rearrange("(f p) -> f p", p=128)
                sp.dma_start(parrow[PAR_AT[name]:PAR_AT[name] + n, :], src).then_inc(par_in, 16)
            sp.dma_start(cconv[0:24, :], cache_dn_conv[0].rearrange("b j n -> (b j) n")).then_inc(small_in, 16)
            sp.dma_start(cshift[0:8, :], cache_rw_shift[0, :, 0]).then_inc(small_in, 16)
            for n, (name, src, slot, width, use) in enumerate(items):
                if name == "g0":
                    sp.wait_ge(rw_y, 2 * NCH)
                if use > 0:
                    before = [i[0] for i in items if i[2] == slot][use - 1]
                    sp.wait_ge(*freed[before])
                if name in ("updn", "uprw"):
                    dst = wslot[slot].rearrange("p k n -> p (k n)").rearrange("p (k n) -> p k n", k=4)
                else:
                    dst = wslot[slot][:, :, 0:width]
                sp.dma_start(dst, src).then_inc(w_landed[slot], 16)
                if n == 0:
                    sp.dma_start(lora[0:64, :], rw_w2[0]).then_inc(small_in, 16)
                    sp.dma_start(lora[64:128, :], rw_a2[0]).then_inc(small_in, 16)
                    sp.dma_start(g2w, rw_g2[0]).then_inc(small_in, 16)
                    sp.dma_start(dtb, dn_dt_bias.broadcast_to([128, 4])).then_inc(small_in, 16)
                    sp.dma_start(alog, dn_a_log.broadcast_to([128, 4])).then_inc(small_in, 16)
                    sp.dma_start(wba, wcols(w_in, OBETA, 8)).then_inc(small_in, 16)
                if name == "v":
                    sp.wait_ge(shift_ready.sem, shift_ready.at(4))
                    sp.dma_start(p_shift[0], shift_out[0:1, :]).then_inc(shift_sent, 16)
                    sp.dma_start(s_shift[0, :, 0], shift_out[1:9, :]).then_inc(shift_sent, 16)
                    sp.dma_start(s_conv[0, :, 0:2], cache_dn_conv[0, :, 1:3]).then_inc(out_dma, 16)
                    sp.wait_ge(conv_ready.sem, conv_ready.at(3))
                    sp.dma_start(p_conv[0, 0], conv_out[0:3, :]).then_inc(conv_sent, 16)
                    sp.dma_start(s_conv[0, :, 2], conv_out[3:11, :]).then_inc(conv_sent, 16)
                if name == "g1":
                    emit_state_outputs(sp)
                if name == "g3":
                    emit_sample_outputs(sp)
                if name == "out0":
                    sp.dma_start(keysT, peer_keys[0].rearrange("h s n c -> n (h s) c")).then_inc(keys_in, 16)
                if name == "out1":
                    emit_norm_rows(sp)
            emit_peer_io(sp)

        @block.gpsimd
        def _(pool):
            step = Steps(pool, pool_step)
            for t, v in ((ones, 1.0), (ident, 0.0), (halves, 0.0), (incl, 1.0), (strict, 1.0),
                         (level, 0.0), (reset, 1.0), (ba, 0.0), (prw[:, :, 0:1 + PAD], 0.0),
                         (pre[:, :, 0:3 + PAD], 0.0), (xnT[:, :, 0:PAD], 0.0)):
                step(nc.gpsimd.memset(t, v))
            step(nc.gpsimd.memset(eps[:, 0:1], 1e-6))
            step(nc.gpsimd.memset(eps[:, 1:2], DK * 1e-6))
            step(nc.gpsimd.memset(eps[:, 2:3], 64e-5))
            step.sync()
            step(nc.gpsimd.affine_select(out=ident, in_=ident, pattern=[[-1, 128]], compare_op=ALU.not_equal,
                                         fill=1.0, base=0, channel_multiplier=1))
            step.sync()
            step(nc.gpsimd.memset(halves[0:64, 0:64], 1.0))
            step.sync()
            step(nc.gpsimd.memset(halves[64:128, 64:128], 1.0))
            step.sync()
            step(nc.gpsimd.affine_select(out=incl, in_=incl, pattern=[[1, TC]], compare_op=ALU.is_ge, fill=0.0,
                                         base=0, channel_multiplier=-1))
            step(nc.gpsimd.affine_select(out=strict, in_=strict, pattern=[[1, TC]], compare_op=ALU.is_gt, fill=0.0,
                                         base=0, channel_multiplier=-1))
            for c in range(NCH):
                step(nc.gpsimd.memset(reset[:, c * TC:c * TC + 1], 0.0))
            odd = []
            for l in range(LEVELS + 1):
                b = 1 << l
                if TC % (2 * b) == 0:
                    odd.append((level[:, l, :].rearrange("p (m s r) -> p m s r", s=2, r=b)[:, :, 1, :], b, TC // (2 * b)))
                else:
                    n = min(b, TC - b)
                    odd.append((level[:, l, b:b + n].rearrange("p (m r) -> p m r", m=1), b, 1))
            for v, b, m in odd:
                step(nc.gpsimd.memset(v, 1.0))
            step.sync()
            for v, b, m in odd:
                step(nc.gpsimd.affine_select(out=v, in_=v, pattern=[[-2 * b, m], [0, v.shape[2]]],
                                             compare_op=ALU.is_ge, fill=0.0, base=0, channel_multiplier=1))
            step.sync()
            for v, b, m in odd:
                step(nc.gpsimd.affine_select(out=v, in_=v, pattern=[[2 * b, m], [0, v.shape[2]]],
                                             compare_op=ALU.is_ge, fill=0.0, base=b - 1, channel_multiplier=-1))
            step.sync()
            nc.gpsimd.memset(gtmp, 0.0).then_inc(consts, 1)
            pool_peer(pool, step)

        @block.tensor
        def _(pe):
            def mm(out, lhsT, rhs, start=True, stop=True, **kw):
                return nc.tensor.matmul(out, lhsT, rhs, start=start, stop=stop, **kw)

            pe.wait_ge(consts, 1)
            for i, n in enumerate(TILE_ROWS):
                pe.wait_ge(xs_ready, i + 1)
                for half in range(2):
                    for q in range(4):
                        k = 4 * half + q
                        ins = nc.tensor.transpose(psv(2 * i + half, 128, 4, 128)[:, q, 0:n],
                                                  xs[0:n, i, k * 128:(k + 1) * 128], ident[0:n, 0:n])
                    ins.then_inc(xT_t, 1)
                if i == 0:
                    pe.wait_ge(par_in, 16 * len(PAR))
                    nc.tensor.transpose(psv(6, 128, PAR_ROWS), parrow[0:PAR_ROWS, :],
                                        ident[0:PAR_ROWS, 0:PAR_ROWS]).then_inc(par_t.sem, 1)
                    pe.wait_ge(small_in, 16 * 8)
                    for f in range(12):
                        nc.tensor.transpose(psv(7, 128, 24, at=24 * f), cconv[0:24, f * 128:(f + 1) * 128],
                                            ident[0:24, 0:24])
                    for f in range(14):
                        ins = nc.tensor.transpose(psv(7, 128, 8, at=288 + 8 * f), cshift[0:8, f * 128:(f + 1) * 128],
                                                  ident[0:8, 0:8])
                    ins.then_inc(cache_t.sem, 1)

            tile = [0]

            def project(name):
                slot = wait_w(pe, name)
                for f in range(place[name][3] // 128):
                    b = tile[0] % 4
                    if tile[0] >= 4:
                        pe.wait_ge(proj_used, tile[0] - 3)
                    for k in range(KT):
                        ins = mm(psv(b, 128, NC - PAD), wslot[slot][:, k, f * 128:(f + 1) * 128], xnT[:, k, PAD:NC],
                                 start=k == 0, stop=k == KT - 1)
                    ins.then_inc(proj_ready, 1)
                    tile[0] += 1

            pe.wait_ge(xT_done, 8)
            for name in ("r", "kr", "vr", "wag"):
                project(name)
            for c in range(NCH + 1):
                cols, n = (ccols(c), TC) if c < NCH else (slice(NP, NC), NS)
                for k in range(KT):
                    ins = mm(psv(4, n, 8, at=8 * c), xnT[:, k, cols], wba[:, k, :], start=k == 0, stop=k == KT - 1)
            ins.then_inc(ba_ready.sem, 1)
            pe.wait_ge(ba_used.sem, ba_used.at(1))
            pe.wait_ge(proj_used, 14)
            for f in range(14):
                ins = nc.tensor.transpose(psv(4 + f // 4, 9, 128, at=128 * (f % 4)), prw[:, f, NP:NP + 9], ident)
                if f % 4 == 3 or f == 13:
                    ins.then_inc(shift_t.sem, 1)
            project("q")
            pe.wait_ge(shift_ready.sem, shift_ready.at(4))
            pe.wait_ge(wag_act.sem, wag_act.at(2))
            for n in range(12):
                if n >= 4:
                    pe.wait_ge(lora_used.sem, lora_used.at(n - 3))
                f = n % 4
                w = (lora[0:64], lora[64:128], g2w)[n // 4][:, f * 128:(f + 1) * 128]
                x = (mix[0:64, 12, :], mix[64:128, 12, :], mix[:, 13, :])[n // 4]
                mm(psv(4 + f, 128, NC), w, x).then_inc(lora_ready.sem, 1)
            project("k")
            pe.wait_ge(lora_used.sem, lora_used.at(12))
            for f in range(4):
                pe.wait_ge(kksq_ready.sem, kksq_ready.at(1))
                mm(psv(4 + f, 128, NC), halves, t0[:, f, :]).then_inc(norm_ready.sem, 1)
            for f in range(4):
                pe.wait_ge(norm_used.sem, norm_used.at(f + 1))
                pe.wait_ge(bonus_in, 1)
                mm(psv(4 + f, 128, NC), halves, t2[:, f, :]).then_inc(bonus_sum.sem, 1)
            project("v")
            pe.wait_ge(bonus_done, 4)
            pe.wait_ge(proj_used, 26)
            for f in range(12):
                ins = nc.tensor.transpose(psv(4 + f // 4, 11, 128, at=128 * (f % 4)), pre[:, f, NP:NP + 11], ident)
                if f % 4 == 3:
                    ins.then_inc(conv_t.sem, 1)
            for c in range(NCH):
                for f in range(4):
                    ins = nc.tensor.transpose(psv(c, TC, 128, at=128 * f), mix[:, 8 + f, ccols(c)], ident)
                ins.then_inc(vtok_t.sem, 1)
            pe.wait_ge(conv_ready.sem, conv_ready.at(3))
            pe.wait_ge(vtok_ready.sem, vtok_ready.at(3))
            pe.wait_ge(qk_sq.sem, qk_sq.at(1))
            for f in range(8):
                mm(psv(f, 128, NC), ones, sqb[:, f, :]).then_inc(qk_sum.sem, 1)
            pe.wait_ge(g_ready, 1)
            pe.wait_ge(qk_root.sem, qk_root.at(8))
            gcols = gt[0:TC, 0:3, :]
            mm(psv(0, TC, 3, 4), incl[0:TC, :], gcols)
            mm(psv(0, 128, 3, 4, at=16), ones[0:TC, :], gcols).then_inc(gsum_ready.sem, 1)
            pe.wait_ge(gb_in, 1)
            for c in range(NCH):
                for h in range(DH):
                    ins = mm(psv(1 + c, 128, TC, at=TC * h), gbc[0:TC, 4 * c + h, :], incl[0:TC, :])
                ins.then_inc(gb_ready.sem, 1)
            pe.wait_ge(qk_done, 1)
            pe.wait_ge(dec_exp.sem, dec_exp.at(2 * NCH))
            for n in range(6):
                c, hp = n // 2, n % 2
                for s in range(2):
                    h = 2 * hp + s
                    ins = mm(psv(n, TC, 2, TC, at=2 * TC * s), qkv[:, 4 + h, ccols(c)], qkv[:, h:h + 5:4, ccols(c)])
                ins.then_inc(kq_ready.sem, 1)
            for n in range(6):
                if n >= 2:
                    pe.wait_ge(tok_ready.sem, tok_ready.at(n - 1))
                c, kv = n // 2, n % 2
                for f in range(4):
                    ins = nc.tensor.transpose(psv(6 + kv, TC, 128, at=128 * f), qkv[:, 4 + 4 * kv + f, ccols(c)], ident)
                ins.then_inc(tok_t.sem, 1)
            pe.wait_ge(tok_ready.sem, tok_ready.at(6))
            pe.wait_ge(rw_vec_ready, 1)
            for n in range(6):
                if n >= 2:
                    pe.wait_ge(prw_ready.sem, prw_ready.at(n - 1))
                c, src = n // 2, (bb, kb)[n % 2]
                for f in range(4):
                    ins = nc.tensor.transpose(psv(6 + n % 2, TC, 128, at=128 * f), src[:, f, ccols(c)], ident)
                ins.then_inc(prw_t.sem, 1)

            def rw_matrix(b, src, g, c, par):
                for s in range(2):
                    f = 2 * g + s
                    rows = slice(64 * par, 64 * par + 64)
                    ins = mm(psv(b, TC, 2, TC, at=2 * TC * s), src[rows, f, ccols(c)], ar[rows, f, :, ccols(c)])
                return ins

            pe.wait_ge(kq_used, 6)
            for n in range(12):
                if n >= 6:
                    pe.wait_ge(rwm_used, n - 5)
                rw_matrix(n % 6, kb, n // 6, n % 6 // 2, n % 2).then_inc(rwm_ready.sem, 1)
            pe.wait_ge(rwm_used, 12)
            pe.wait_ge(prw_ready.sem, prw_ready.at(6))
            for g in range(3):
                if g > 0:
                    for n in range(6):
                        pe.wait_ge(inv_z_used, 18 * g)
                        rw_matrix(n, bb, g - 1, n // 2, n % 2).then_inc(rwb_ready, 1)
                    pe.wait_ge(rwb_used, 6 * g)
                for l in range(LEVELS + 1):
                    for s in range(3):
                        n = (g * LEVELS + l - 1) * 3 + s
                        if l >= 1:
                            pe.wait_ge(inv_c, g * LEVELS + l)
                            pe.wait_ge(inv_x_used, (g * LEVELS + l - 1) * 3 + s + 1)
                            for q in range(4):
                                m = 4 * s + q
                                ins = mm(psv(s, TC, TC, at=TC * q), ct[0:TC, m, :], xx[0:TC, m, :])
                            ins.then_inc(inv_y, 1)
                    for s in range(3):
                        n = (g * LEVELS + l - 1) * 3 + s
                        if l >= 1:
                            pe.wait_ge(inv_y_used, n + 1)
                            for q in range(4):
                                m = 4 * s + q
                                ins = mm(psv(3 + s, TC, TC, at=TC * q), yy[0:TC, m, :], xT[0:TC, 12 * g + m, :])
                            ins.then_inc(inv_z, 1)
                    for s in range(3):
                        n = (g * LEVELS + l - 1) * 3 + s
                        if l < LEVELS:
                            nx = (g * LEVELS + l) * 3 + s
                            if l == 0:
                                pe.wait_ge(inv_first, g + 1)
                            else:
                                pe.wait_ge(inv_z_used, n + 1)
                            if nx >= 2:
                                pe.wait_ge(inv_x_used, nx - 1)
                            for q in range(4):
                                ins = nc.tensor.transpose(psv(6 + nx % 2, TC, TC, at=TC * q),
                                                          xT[0:TC, 12 * g + 4 * s + q, :], ident[0:TC, 0:TC])
                            ins.then_inc(inv_x, 1)
            pe.wait_ge(inv_z_used, 18 * 3)

            for c in range(NCH):
                def xTm(m):
                    return xT[0:TC, m, :]
                if c > 0:
                    pe.wait_ge(dn_s_done, c)
                    for h in range(DH):
                        ins = mm(psv(0, TC, 128, at=128 * h), qkh[:, 4 + h, ccols(c)], s_dn_p[:, 128 * h:128 * h + 128])
                    ins.then_inc(dn_r, 1)
                    pe.wait_ge(rw_s_done, c)
                    pe.wait_ge(rw_yt_used, c)
                for h in range(RH):
                    rows, f, m = slice(64 * (h % 2), 64 * (h % 2) + 64), h // 2, 12 * (h // 4) + 4 * c + h % 4
                    out = psv(4 + h % 2, TC, 64, at=64 * f)
                    if c > 0:
                        mm(out, ar[rows, f, 0, ccols(c)], s_rw_p[rows, f, :], stop=False)
                    ins = mm(out, akT[0:TC, m, :], v_rw[0:TC, c, 64 * h:64 * h + 64], start=c == 0)
                ins.then_inc(rw_r, 1)
                pe.wait_ge(dn_r_done, c + 1)
                for h in range(DH):
                    ins = mm(psv(1, TC, 128, at=128 * h), xTm(4 * c + h), r_buf[0:TC, 128 * h:128 * h + 128])
                ins.then_inc(dn_u, 1)
                pe.wait_ge(rw_r_done, 2 * c + 2)
                if c > 0:
                    pe.wait_ge(rw_u_done, c)
                for h in range(RH):
                    m = 12 + 12 * (h // 4) + 4 * c + h % 4
                    ins = mm(psv(6, TC, 64, at=64 * h), xTm(m), r_bufw[0:TC, 64 * h:64 * h + 64])
                ins.then_inc(rw_u, 1)
                pe.wait_ge(dn_u_done, c + 1)
                for h in range(DH):
                    ins = mm(psv(3, 128, 128, at=128 * h), k_dn[0:TC, c, 128 * h:128 * h + 128],
                             u_buf[0:TC, 128 * h:128 * h + 128])
                ins.then_inc(dn_s, 1)
                if c > 0:
                    pe.wait_ge(dn_ot_used, c)
                for h in range(DH):
                    out = psv(2, TC, 128, at=128 * h)
                    if c > 0:
                        mm(out, qkh[:, h, ccols(c)], s_dn_p[:, 128 * h:128 * h + 128], stop=False)
                    ins = mm(out, qkd[0:TC, 4 * c + h, :], u_buf[0:TC, 128 * h:128 * h + 128], start=c == 0)
                ins.then_inc(dn_o, 1)
                pe.wait_ge(rw_u_done, c + 1)
                for h in range(RH):
                    hs = slice(64 * h, 64 * h + 64)
                    out = psv(7, 128, 64, at=64 * (h // 2))[64 * (h % 2):64 * (h % 2) + 64, :]
                    mm(out, b_rw[0:TC, c, hs], u_bufw[0:TC, hs], stop=False)
                    ins = mm(out, k_rw[0:TC, c, hs], v_rw[0:TC, c, hs], start=False)
                ins.then_inc(rw_s, 1)
                for par in range(2):
                    for h in range(par, RH, 2):
                        hs = slice(64 * h, 64 * h + 64)
                        rows, f, m = slice(64 * par, 64 * par + 64), h // 2, 12 * (h // 4) + 4 * c + h % 4
                        out = psv(4 + par, TC, 64, at=64 * f)
                        if c > 0:
                            mm(out, ar[rows, f, 1, ccols(c)], s_rw_p[rows, f, :], stop=False)
                        mm(out, rbT[0:TC, m, :], u_bufw[0:TC, hs], start=c == 0, stop=False)
                        ins = mm(out, rkT[0:TC, m, :], v_rw[0:TC, c, hs], start=False)
                    ins.then_inc(rw_y, 1)
                pe.wait_ge(dn_on, c + 1)
                for h in range(DH):
                    ins = nc.tensor.transpose(psv(2, 128, TC, at=TC * h), on_o[0:TC, 128 * h:128 * h + 128],
                                              ident[0:TC, 0:TC])
                ins.then_inc(dn_ot, 1)
                pe.wait_ge(rw_yn, c + 1)
                for f in range(4):
                    ins = nc.tensor.transpose(psv(4, 128, TC, at=TC * f), yw_o[0:TC, 128 * f:128 * f + 128],
                                              ident[0:TC, 0:TC])
                ins.then_inc(rw_yt, 1)
            pe_rest(pe, mm)

        @block.scalar
        def _(act):
            step = Steps(act, act_step)

            def fn(out, in_, func=ACT.Copy, **kw):
                return nc.scalar.activation(out, in_, func, **kw)

            act.wait_ge(x_in, 64)
            act.wait_ge(consts, 1)
            for i, n in enumerate(TILE_ROWS):
                step(fn(xs[0:n, i, :], xtok[0:n, i, :], ACT.Square, accum_out=ss[0:n, i:i + 1]))
            for i, n in enumerate(TILE_ROWS):
                step.sync(2 - i)
                fn(rs[0:n, i:i + 1], ss[0:n, i:i + 1], ACT.Sqrt, scale=1.0 / D,
                   bias=eps[0:n, 0:1]).then_inc(rs_ready, 1)
            act.wait_ge(par_t.sem, par_t.at(1))
            fn(par, psv(6, 128, PAR_ROWS)).then_inc(par_ready.sem, 1)
            act.wait_ge(cache_t.sem, cache_t.at(1))
            fn(cconvT.rearrange("p f c -> p (f c)"), psv(7, 128, 288)).then_inc(cache_ready.sem, 1)
            fn(cshiftT.rearrange("p f c -> p (f c)"), psv(7, 128, 112, at=288)).then_inc(cache_ready.sem, 1)
            tile = [0]

            def evacuate(dests, func=ACT.Copy, n=NC - PAD):
                for d in dests:
                    act.wait_ge(proj_ready, tile[0] + 1)
                    fn(d, psv(tile[0] % 4, 128, n), func).then_inc(proj_used, 1)
                    tile[0] += 1

            evacuate([prw[:, f, 1 + PAD:1 + NC] for f in range(14)])
            act.wait_ge(ba_ready.sem, ba_ready.at(1))
            step(fn(ba[0:TC, 0:3, :], psv(4, TC, 3, 8)))
            fn(ba[0:NS, 3, :], psv(4, NS, 8, at=24)).then_inc(ba_used.sem, 1)
            act.wait_ge(par2_ready, 1)
            act.wait_ge(proj_used, 14)
            for f in range(14):
                fn(mix[:, f, 0:NP], prw[:, f, 1:1 + NP], scale=omu[:, f:f + 1]).then_inc(mix_part.sem, 1)
            for b in range(4):
                act.wait_ge(shift_t.sem, shift_t.at(b + 1))
                n = 512 if b < 3 else 256
                fn(shift_out[0:9, 512 * b:512 * b + n], psv(4 + b, 9, n)).then_inc(shift_ready.sem, 1)
            act.wait_ge(mix_ready, 1)
            fn(mix[0:64, 12, :], mix[0:64, 12, :], ACT.Tanh).then_inc(wag_act.sem, 1)
            fn(mix[:, 13, :], mix[:, 13, :], ACT.Sigmoid).then_inc(wag_act.sem, 1)
            evacuate([pre[:, f, 3 + PAD:3 + NC] for f in range(4)])
            for n in range(12):
                f = n % 4
                act.wait_ge(lora_ready.sem, lora_ready.at(n + 1))
                p = psv(4 + f, 128, NC)
                if n < 4:
                    ins = fn(ld[:, f, :], p, ACT.Sigmoid, bias=par[:, PAR_AT["w0"] + f:PAR_AT["w0"] + f + 1])
                elif n < 8:
                    ins = fn(aa[:, f, :], p, ACT.Sigmoid, bias=par[:, PAR_AT["a0"] + f:PAR_AT["a0"] + f + 1])
                else:
                    ins = fn(gate[:, f, :], p)
                ins.then_inc(lora_used.sem, 1)
            act.wait_ge(kk0_ready, 1)
            act.wait_ge(shift_t.sem, shift_t.at(4))
            fn(t0, kk, ACT.Square).then_inc(kksq_ready.sem, 1)
            evacuate([pre[:, 4 + f, 3 + PAD:3 + NC] for f in range(4)])
            for f in range(4):
                act.wait_ge(norm_ready.sem, norm_ready.at(f + 1))
                fn(t1[:, f, :], psv(4 + f, 128, NC), ACT.Sqrt, bias=eps[:, 0:1]).then_inc(norm_used.sem, 1)
            act.wait_ge(cum_ready, 2)
            act.wait_ge(norm_ready.sem, norm_ready.at(4))
            fn(t0[:, :, 0:NP], cum[:, :, 0:NP], ACT.Exp).then_inc(exp_ready.sem, 1)
            fn(t1[:, :, 0:NP], cum[:, :, 0:NP], ACT.Exp, scale=-1.0).then_inc(exp_ready.sem, 1)
            fn(t2[:, :, 0:NP], t2[:, :, 0:NP], ACT.Exp).then_inc(exp_ready.sem, 1)
            fn(sv[:, 1, :, :], ld[:, :, NP:NC], ACT.Exp).then_inc(exp_ready.sem, 1)
            evacuate([pre[:, 8 + f, 3 + PAD:3 + NC] for f in range(4)])
            act.wait_ge(proj_used, 26)
            act.wait_ge(par_t.sem, par_t.at(1))
            for b in range(3):
                act.wait_ge(conv_t.sem, conv_t.at(b + 1))
                fn(conv_out[0:11, 512 * b:512 * b + 512], psv(4 + b, 11, 512)).then_inc(conv_ready.sem, 1)
            act.wait_ge(rw_vec_ready, 1)
            for c in range(NCH):
                act.wait_ge(vtok_t.sem, vtok_t.at(c + 1))
                fn(v_rw[0:TC, c, :], psv(c, TC, 512)).then_inc(vtok_ready.sem, 1)
            act.wait_ge(vtok_ready.sem, vtok_ready.at(3))
            for f in range(12):
                w = par[:, PAR_AT["conv"] + 36 + f:PAR_AT["conv"] + 37 + f]
                fn(qkv[:, f, 0:NP], pre[:, f, 3:3 + NP], scale=w).then_inc(tap_ready.sem, 1)
            act.wait_ge(conv_done, 1)
            for i in range(3):
                fn(qkv[:, 4 * i:4 * i + 4, :], qkv[:, 4 * i:4 * i + 4, :], ACT.Silu).then_inc(silu_done.sem, 1)
            act.wait_ge(silu_done.sem, silu_done.at(2))
            fn(sqb, qkv[:, 0:8, :], ACT.Square).then_inc(qk_sq.sem, 1)
            for f in range(8):
                act.wait_ge(qk_sum.sem, qk_sum.at(f + 1))
                fn(rnb[:, f, :], psv(f, 128, NC), ACT.Sqrt, scale=float(DK) if f < 4 else 1.0,
                   bias=eps[:, 1:2] if f < 4 else eps[:, 0:1]).then_inc(qk_root.sem, 1)
            act.wait_ge(ln_done, 1)
            step(fn(gtmp, gtmp, ACT.Exp, scale=-1.0))
            step.sync()
            step(fn(gtmp, gtmp, ACT.Ln, bias=1.0))
            step(fn(bt, ba[:, :, 0:4], ACT.Exp, scale=-1.0))
            fn(alog, alog, ACT.Exp).then_inc(ln_done, 1)
            act.wait_ge(gb_in, 1)
            step(fn(gend, psv(0, 128, 3, 4, at=16), ACT.Exp))
            fn(gout[0:TC], gout[0:TC], ACT.Exp).then_inc(gexp_done.sem, 1)
            for c in range(NCH):
                act.wait_ge(gb_ready.sem, gb_ready.at(c + 1))
                act.wait_ge(dec_in, c + 1)
                fn(edec[:, 4 * c:4 * c + 4, :], psv(1 + c, 128, 4, TC), ACT.Exp).then_inc(dec_exp.sem, 1)
                fn(dec[0:TC, 4 * c:4 * c + 4, :], dec[0:TC, 4 * c:4 * c + 4, :], ACT.Exp).then_inc(dec_exp.sem, 1)
            act.wait_ge(gexp_done.sem, gexp_done.at(1))
            act.wait_ge(dec_ready, 1)
            for n in range(6):
                act.wait_ge(tok_t.sem, tok_t.at(n + 1))
                c = n // 2
                if n % 2 == 0:
                    for h in range(DH):
                        ins = fn(k_dn[0:TC, c, 128 * h:128 * h + 128], psv(6, TC, 128, at=128 * h),
                                 scale=gout[0:TC, c, h:h + 1])
                        if h < DH - 1:
                            step(ins)
                else:
                    ins = fn(v_dn[0:TC, c, :], psv(7, TC, 512))
                ins.then_inc(tok_ready.sem, 1)
            act.wait_ge(shift_sent, 32)
            for n in range(6):
                act.wait_ge(prw_t.sem, prw_t.at(n + 1))
                fn((b_rw, k_rw)[n % 2][0:TC, n // 2, :], psv(6 + n % 2, TC, 512)).then_inc(prw_ready.sem, 1)
            for g in range(3):
                for l in range(LEVELS + 1):
                    for s in range(3):
                        if l >= 1:
                            act.wait_ge(inv_y, (g * LEVELS + l - 1) * 3 + s + 1)
                            fn(yy[0:TC, 4 * s:4 * s + 4, :], psv(s, TC, 4, TC)).then_inc(inv_y_used, 1)
                    for s in range(3):
                        if l < LEVELS:
                            nx = (g * LEVELS + l) * 3 + s
                            act.wait_ge(inv_x, nx + 1)
                            fn(xx[0:TC, 4 * s:4 * s + 4, :], psv(6 + nx % 2, TC, 4, TC)).then_inc(inv_x_used, 1)
            for c in range(NCH):
                for par_ in range(2):
                    act.wait_ge(rw_r, c + 1)
                    src = psv(4 + par_, TC, 4, 64)
                    fn(r_bufw[0:TC].rearrange("p (f s v) -> p f s v", f=4, s=2)[:, :, par_, :], src).then_inc(rw_r_done, 1)
                act.wait_ge(rw_u, c + 1)
                fn(u_bufw[0:TC], psv(6, TC, 512), scale=-1.0).then_inc(rw_u_done, 1)
                act.wait_ge(dn_o, c + 1)
                step(fn(o_buf[0:TC], psv(2, TC, 512)))
                if c > 0:
                    act.wait_ge(dn_on, c)
                fn(sq_o[0:TC], psv(2, TC, 512), ACT.Square).then_inc(dn_o_used, 1)
                act.wait_ge(dn_ss, c + 1)
                fn(stat[0:TC, 4:8], stat[0:TC, 0:4], ACT.Sqrt, scale=1.0 / DK, bias=eps[0:TC, 0:1]).then_inc(dn_root, 1)
                act.wait_ge(rw_c, c + 1)
                fn(sqw_o[0:TC], yw_o[0:TC], ACT.Square).then_inc(rw_sq, 1)
                act.wait_ge(rw_var, c + 1)
                fn(stat[0:TC, 24:32], stat[0:TC, 16:24], ACT.Sqrt, scale=1.0 / RN, bias=eps[0:TC, 2:3]).then_inc(rw_root, 1)
                act.wait_ge(dn_ot, c + 1)
                fn(odn[:, :, ccols(c)], psv(2, 128, 4, TC)).then_inc(dn_ot_used, 1)
                act.wait_ge(rw_yt, c + 1)
                fn(orw[:, :, ccols(c)], psv(4, 128, 4, TC)).then_inc(rw_yt_used, 1)
            act_rest(act, step, fn, evacuate)

        @block.vector
        def _(dve):
            step = Steps(dve, vec_step)
            v = nc.vector
            tt, ts, stt = v.tensor_tensor, v.tensor_scalar, v.scalar_tensor_tensor

            def pc(name, f=0, n=1):
                return par[:, PAR_AT[name] + f:PAR_AT[name] + f + n]

            for i, n in enumerate(TILE_ROWS):
                dve.wait_ge(rs_ready, i + 1)
                step(v.reciprocal(rs[0:n, i:i + 1], rs[0:n, i:i + 1]))
                step.sync()
                ts(xs[0:n, i, :], xtok[0:n, i, :], rs[0:n, i:i + 1], None, ALU.mult).then_inc(xs_ready, 1)
            dve.wait_ge(par_ready.sem, par_ready.at(1))
            step(ts(omu, pc("mu", 0, 14), -1.0, 1.0, ALU.mult, ALU.add))
            ts(omka, pc("k_a", 0, 4), -1.0, 1.0, ALU.mult, ALU.add).then_inc(par2_ready, 1)
            for i in range(3):
                for half in range(2):
                    dve.wait_ge(xT_t, 2 * i + half + 1)
                    ks = slice(4 * half, 4 * half + 4)
                    moves = ([(slice(0, 128), slice(T0 + 128 * i, T0 + 128 * i + 128))] if i < 2 else
                             [(slice(0, NS), slice(NP, NC)), (slice(NS, NS + META), slice(PAD, T0))])
                    for a, b in moves:
                        src = psv(2 * i + half, 128, 4, 128)[:, :, a]
                        n = a.stop - a.start
                        tt(xnT[:, ks, b], src, row(pc("ln1", 4 * half, 4), 128, 4, n), ALU.mult).then_inc(xT_done, 1)
            dve.wait_ge(par2_ready, 1)
            for f in range(14):
                dve.wait_ge(mix_part.sem, mix_part.at(f + 1))
                step(stt(mix[:, f, 0:NP], prw[:, f, 0:NP], pc("mu", f), mix[:, f, 0:NP], ALU.mult, ALU.add))
            dve.wait_ge(cache_ready.sem, cache_ready.at(2))
            step(tt(dmix, cshiftT, prw[:, :, 1 + NP:1 + NC], ALU.subtract))
            step.sync()
            step(tt(dmix, dmix, row(pc("mu", 0, 14), 128, 14, 8), ALU.mult))
            step.sync()
            tt(mix[:, :, NP:NC], dmix, prw[:, :, 1 + NP:1 + NC], ALU.add).then_inc(mix_ready, 1)
            mr, mk, mv = mix[:, 0:4, :], mix[:, 4:8, :], mix[:, 8:12, :]
            dve.wait_ge(mix_ready, 1)
            for f in range(4):
                ins = ts(kk[:, f, :], mk[:, f, :], pc("k_k", f), None, ALU.mult)
                if f < 3:
                    step(ins)
            ins.then_inc(kk0_ready, 1)
            dve.wait_ge(lora_used.sem, lora_used.at(4))
            step(ts(ld, ld, -EDEC, None, ALU.mult))
            step.sync()
            for f in range(4):
                step(v.tensor_tensor_scan(cum[:, f, 0:NP], reset, ld[:, f, 0:NP], 0.0, ALU.mult, ALU.add))
            step.sync()
            v.tensor_copy(sv[:, 3], mv[:, :, NP:NC]).then_inc(cum_ready, 1)
            dve.wait_ge(lora_used.sem, lora_used.at(8))
            for f in range(4):
                step(ts(t2[:, f, :], aa[:, f, :], pc("k_a", f), omka[:, f:f + 1], ALU.mult, ALU.add))
            step.sync()
            step(tt(mk, mk, t2, ALU.mult))
            step.sync()
            for f in range(4):
                ins = stt(t2[:, f, :], mk[:, f, :], pc("r_k", f), mr[:, f, :], ALU.mult, ALU.mult)
                if f < 3:
                    step(ins)
            ins.then_inc(bonus_in, 1)
            dve.wait_ge(norm_used.sem, norm_used.at(4))
            step(v.reciprocal(t1, t1))
            step.sync()
            step(tt(kk, kk, t1, ALU.mult))
            for f in range(4):
                dve.wait_ge(bonus_sum.sem, bonus_sum.at(f + 1))
                tt(bonus[:, f, :], psv(4 + f, 128, NC), mv[:, f, :], ALU.mult).then_inc(bonus_done, 1)
            step.sync()
            step(tt(aa, aa, kk, ALU.mult))
            step(tt(t2[:, :, 0:NP], cum[:, :, 0:NP], ld[:, :, 0:NP], ALU.subtract))
            step.sync()
            v.tensor_copy(sv[:, 5], aa[:, :, NP:NC]).then_inc(cum_ready, 1)
            step(v.tensor_copy(sv[:, 0], mr[:, :, NP:NC]))
            step(v.tensor_copy(sv[:, 2], mk[:, :, NP:NC]))
            step(v.tensor_copy(sv[:, 4], kk[:, :, NP:NC]))
            dve.wait_ge(shift_sent, 32)
            dve.wait_ge(exp_ready.sem, exp_ready.at(1))
            step(v.tensor_copy(wc, t0[:, :, TC - 1:NP:TC]))
            step(tt(ar[:, :, 1, :], mr[:, :, 0:NP], t0[:, :, 0:NP], ALU.mult))
            dve.wait_ge(exp_ready.sem, exp_ready.at(2))
            step(tt(bb, aa[:, :, 0:NP], t1[:, :, 0:NP], ALU.mult))
            step(tt(kb, mk[:, :, 0:NP], t1[:, :, 0:NP], ALU.mult))
            dve.wait_ge(exp_ready.sem, exp_ready.at(3))
            tt(ar[:, :, 0, :], kk[:, :, 0:NP], t2[:, :, 0:NP], ALU.mult).then_inc(rw_vec_ready, 1)
            dve.wait_ge(vtok_ready.sem, vtok_ready.at(3))
            cw = [row(pc("conv", 12 * j, 12), 128, 12, 8) for j in range(4)]
            cc = cconvT.rearrange("p f (b j) -> p f b j", j=3)
            dve.wait_ge(proj_used, 26)
            qs = qkv[:, :, NP:NC]
            step(tt(qs, pre[:, :, 3 + NP:3 + NC], cw[3], ALU.mult))
            for j in range(3):
                step.sync()
                step(tt(cst, cc[:, :, :, j], cw[j], ALU.mult))
                step.sync()
                step(tt(qs, qs, cst, ALU.add))
            for j in range(3):
                for f in range(12):
                    if j == 0:
                        dve.wait_ge(tap_ready.sem, tap_ready.at(f + 1))
                    else:
                        step.sync(11)
                    ins = stt(qkv[:, f, 0:NP], pre[:, f, j:j + NP], pc("conv", 12 * j + f), qkv[:, f, 0:NP],
                              ALU.mult, ALU.add)
                    if j == 2 and f == 11:
                        ins.then_inc(conv_done, 1)
                    else:
                        step(ins)
            step(tt(gt, ba[:, :, 4:8], dtb.unsqueeze(1).broadcast_to([128, 4, 4]), ALU.add))
            step.sync()
            step(ts(gtmp, gt, -1.0, None, ALU.mult))
            step.sync()
            tt(gtmp, gtmp, gt, ALU.max).then_inc(ln_done, 1)
            dve.wait_ge(ln_done, 2)
            step(stt(gt, gt, 0.0, gtmp, ALU.max, ALU.add))
            step(ts(bt, bt, 1.0, None, ALU.add))
            step.sync()
            step(v.reciprocal(bt, bt))
            stt(gt, gt, -1.0, alog.unsqueeze(1).broadcast_to([128, 4, 4]), ALU.mult, ALU.mult).then_inc(g_ready, 1)
            dve.wait_ge(qk_root.sem, qk_root.at(8))
            step(v.reciprocal(rnb, rnb))
            step.sync()
            step(tt(qkv[:, 0:8, :], qkv[:, 0:8, :], rnb, ALU.mult))
            dve.wait_ge(silu_done.sem, silu_done.at(3))
            step.sync()
            v.tensor_copy(sd, qkv[:, :, NP:NC]).then_inc(qk_done, 1)
            dve.wait_ge(g_ready, 1)
            dve.wait_ge(gsum_ready.sem, gsum_ready.at(1))
            step(v.tensor_copy(gcum[0:TC], psv(0, TC, 3, 4)))
            step.sync()
            step(v.tensor_copy(gbc[0:TC], gt[0:TC, 0:3, :].rearrange("p c h -> p (c h)").unsqueeze(2).broadcast_to([TC, 12, 128])))
            tt(gout[0:TC], psv(0, TC, 3, 4, at=16), gcum[0:TC], ALU.subtract).then_inc(gb_in, 1)
            gc12 = gcum[0:TC].rearrange("p c h -> p (c h)")
            for c in range(NCH):
                dve.wait_ge(gb_ready.sem, gb_ready.at(c + 1))
                g4 = slice(4 * c, 4 * c + 4)
                step(tt(dec[0:TC, g4, :], psv(1 + c, TC, 4, TC), row(gc12[:, g4], TC, 4, TC), ALU.subtract))
                step.sync()
                ts(dec[0:TC, g4, :], dec[0:TC, g4, :], 0.0, None, ALU.min).then_inc(dec_in, 1)
            dve.wait_ge(dec_exp.sem, dec_exp.at(6))
            dve.wait_ge(conv_sent, 32)
            for c in range(NCH):
                e = edec[:, 4 * c:4 * c + 4, :]
                step(tt(qkh[:, 0:4, ccols(c)], qkv[:, 0:4, ccols(c)], e, ALU.mult))
                step(tt(qkh[:, 4:8, ccols(c)], qkv[:, 4:8, ccols(c)], e, ALU.mult))
            step(tt(dst[0:TC], dec[0:TC], strict[0:TC].unsqueeze(1).broadcast_to([TC, 12, TC]), ALU.mult))
            step.sync()
            tt(dec[0:TC], dec[0:TC], incl[0:TC].unsqueeze(1).broadcast_to([TC, 12, TC]), ALU.mult).then_inc(dec_ready, 1)
            dve.wait_ge(dec_ready, 1)
            for n in range(6):
                dve.wait_ge(kq_ready.sem, kq_ready.at(n + 1))
                c, hp = n // 2, n % 2
                p = psv(n, TC, 2, 2, TC)
                for s in range(2):
                    h = 2 * hp + s
                    step(stt(bT[0:TC, 4 * c + h, :], p[:, s, 1, :], bt[0:TC, c, h:h + 1], dst[0:TC, 4 * c + h, :],
                             ALU.mult, ALU.mult))
                hs = slice(4 * c + 2 * hp, 4 * c + 2 * hp + 2)
                tt(qkd[0:TC, hs, :], p[:, :, 0, :], dec[0:TC, hs, :], ALU.mult).then_inc(kq_used, 1)

            def pair(base, g, n):
                m = 12 * g + 4 * (n // 2) + n % 2
                return base[0:TC, m:m + 3:2, :]

            m_incl = incl[0:TC].unsqueeze(1).broadcast_to([TC, 2, TC])
            m_strict = strict[0:TC].unsqueeze(1).broadcast_to([TC, 2, TC])
            for n in range(12):
                dve.wait_ge(rwm_ready.sem, rwm_ready.at(n + 1))
                p = psv(n % 6, TC, 2, 2, TC)
                step(tt(pair(akT, n // 6, n % 6), p[:, :, 0, :], m_strict, ALU.mult))
                tt(pair(rkT, n // 6, n % 6), p[:, :, 1, :], m_incl, ALU.mult).then_inc(rwm_used, 1)
            for g in range(3):
                if g > 0:
                    for n in range(6):
                        dve.wait_ge(rwb_ready, 6 * (g - 1) + n + 1)
                        p = psv(n, TC, 2, 2, TC)
                        step(tt(pair(bT, 0, n), p[:, :, 0, :], m_strict, ALU.mult))
                        tt(pair(rbT, g - 1, n), p[:, :, 1, :], m_incl, ALU.mult).then_inc(rwb_used, 1)
                xg = xT[0:TC, 12 * g:12 * g + 12, :]
                for l in range(LEVELS + 1):
                    mask = level[0:TC, l, :].unsqueeze(1).broadcast_to([TC, 12, TC])
                    if l == 0:
                        step.sync()
                        step(tt(xg, bT[0:TC], mask, ALU.mult))
                        step.sync()
                        tt(xg, ident[0:TC, 0:TC].unsqueeze(1).broadcast_to([TC, 12, TC]), xg,
                           ALU.subtract).then_inc(inv_first, 1)
                    else:
                        n = (g * LEVELS + l - 1) * 3
                        if n > 0:
                            dve.wait_ge(inv_y, n)
                        tt(ct[0:TC], bT[0:TC], mask, ALU.mult).then_inc(inv_c, 1)
                        for s in range(3):
                            dve.wait_ge(inv_z, n + s + 1)
                            xs4 = xT[0:TC, 12 * g + 4 * s:12 * g + 4 * s + 4, :]
                            tt(xs4, xs4, psv(3 + s, TC, 4, TC), ALU.subtract).then_inc(inv_z_used, 1)
                        if l == 1:
                            dve.wait_ge(inv_first, g + 1)

            for c in range(NCH):
                if c == 0:
                    dve.wait_ge(tok_ready.sem, tok_ready.at(6))
                    v.tensor_copy(r_buf[0:TC], v_dn[0:TC, 0, :]).then_inc(dn_r_done, 1)
                else:
                    dve.wait_ge(dn_r, c)
                    tt(r_buf[0:TC], v_dn[0:TC, c, :], psv(0, TC, 512), ALU.subtract).then_inc(dn_r_done, 1)
                dve.wait_ge(dn_u, c + 1)
                tt(u_buf[0:TC].rearrange("p (h v) -> p h v", h=4), psv(1, TC, 4, 128), row(bt[0:TC, c, :], TC, 4, 128),
                   ALU.mult).then_inc(dn_u_done, 1)
                dve.wait_ge(dn_o, c + 1)
                dve.wait_ge(dn_s, c + 1)
                sp4 = s_dn_p.rearrange("p (h v) -> p h v", h=4)
                if c == 0:
                    v.tensor_copy(s_dn_p, psv(3, 128, 512)).then_inc(dn_s_done, 1)
                else:
                    step(tt(sp4, sp4, row(gend[:, c, :], 128, 4, 128), ALU.mult))
                    step.sync()
                    tt(s_dn_p, s_dn_p, psv(3, 128, 512), ALU.add).then_inc(dn_s_done, 1)
                dve.wait_ge(rw_s, c + 1)
                dve.wait_ge(rw_y, 2 * c + 2)
                if c > 0:
                    step(tt(s_rw_p, s_rw_p, psv(7, 128, 4, 64), ALU.add))
                    step.sync()
                tt(s_rw_p, s_rw_p if c > 0 else psv(7, 128, 4, 64), row(wc[:, :, c], 128, 4, 64),
                   ALU.mult).then_inc(rw_s_done, 1)
                dve.wait_ge(dn_o_used, c + 1)
                v.tensor_reduce(stat[0:TC, 0:4], sq_o[0:TC].rearrange("p (h v) -> p h v", h=4), AX,
                                ALU.add).then_inc(dn_ss, 1)
                for par_ in range(2):
                    step(v.tensor_reduce(stat[0:TC, 8 + par_:16:2], psv(4 + par_, TC, 4, 64), AX, ALU.add))
                step.sync()
                step(ts(stat[0:TC, 8:16], stat[0:TC, 8:16], 1.0 / RN, None, ALU.mult))
                step.sync()
                if c > 0:
                    dve.wait_ge(rw_yt, c)
                yw = yw_o[0:TC].rearrange("p (f s v) -> p f s v", f=4, s=2)
                for par_ in range(2):
                    ins = tt(yw[:, :, par_, :], psv(4 + par_, TC, 4, 64), row(stat[0:TC, 8 + par_:16:2], TC, 4, 64),
                             ALU.subtract)
                    if par_ == 0:
                        step(ins)
                ins.then_inc(rw_c, 1)
                dve.wait_ge(dn_root, c + 1)
                step(v.reciprocal(stat[0:TC, 4:8], stat[0:TC, 4:8]))
                step.sync()
                if c > 0:
                    dve.wait_ge(dn_ot, c)
                tt(on_o[0:TC].rearrange("p (h v) -> p h v", h=4), o_buf[0:TC].rearrange("p (h v) -> p h v", h=4),
                   row(stat[0:TC, 4:8], TC, 4, 128), ALU.mult).then_inc(dn_on, 1)
                dve.wait_ge(rw_sq, c + 1)
                v.tensor_reduce(stat[0:TC, 16:24], sqw_o[0:TC].rearrange("p (h v) -> p h v", h=8), AX,
                                ALU.add).then_inc(rw_var, 1)
                dve.wait_ge(rw_root, c + 1)
                step(v.reciprocal(stat[0:TC, 24:32], stat[0:TC, 24:32]))
                step.sync()
                y8 = yw_o[0:TC].rearrange("p (h v) -> p h v", h=8)
                tt(y8, y8, row(stat[0:TC, 24:32], TC, 8, 64), ALU.mult).then_inc(rw_yn, 1)
            vec_rest(dve, step, v, tt, ts, stt, pc)


_INS = ["x_prompt", "x_sample", "cache_dn_conv", "state_dn", "cache_rw_shift", "state_rw", "meta_tokens", "ln1", "w_in",
        "dn_conv_w", "dn_a_log", "dn_dt_bias", "dn_norm_w", "rw_mu", "rw_w0", "rw_w2", "rw_a0", "rw_a2", "rw_g2",
        "rw_k_k", "rw_k_a", "rw_r_k", "rw_gn_w", "rw_gn_b", "w_up_dn", "w_up_rw", "w_out", "ln2", "peer_wq",
        "peer_keys", "peer_u", "peer_v", "ln_f"]
_OUTS = [(1, 256, 1024), (8, 1, 1024), (1, 1, 3, 1536), (1, 1, 4, 128, 128), (1, 1, 1, 1792), (1, 1, 8, 64, 64),
         (1, 8, 3, 1536), (1, 8, 4, 128, 128), (1, 8, 1, 1792), (1, 8, 8, 64, 64)]


def kernel(**inputs):
    import numpy as _np
    import concourse.bacc as _bacc
    from concourse import mybir as _mybir
    from concourse.bass_utils import run_bass_kernel_spmd as _run

    nc = _bacc.Bacc("TRN2", target_bir_lowering=False, num_devices=1)
    arrays, args = {}, []
    for name in _INS:
        a = _np.ascontiguousarray(inputs[name])
        arrays[f"in_{name}"] = a
        args.append(nc.dram_tensor(f"in_{name}", a.shape, _mybir.dt.from_np(a.dtype), kind="ExternalInput").ap())
    for i, shape in enumerate(_OUTS):
        args.append(nc.dram_tensor(f"out_{i}", shape, _mybir.dt.float32, kind="ExternalOutput").ap())
    hybrid_step(nc, *args)
    r = _run(nc, [arrays], core_ids=[0])
    return tuple(r.results[0][f"out_{i}"] for i in range(len(_OUTS)))
```

```python
from contextlib import ExitStack

import concourse.bass as bass
from concourse import mybir

F32 = mybir.dt.float32
U32 = mybir.dt.uint32
ALU = mybir.AluOpType
ACT = mybir.ActivationFunctionType
AX = mybir.AxisListType.X

D = 1024
KT = D // 128
SEQ, META, NS = 256, 16, 8
PAD = 16
TC, NCH = 96, 3
NP = TC * NCH
NC = NP + NS
T0 = PAD + META
NX = NC - T0
DH, DK = 4, 128
RH, RN = 8, 64
NQKV, OZ, OBETA, ORW, NRW = 1536, 1536, 2048, 2056, 1792
OGATE = ORW + NRW
PH, PK, PT = 8, 128, 16
SLOT = 4096
NCAND = 54
PAIRS = [(0, 1, 16), (1, 1, 8), (2, 2, 5), (4, 4, 3), (8, 8, 1)]
LEVELS = 6
EDEC = float(2.718281828459045 ** -0.5)
GELU_C = 0.7978845608028654
NEG = -3.0e38

PAR = [("ln1", 8), ("conv", 48), ("mu", 14), ("w0", 4), ("a0", 4), ("k_k", 4), ("k_a", 4), ("r_k", 4),
       ("gn_w", 4), ("gn_b", 4), ("dn_norm", 1)]
PAR_AT = {name: sum(n for _, n in PAR[:i]) for i, (name, _) in enumerate(PAR)}
PAR_ROWS = sum(n for _, n in PAR)


class Steps:

    def __init__(self, eng, sem, base=0):
        self.eng, self.sem, self.n, self.base = eng, sem, 0, base

    def __call__(self, instruction):
        instruction.then_inc(self.sem, 1)
        self.n += 1

    def sync(self, lag=0):
        if self.n > lag:
            self.eng.wait_ge(self.sem, self.base + self.n - lag)


class Signal:

    def __init__(self, sem, before):
        self.sem, self.before = sem, before

    def at(self, n):
        return self.before + n


def series(sem, *counts):
    return [Signal(sem, sum(counts[:i])) for i in range(len(counts))]


def hybrid_step(nc, x_prompt, x_sample, cache_dn_conv, state_dn, cache_rw_shift, state_rw, meta_tokens, ln1, w_in,
                dn_conv_w, dn_a_log, dn_dt_bias, dn_norm_w, rw_mu, rw_w0, rw_w2, rw_a0, rw_a2, rw_g2, rw_k_k,
                rw_k_a, rw_r_k, rw_gn_w, rw_gn_b, w_up_dn, w_up_rw, w_out, ln2, peer_wq, peer_keys, peer_u,
                peer_v, ln_f, y_prompt, y_sample, p_conv, p_dn, p_shift, p_rw, s_conv, s_dn, s_shift, s_rw):
    with ExitStack() as ctx:
        sb_all = ctx.enter_context(nc.sbuf_tensor("sb_all", [128, 52900], F32))
        bank = [ctx.enter_context(nc.psum_tensor(f"bank{i}", [128, 512], F32)) for i in range(8)]

        def sem(name):
            return ctx.enter_context(nc.semaphore(name))

        def view(at, *shape):
            n = 1
            for s in shape:
                n *= s
            v = sb_all[:, at:at + n]
            if len(shape) == 2:
                v = v.rearrange("p (a b) -> p a b", a=shape[0])
            if len(shape) == 3:
                v = v.rearrange("p (a b c) -> p a b c", a=shape[0], b=shape[1])
            return v

        def psv(b, n, *shape, at=0):
            size = 1
            for s in shape:
                size *= s
            v = bank[b][0:n, at:at + size]
            if len(shape) == 2:
                v = v.rearrange("p (a b) -> p a b", a=shape[0])
            if len(shape) == 3:
                v = v.rearrange("p (a b c) -> p a b c", a=shape[0], b=shape[1])
            return v

        def row(v, n, *shape):
            return v.unsqueeze(len(v.shape)).broadcast_to([n, *shape])

        at = [0]

        def take(n):
            at[0] += n
            return at[0] - n

        W = take(3 * SLOT)
        wslot = [view(W + i * SLOT, KT, 512) for i in range(3)]
        ident = view(take(128), 128)
        ones = view(take(128), 128)
        halves = view(take(128), 128)
        incl = view(take(TC), TC)
        strict = view(take(TC), TC)
        level = view(take((LEVELS + 1) * TC), LEVELS + 1, TC)
        reset = view(take(NP), NP)
        par = view(take(PAR_ROWS), PAR_ROWS)
        omu = view(take(14), 14)
        omka = view(take(4), 4)
        eps = view(take(4), 4)
        ss = view(take(4), 4)
        rs = view(take(4), 4)
        ba = view(take(32), 4, 8)
        bt = view(take(16), 4, 4)
        gt = view(take(16), 4, 4)
        gtmp = view(take(16), 4, 4)
        dtb = view(take(4), 4)
        alog = view(take(4), 4)
        gcum = view(take(12), 3, 4)
        gend = view(take(12), 3, 4)
        gout = view(take(12), 3, 4)
        wc = view(take(12), 4, 3)
        stat = view(take(64), 64)
        sd = view(take(96), 12, 8)
        sdv = view(take(8 * 32), 8, 32)
        sv = view(take(192), 6, 4, 8)
        wba = view(take(64), 8, 8)
        XN = take(KT * NC)
        xnT = view(XN, KT, NC)
        A, B, C, E, G, H = take(3588), take(4158), take(4144), take(4736), take(4608), take(2368)
        I1, I2, I3, I4, T = take(2304), take(1536), take(1536), take(1152), take(4608)
        assert at[0] <= 52900, at[0]

        xtok = view(C, 3, D)
        xs = view(E, 3, D)
        parrow = view(I1, 128)
        pre = view(A, 12, 3 + NC)
        prw = view(B, 14, 1 + NC)
        mix = view(C, 14, NC)
        cconv = view(T, NQKV)
        cshift = view(T + 1536, NRW)
        lora = view(T + 3328, 512)
        g2w = view(T + 3840, 512)
        cconvT = view(I2, 12, 24)
        cshiftT = view(I2 + 288, 14, 8)
        cst = view(I2 + 400, 12, 8)
        dmix = view(I2 + 500, 14, 8)
        shift_out = view(G, NRW)
        conv_out = view(I1, NQKV)
        ld, aa, kk, cum = (view(E + i * 4 * NC, 4, NC) for i in range(4))
        t0, t1, t2 = (view(B + i * 4 * NC, 4, NC) for i in range(3))
        gate, bonus = view(H, 4, NC), view(H + 4 * NC, 4, NC)
        ar = view(G, 4, 2, NP)
        bb = view(G + 8 * NP, 4, NP)
        kb = view(W + SLOT + 3 * 2304, 4, NP)
        zs = [view(B + 3584, NX), view(B + 3584 + NX, NX), view(C + 12 * NC, NX), view(C + 12 * NC + NX, NX)]

        def gates(n):
            return view(G + 12 * NP + n * NX if n < 4 else A + (n - 4) * NX if n < 12 else G + (n - 12) * NX, NX)

        v_rw, b_rw, k_rw = view(T, 3, 512), view(T + 1536, 3, 512), view(T + 3072, 3, 512)
        qkv = view(C, 12, NC)
        sqb = view(B, 8, NC)
        rnb = view(E, 8, NC)
        gbc = view(I3, 12, 128)
        dec, edec, dst = view(A, 12, TC), view(A + 1152, 12, TC), view(A + 2304, 12, TC)
        qkh = view(I1, 8, NP)
        k_dn, v_dn = view(I2, 3, 512), view(I3, 3, 512)
        qkd = view(I4, 12, TC)
        bT = view(E, 12, TC)
        xx = view(E + 1152, 12, TC)
        yy = view(E + 2304, 12, TC)
        xT = view(B, 36, TC)
        akT, rbT, rkT = (view(W + SLOT + i * 2304, 24, TC) for i in range(3))
        S = A + 8 * NX
        s_dn_p = view(S, 512)
        s_rw_p = view(S + 1024, 4, 64)
        r_buf, u_buf, o_buf = view(S + 512, 512), view(G + 8 * NP, 512), view(G + 8 * NP + 512, 512)
        r_bufw, u_bufw = view(W + SLOT + 3 * 2304, 512), view(W + SLOT + 3 * 2304 + 512, 512)
        odn, orw = view(C, 4, NC), view(C + 4 * NC, 4, NC)
        sq_o, on_o = view(C + 8 * NC, 512), view(C + 8 * NC + 512, 512)
        yw_o, sqw_o = view(E + 3456, 512), view(E + 3968, 512)

        items = []

        def item(name, source, slot, width=512):
            use = sum(1 for i in items if i[2] == slot)
            items.append((name, source, slot, width, use))

        def wcols(w, lo, n):
            return w[0].rearrange("(k p) n -> p k n", p=128)[:, :, lo:lo + n]

        for name, lo, n, slot in (("r", ORW, 512, 0), ("kr", ORW + 512, 512, 1), ("vr", ORW + 1024, 512, 2),
                                  ("wag", ORW + 1536, 256, 0), ("q", 0, 512, 1), ("k", 512, 512, 2),
                                  ("v", 1024, 512, 0), ("z", OZ, 512, 0), ("g0", OGATE, 512, 0),
                                  ("g1", OGATE + 512, 512, 0), ("g2", OGATE + 1024, 512, 0),
                                  ("g3", OGATE + 1536, 512, 0)):
            item(name, wcols(w_in, lo, n), slot, n)
        item("updn", w_up_dn[0].rearrange("(k p) n -> p k n", p=128), 1)
        item("uprw", w_up_rw[0].rearrange("(k p) n -> p k n", p=128), 2)
        item("out0", wcols(w_out, 0, 512), 0)
        item("out1", wcols(w_out, 512, 512), 1)
        for i in range(4):
            item(f"wq{i}", wcols(peer_wq, 512 * i, 512), (i + 2) % 3)
        place = {i[0]: i for i in items}

        w_landed = [sem(f"w_landed{i}") for i in range(3)]
        x_in = sem("x_in")
        small_in = sem("small_in")
        par_in = sem("par_in")
        consts = sem("consts")
        pool_step = sem("pool_step")
        vec_step = sem("vec_step")
        act_step = sem("act_step")
        rs_ready = sem("rs_ready")
        xs_ready = sem("xs_ready")
        xT_t = sem("xT_t")
        xT_done = sem("xT_done")
        par2_ready = sem("par2_ready")
        proj_ready = sem("proj_ready")
        proj_used = sem("proj_used")
        out_dma = sem("out_dma")
        shift_sent = sem("shift_sent")
        conv_sent = sem("conv_sent")
        mix_ready = sem("mix_ready")
        kk0_ready = sem("kk0_ready")
        bonus_in = sem("bonus_in")
        bonus_done = sem("bonus_done")
        cum_ready = sem("cum_ready")
        rw_vec_ready = sem("rw_vec_ready")
        conv_done = sem("conv_done")
        qk_done = sem("qk_done")
        ln_done = sem("ln_done")
        g_ready = sem("g_ready")
        gb_in = sem("gb_in")
        dec_in = sem("dec_in")
        dec_ready = sem("dec_ready")
        kq_used = sem("kq_used")
        rwm_used = sem("rwm_used")
        inv_y = sem("inv_y")
        inv_y_used = sem("inv_y_used")
        inv_z = sem("inv_z")
        inv_z_used = sem("inv_z_used")
        inv_x = sem("inv_x")
        inv_x_used = sem("inv_x_used")
        inv_first = sem("inv_first")
        inv_c = sem("inv_c")
        rwb_ready = sem("rwb_ready")
        rwb_used = sem("rwb_used")
        dn_r = sem("dn_r")
        dn_r_done = sem("dn_r_done")
        dn_u = sem("dn_u")
        dn_u_done = sem("dn_u_done")
        dn_o = sem("dn_o")
        dn_o_used = sem("dn_o_used")
        dn_s = sem("dn_s")
        dn_s_done = sem("dn_s_done")
        dn_ss = sem("dn_ss")
        dn_root = sem("dn_root")
        dn_on = sem("dn_on")
        dn_ot = sem("dn_ot")
        dn_ot_used = sem("dn_ot_used")
        rw_r = sem("rw_r")
        rw_r_done = sem("rw_r_done")
        rw_u = sem("rw_u")
        rw_u_done = sem("rw_u_done")
        rw_y = sem("rw_y")
        rw_s = sem("rw_s")
        rw_s_done = sem("rw_s_done")
        rw_c = sem("rw_c")
        rw_sq = sem("rw_sq")
        rw_var = sem("rw_var")
        rw_root = sem("rw_root")
        rw_yn = sem("rw_yn")
        rw_yt = sem("rw_yt")
        rw_yt_used = sem("rw_yt_used")
        up_ready = sem("up_ready")
        h_ready = sem("h_ready")
        query_ready = sem("query_ready")
        state_sent = sem("state_sent")
        st_in = sem("st_in")
        strw_in = sem("strw_in")
        strw_sent = sem("strw_sent")
        st_sent = sem("st_sent")
        svp_in = sem("svp_in")
        ytok_in = sem("ytok_in")
        x_again = sem("x_again")
        rows_in = sem("rows_in")
        keys_in = sem("keys_in")
        sc_sent = sem("sc_sent")
        y_sent = sem("y_sent")
        pst_t = sem("pst_t")
        svt_t = sem("svt_t")
        gbs_ready = sem("gbs_ready")
        gbs_sum = sem("gbs_sum")
        yv_ready = sem("yv_ready")
        syt_ready = sem("syt_ready")
        syt_t = sem("syt_t")
        kqp_ready = sem("kqp_ready")
        sdn_mv = sem("sdn_mv")
        delta_ready = sem("delta_ready")
        osq_sum = sem("osq_sum")
        tokd_t = sem("tokd_t")
        spread_ready = sem("spread_ready")
        outer = sem("outer")
        outer_used = sem("outer_used")
        ssq_ready = sem("ssq_ready")
        branches_ready = sem("branches_ready")
        up_used = sem("up_used")
        merged = sem("merged")
        h_used = sem("h_used")
        hsq = sem("hsq")
        hroot = sem("hroot")
        xn2_ready = sem("xn2_ready")
        xn2_t = sem("xn2_t")
        keys_t = sem("keys_t")
        score = sem("score")
        score_used = sem("score_used")
        u_free = sem("u_free")
        v_free = sem("v_free")
        idx_ready = sem("idx_ready")
        topk_step = sem("topk_step")
        cv_ready = sem("cv_ready")
        gexp_ready = sem("gexp_ready")
        gelu_step = sem("gelu_step")
        gelu_in = sem("gelu_in")
        tanh_ready = sem("tanh_ready")
        w_ready = sem("w_ready")
        held_steps = sem("held_steps")
        diag_ready = sem("diag_ready")
        peer_done = sem("peer_done")
        fsq = sem("fsq")
        froot = sem("froot")
        y_ready = sem("y_ready")
        u_in = [sem(f"u_in{i}") for i in range(8)]
        v_in = [sem(f"v_in{i}") for i in range(8)]
        (par_ready, cache_ready, ba_used, mix_part, shift_ready, wag_act, lora_used, kksq_ready, norm_used,
            exp_ready, conv_ready, vtok_ready, tap_ready, silu_done, qk_sq, qk_root, gexp_done, dec_exp,
            tok_ready, prw_ready) = series(sem("act_signals"), 1, 2, 1, 14, 4, 2, 12, 1, 4, 4, 3, 3, 12, 3, 1,
            8, 1, 6, 6, 6)
        (svt_ready, sroot, pst_ready, syt_used, egb_ready, oroot, tokd_ready, keys_ready, xn2T_ready, score_free,
            query_used) = series(sem("act_signals2"), 6, 1, 1, 1, 1, 1, 1, 4, 6, 1, 16)
        (par_t, cache_t, ba_ready, shift_t, lora_ready, norm_ready, bonus_sum, conv_t, vtok_t, qk_sum,
            gsum_ready, gb_ready, kq_ready, tok_t, prw_t, rwm_ready) = series(sem("pe_signals"), 1, 1, 1, 4, 12,
            4, 4, 3, 3, 8, 1, 3, 6, 6, 6, 12)
        ct = view(E + 3456, 12, TC)

        svt = view(E, RH, 6, RN)
        prwo = view(T + 3072, 8, 64)
        strw, prod = view(E, 32, 64), view(E + 2048, 16, 64)
        svp = view(E + 3072, 6, 64)
        vhalf, sa, yv = (view(S + 1280 + 32 * i, 32) for i in range(3))
        ytok = view(I3, 512)
        st = view(E, 32, 128)
        gbs = view(I1, 8, 128)
        stok = view(G + 4 * NX, 2, 512)
        spread = view(I1, 8, 128)
        mm_ = view(B, KT, NX)
        htok = view(T, 3, D)
        xn2 = view(C + 512, 3, D)
        xn2T = view(H, KT, NX)
        scratch = view(G, D)
        qT = view(G, 2, 4, NX)
        keysT = view(XN, 16, 128)
        ssc = view(I1, 2048)
        ln2row, lnfrow, xsrep = view(I2, D), view(I2 + D, D), view(I2 + 2 * D, D)
        zero512 = view(I4, 512)
        sc_all = view(E, 17, 256)
        uring = [view(A + j * D, D) for j in range(8)]
        vring = [view(W + j * D, D) for j in range(8)]
        squares = view(G, D)
        diag = view(G + 8 * NX, 8, 128)
        onehot = view(G + 8 * NX + D, PT, NCAND)
        ORDER = (0, 2, 1)
        small = [T + 3072]

        def tiny(*shape):
            n = 1
            for s in shape:
                n *= s
            small[0] += n
            assert small[0] <= T + 4608
            return view(small[0] - n, *shape)

        cur, curm = tiny(2, 128), tiny(2, 128)
        best = tiny(2, PT)
        keyf = tiny(2, PT)
        cand, candm, cidx = tiny(NCAND), tiny(NCAND), tiny(NCAND)
        cv, posf, eidf, ncv0 = tiny(PT), tiny(PT), tiny(PT), tiny(1)
        iota = tiny(NCAND)
        gexp, gsum, hdot, wgt = tiny(2, PT), tiny(2, 1), tiny(2, PT), tiny(2, PT)
        g1, g2 = tiny(PT), tiny(PT)
        selh, sel = tiny(8, 8), tiny(8)
        key_i = ctx.enter_context(nc.sbuf_tensor("key_i", [128, 2 * PT], U32))
        pos_i = ctx.enter_context(nc.sbuf_tensor("pos_i", [128, PT], U32))
        idx = ctx.enter_context(nc.sbuf_tensor("idx", [128, 2 * PT], U32))


        def emit_sample_rwkv_in(sp):
            sp.wait_ge(svt_ready.sem, svt_ready.at(6))
            for b in range(NS):
                for half in range(2):
                    p = 64 * half + 8 * b
                    sp.dma_start(svp[p:p + 8].rearrange("p x n -> p (x n)"),
                                 svt[b:b + 1].rearrange("p h x n -> p h (x n)")).then_inc(svp_in, 16)
            sp.wait_ge(svp_in, 16 * 16)
            for half in range(2):
                sp.dma_start(strw[64 * half:64 * half + 64],
                             state_rw[0].rearrange("b h v k -> (b h) v k")[:, 32 * half:32 * half + 32, :]
                             ).then_inc(strw_in, 16)

        def emit_sample_rwkv_out(sp):
            sp.wait_ge(yv_ready, 1)
            sp.wait_ge(dn_r_done, 1)
            for b in range(NS):
                for half in range(2):
                    p = 64 * half + 8 * b
                    sp.dma_start(ytok[b:b + 1].rearrange("p (h n) -> p h n", n=RN)[:, :, 32 * half:32 * half + 32],
                                 yv[p:p + 8]).then_inc(ytok_in, 16)
            for half in range(2):
                sp.dma_start(s_rw[0].rearrange("b h v k -> (b h) v k")[:, 32 * half:32 * half + 32, :],
                             strw[64 * half:64 * half + 64]).then_inc(strw_sent, 16)

        def emit_states_in(sp, heads):
            for h in heads:
                sp.dma_start(st[:, 8 * h:8 * h + 8, :], state_dn[0, :, h].rearrange("b k v -> k b v")).then_inc(st_in, 16)

        def emit_state_outputs(sp):
            sp.wait_ge(dn_s_done, NCH)
            sp.dma_start(p_dn[0, 0].rearrange("h k v -> k h v"),
                         s_dn_p.rearrange("p (h v) -> p h v", h=4)).then_inc(state_sent, 16)
            sp.wait_ge(pst_ready.sem, pst_ready.at(1))
            sp.dma_start(p_rw[0, 0].rearrange("h v k -> v h k"), prwo[0:64]).then_inc(state_sent, 16)

        def emit_x_again(sp):
            for i in range(2):
                sp.dma_start(htok[:, i, :], x_prompt[0, 128 * i:128 * i + 128]).then_inc(x_again, 16)
            sp.dma_start(htok[0:NS, 2, :], x_sample[:, 0]).then_inc(x_again, 16)

        def emit_sample_states(sp):
            for h in range(DH):
                sp.wait_ge(outer_used, 2 * h + 2)
                sp.dma_start(s_dn[0, :, h].rearrange("b k v -> k b v"), st[:, 8 * h:8 * h + 8, :]).then_inc(st_sent, 16)

        def emit_norm_rows(sp):
            sp.wait_ge(branches_ready, 1)
            sp.dma_start(ln2row, ln2.broadcast_to([128, D])).then_inc(rows_in, 16)
            sp.dma_start(lnfrow, ln_f.rearrange("(a d) -> a d", a=1).broadcast_to([128, D])).then_inc(rows_in, 16)

        def emit_peer_io(sp):
            sp.wait_ge(xn2_ready, 3)
            for h in range(PH):
                sp.dma_start(xsrep[NS * h:NS * h + NS], xn2[0:NS, 2, :]).then_inc(sc_sent, 16)
            sp.wait_ge(score_used, 12)
            sp.wait_ge(score_free.sem, score_free.at(1))
            for h in range(PH):
                sp.dma_start(sc_all[NS * h:NS * h + NS, 8, :], ssc[0:NS, 256 * h:256 * h + 256]).then_inc(sc_sent, 16)
            for n, i in enumerate(ORDER):
                sp.wait_ge(y_ready, n + 1)
                sp.dma_start(y_prompt[0, 128 * i:128 * i + 128] if i < 2 else y_sample[:, 0],
                             xn2[0:128 if i < 2 else NS, i, :]).then_inc(y_sent, 16)
            sp.wait_ge(y_sent, 48)
            for s, n in ((out_dma, 16), (shift_sent, 32), (conv_sent, 32), (state_sent, 32), (strw_sent, 32), (st_sent, 64)):
                sp.wait_ge(s, n)

        def held(eng, s, value):
            eng.wait_ge(s, value)
            eng.sem_inc(held_steps, 1)

        def gather(pool, ring, landed, table, p, j, n):
            pool.indirect_dma_start(ring[j % 8][0:n], None, table[0],
                                    bass.IndirectOffsetOnAxis(ap=idx[0:n, PT * p + j:PT * p + j + 1], axis=0)
                                    ).then_inc(landed[j % 8], 16)

        def pool_unit(pool, u, p, n=128):
            pool.wait_ge(idx_ready, u + 1)
            pool.sem_inc(held_steps, 1)
            for ring, landed, table, free in ((uring, u_in, peer_u, u_free), (vring, v_in, peer_v, v_free)):
                for j in range(PT):
                    held(pool, free, 16 * u + (j + 1))
                    gather(pool, ring, landed, table, p, j, n)

        def sample_rwkv(pool, step):
            g = nc.gpsimd
            pool.wait_ge(svp_in, 16 * 16)
            pool.wait_ge(strw_in, 32)

            def over_v(x):
                return svp[:, x, :].unsqueeze(1).broadcast_to([128, 16, 64])

            def over_k(x):
                return row(x, 128, 16, 64)

            def summed(out):
                n = 32
                while n > 1:
                    step(g.tensor_tensor(prod[:, :, 0:n], prod[:, :, 0:n], prod[:, :, n:2 * n], ALU.add))
                    step.sync()
                    n //= 2
                return g.tensor_tensor(out, prod[:, :, 0], prod[:, :, 1], ALU.add)

            step(g.tensor_copy(vhalf[0:64], svp[0:64, 3, 0:32]))
            step.sync()
            step(g.tensor_copy(vhalf[64:128], svp[64:128, 3, 32:64]))
            step.sync()
            for half in range(2):
                vs = slice(16 * half, 16 * half + 16)
                s_ = strw[:, vs, :]
                step(g.tensor_tensor(prod, s_, over_v(4), ALU.mult))
                step.sync()
                step(g.tensor_tensor(s_, s_, over_v(1), ALU.mult))
                step(summed(sa[:, vs]))
                step.sync()
                step(g.tensor_tensor(prod, over_v(5), over_k(sa[:, vs]), ALU.mult))
                step.sync()
                step(g.tensor_tensor(s_, s_, prod, ALU.subtract))
                step.sync()
                step(g.tensor_tensor(prod, over_v(2), over_k(vhalf[:, vs]), ALU.mult))
                step.sync()
                step(g.tensor_tensor(s_, s_, prod, ALU.add))
                step.sync()
                step(g.tensor_tensor(prod, s_, over_v(0), ALU.mult))
                step.sync()
                ins = summed(yv[:, vs])
                if half == 0:
                    step(ins)
                    step.sync()
            ins.then_inc(yv_ready, 1)

        def pool_peer(pool, step):
            pool.wait_ge(h_used, 6)
            step(nc.gpsimd.iota(iota, [[1, NCAND]], base=0, channel_multiplier=0, allow_small_or_imprecise_dtypes=True))
            step(nc.gpsimd.memset(selh, 0.0))
            step(nc.gpsimd.memset(zero512, 0.0))
            step.sync()
            nc.gpsimd.affine_select(out=selh, in_=selh, pattern=[[-8, 8], [-1, 8]], compare_op=ALU.not_equal, fill=1.0,
                                    base=0, channel_multiplier=1).then_inc(consts, 1)
            with pool.Fori(0, 4) as i:
                for p in range(2):
                    pool_unit(pool, i * 2 + p, p)
            pool_unit(pool, 8, 0, NS * PH)
            with pool.Fori(0, 4) as i:
                for p in range(2):
                    pool_unit(pool, i * 2 + (9 + p), 1 - p)

        def pe_rest(pe, mm, project):
            pe.wait_ge(rw_s_done, NCH)
            pe.wait_ge(dn_s_done, NCH)
            pe.wait_ge(rw_yt_used, NCH)
            pe.wait_ge(dn_ot_used, NCH)
            for f in range(4):
                ins = nc.tensor.transpose(psv(7, 64, 128, at=128 * f), s_rw_p[:, f, :], ident)
            ins.then_inc(pst_t, 1)
            pe.wait_ge(syt_ready, 1)
            for f in range(4):
                ins = nc.tensor.transpose(psv(4, 128, NS, at=NS * f), ytok[0:NS, 128 * f:128 * f + 128],
                                          ident[0:NS, 0:NS])
            ins.then_inc(syt_t, 1)
            pe.wait_ge(gbs_ready, 1)
            for i in range(8):
                ins = mm(psv(6, 128, NS, at=NS * i), gbs[0:NS, i, :], ident[0:NS, 0:NS])
            ins.then_inc(gbs_sum, 1)
            project("g3", T0, part=(0, 2))
            pe.wait_ge(kqp_ready, 1)
            pe.wait_ge(pst_ready.sem, pst_ready.at(1))
            mm(psv(7, 128, 32), ones, sdv[:, 2, :])
            for h in range(DH):
                pe.wait_ge(st_in, 64)
                for b in range(NS):
                    ins = mm(psv(5, 128, 2, at=2 * (8 * h + b)), st[:, 8 * h + b, :], sd[:, h:h + 5:4, b])
            ins.then_inc(sdn_mv, 1)
            project("g3", T0, part=(2, 4))
            pe.wait_ge(delta_ready, 1)
            mm(psv(6, 128, 32), ones, sdv[:, 5, :]).then_inc(osq_sum, 1)
            for h in range(DH):
                nc.tensor.transpose(psv(4, NS, 128, at=128 * h), sdv[:, 3, 8 * h:8 * h + 8], ident)
            for h in range(DH):
                ins = nc.tensor.transpose(psv(5, NS, 128, at=128 * h), sd[:, 4 + h, :], ident)
            ins.then_inc(tokd_t, 1)
            pe.wait_ge(oroot.sem, oroot.at(1))

            def outer_product(n):
                h, half = n // 2, n % 2
                pe.wait_ge(spread_ready, h + 1)
                if n >= 2:
                    pe.wait_ge(outer_used, n - 1)
                mm(psv(6 + n % 2, 128, 4, 128), stok[0:NS, 1, 128 * h:128 * h + 128],
                   spread[0:NS, 4 * half:4 * half + 4, :]).then_inc(outer, 1)

            pe.wait_ge(proj_used, 46)
            pe.wait_ge(branches_ready, 1)
            for n in range(16):
                name, src = (("updn", odn), ("uprw", orw))[n // 8]
                if n % 8 == 0:
                    slot = wait_w(pe, name)
                    w = wslot[slot].rearrange("p k n -> p (k n)").rearrange("p (k n) -> p k n", k=4)
                if n >= 4:
                    pe.wait_ge(up_used, n - 3)
                f = n % 8
                for k in range(4):
                    ins = mm(psv(n % 4, 128, NX), w[:, k, f * 128:f * 128 + 128], src[:, k, T0:NC], start=k == 0, stop=k == 3)
                ins.then_inc(up_ready, 1)
            pe.wait_ge(keys_in, 16)
            pe.wait_ge(tokd_ready.sem, tokd_ready.at(1))
            for n in range(4):
                for q in range(4):
                    ins = nc.tensor.transpose(psv(4 + n, 128, 128, at=128 * q), keysT[:, 4 * n + q, :], ident)
                ins.then_inc(keys_t, 1)
            pe.wait_ge(up_used, 16)
            pe.wait_ge(merged, 8)
            pe.wait_ge(keys_ready.sem, keys_ready.at(4))
            for n in range(6):
                half, i = n // 3, n % 3
                if i == 0:
                    slot = wait_w(pe, f"out{half}")
                rows, cols = (128, slice(128 * i, 128 * i + 128)) if i < 2 else (NS, slice(SEQ, SEQ + NS))
                for k in range(KT):
                    ins = mm(psv(n, rows, 512), mm_[:, k, cols], wslot[slot][:, k, :], start=k == 0, stop=k == KT - 1)
                ins.then_inc(h_ready, 1)
                if n < 4:
                    outer_product(2 * n)
                    outer_product(2 * n + 1)
            pe.wait_ge(h_used, 6)
            for i, n in enumerate((128, 128, NS)):
                pe.wait_ge(xn2_ready, i + 1)
                for half in range(2):
                    for q in range(4):
                        k = 4 * half + q
                        ins = nc.tensor.transpose(psv(2 * i + half, 128, 4, 128)[:, q, 0:n],
                                                  xn2[0:n, i, k * 128:(k + 1) * 128], ident[0:n, 0:n])
                    ins.then_inc(xn2_t, 1)
            pe.wait_ge(xn2T_ready.sem, xn2T_ready.at(6))
            for hp in range(4):
                slot = wait_w(pe, f"wq{hp}")
                for q in range(4):
                    n = 4 * hp + q
                    if n >= 4:
                        pe.wait_ge(query_used.sem, query_used.at(n - 3))
                    for k in range(KT):
                        ins = mm(psv(q, 128, NX), wslot[slot][:, k, 128 * q:128 * q + 128], xn2T[:, k, :],
                                 start=k == 0, stop=k == KT - 1)
                    ins.then_inc(query_ready, 1)
                if hp == 2:
                    pe.wait_ge(query_ready, 12)
                    pe.sem_inc(v_free, 8)
                pe.wait_ge(query_used.sem, query_used.at(4 * hp + 4))
                for i in range(3):
                    n = 3 * hp + i
                    if n >= 4:
                        pe.wait_ge(score_used, n - 3)
                    rows, cols = (128, slice(128 * i, 128 * i + 128)) if i < 2 else (NS, slice(SEQ, SEQ + NS))
                    for q in range(4):
                        ins = mm(psv(4 + n % 4, rows, 128, at=128 * q), qT[:, hp % 2, q, cols], keysT[:, 4 * hp + q, :])
                    ins.then_inc(score, 1)
            pe.wait_ge(score_used, 12)
            pe.wait_ge(consts, 2)

            def weigh(t, lhsT, rows, out_rows, j, start=False, stop=False):
                for half in range(2):
                    ins = mm(psv(2 * t + half, out_rows, 512), lhsT, vring[j % 8][0:rows, 512 * half:512 * half + 512],
                             start=start, stop=stop)
                return ins

            def weigh_tile(t, first):
                for half in range(2):
                    mm(psv(2 * t + half, 128, 512), ident, zero512, stop=False)
                with pe.Fori(0, 4) as i:
                    for p in range(2):
                        u = i * 2 + (first + p)
                        for j in range(PT):
                            pe.wait_ge(v_in[j % 8], 32 * u + 16 * (j // 8 + 1))
                            pe.wait_ge(diag_ready, 16 * u + (j + 1))
                            weigh(t, diag[:, j % 8, :], 128, 128, j).then_inc(v_free, 1)
                for half in range(2):
                    ins = mm(psv(2 * t + half, 128, 512), ident, zero512, start=False)
                ins.then_inc(peer_done, 1)

            weigh_tile(0, 0)
            for j in range(PT):
                pe.wait_ge(v_in[j % 8], 32 * 8 + 16 * (j // 8 + 1))
                pe.wait_ge(diag_ready, 16 * 8 + j + 1)
                ins = weigh(2, diag[0:NS * PH, j % 8, 0:NS], NS * PH, NS, j, start=j == 0, stop=j == PT - 1)
                ins.then_inc(v_free, 1)
            pe.wait_ge(v_free, 16 * 9 + 8)
            pe.sem_inc(peer_done, 1)
            weigh_tile(1, 9)

        def act_rest(act, step, fn, evacuate):
            act.wait_ge(pst_t, 1)
            fn(prwo[0:64].rearrange("p h k -> p (h k)"), psv(7, 64, 512)).then_inc(pst_ready.sem, 1)
            act.wait_ge(syt_t, 1)
            fn(orw[:, :, NP:NC], psv(4, 128, 4, NS)).then_inc(syt_used.sem, 1)
            act.wait_ge(gbs_sum, 1)
            step(fn(sdv[:, 1, :], psv(6, 128, 32, at=32)))
            fn(sdv[:, 0, :], psv(6, 128, 32), ACT.Exp).then_inc(egb_ready.sem, 1)
            evacuate([gates(12 + f) for f in range(4)], ACT.Sigmoid, NX)
            act.wait_ge(osq_sum, 1)
            fn(sdv[:, 6, :], psv(6, 128, 32), ACT.Sqrt, scale=1.0 / DK, bias=eps[:, 0:1]).then_inc(oroot.sem, 1)
            act.wait_ge(tokd_t, 1)
            step(fn(stok[0:NS, 0, :], psv(4, NS, 512)))
            fn(stok[0:NS, 1, :], psv(5, NS, 512)).then_inc(tokd_ready.sem, 1)
            for n in range(4):
                act.wait_ge(keys_t, 4)
                fn(keysT[:, 4 * n:4 * n + 4, :], psv(4 + n, 128, 4, 128)).then_inc(keys_ready.sem, 1)
            for i, n in enumerate((128, 128, NS)):
                act.wait_ge(h_used, 6)
                fn(scratch[0:n], htok[0:n, i, :], ACT.Square, accum_out=ss[0:n, i:i + 1]).then_inc(hsq, 1)
                act.wait_ge(hsq, i + 1)
                fn(rs[0:n, i:i + 1], ss[0:n, i:i + 1], ACT.Sqrt, scale=1.0 / D, bias=eps[0:n, 0:1]).then_inc(hroot, 1)
            for i, n in enumerate((128, 128, NS)):
                for half in range(2):
                    act.wait_ge(xn2_t, 2 * i + half + 1)
                    fn(xn2T[:, 4 * half:4 * half + 4, 128 * i:128 * i + n],
                       psv(2 * i + half, 128, 4, 128)[:, :, 0:n]).then_inc(xn2T_ready.sem, 1)
            act.wait_ge(consts, 2)
            act.wait_ge(st_sent, 64)
            act.wait_ge(state_sent, 32)
            fn(sc_all[:, 8, :], zero512[:, 0:256]).then_inc(score_free.sem, 1)

            def softmax_exp(u, p):
                act.wait_ge(cv_ready, u + 1)
                fn(gexp[:, p, :], cv, ACT.Exp, bias=ncv0, accum_out=gsum[:, p, :]).then_inc(gexp_ready, 1)

            for hp in range(4):
                if hp == 2:
                    softmax_exp(0, 0)
                for q in range(4):
                    n = 4 * hp + q
                    if hp >= 2:
                        act.wait_ge(score, 3 * hp - 3)
                    act.wait_ge(query_ready, n + 1)
                    fn(qT[:, hp % 2, q, :], psv(q, 128, NX)).then_inc(query_used.sem, 1)
                for i in range(3):
                    n = 3 * hp + i
                    act.wait_ge(score, n + 1)
                    if i < 2:
                        dst = sc_all[:, 9 * i + 2 * hp:9 * i + 2 * hp + 2, :].rearrange("p u n -> p (u n)")
                    else:
                        dst = ssc[0:NS, 512 * hp:512 * hp + 512]
                    fn(dst, psv(4 + n % 4, 128 if i < 2 else NS, 512)).then_inc(score_used, 1)

            def act_unit(u, p, n=128, last=False):
                act.wait_ge(gelu_in, u + 1)
                fn(g2[0:n], g1[0:n], ACT.Tanh, scale=GELU_C).then_inc(tanh_ready, 1)
                act.wait_ge(w_ready, u + 1)
                for j in range(PT):
                    act.wait_ge(v_free, 16 * u + (j + 1))
                    out, src = (diag[:, j % 8, :], ident) if n == 128 else (diag[0:n, j % 8, 0:NS], sel[0:n])
                    fn(out, src, scale=wgt[0:n, p, j:j + 1]).then_inc(diag_ready, 1)
                if not last:
                    softmax_exp(u + 1, 1 - p)

            with act.Fori(0, 4) as i:
                for p in range(2):
                    act_unit(i * 2 + p, p)

            def final_root(order):
                i = ORDER[order]
                n = 128 if i < 2 else NS
                act.wait_ge(fsq, order + 1)
                step(fn(squares[0:n], htok[0:n, i, :], ACT.Square, accum_out=ss[0:n, i:i + 1]))
                step.sync()
                fn(rs[0:n, i:i + 1], ss[0:n, i:i + 1], ACT.Sqrt, scale=1.0 / D, bias=eps[0:n, 0:1]).then_inc(froot, 1)

            act_unit(8, 0, NS * PH)
            final_root(0)
            with act.Fori(0, 3) as i:
                for p in range(2):
                    act_unit(i * 2 + (9 + p), 1 - p)
            act_unit(15, 1)
            act_unit(16, 0, last=True)
            final_root(1)
            final_root(2)

        def vec_rest(dve, step, v, tt, ts, stt, pc):
            dve.wait_ge(dn_o, NCH)
            step(v.tensor_copy(gbs[0:NS, 0:4, :], row(gt[0:NS, 3, :], NS, 4, 128)))
            v.tensor_copy(gbs[0:NS, 4:8, :], row(bt[0:NS, 3, :], NS, 4, 128)).then_inc(gbs_ready, 1)
            s32 = [sdv[:, i, :] for i in range(8)]
            s48 = [sdv[:, i, :].rearrange("p (h b) -> p h b", h=4) for i in range(8)]
            tt(s48[2], sd[:, 0:4, :], sd[:, 4:8, :], ALU.mult).then_inc(kqp_ready, 1)
            dve.wait_ge(sdn_mv, 1)
            dve.wait_ge(egb_ready.sem, egb_ready.at(1))
            p2 = psv(5, 128, 32, 2)
            step(tt(s32[3], p2[:, :, 1], s32[0], ALU.mult))
            step(tt(s32[4], p2[:, :, 0], s32[0], ALU.mult))
            step.sync()
            step(tt(s48[3], sd[:, 8:12, :], s48[3], ALU.subtract))
            step.sync()
            step(tt(s32[3], s32[3], s32[1], ALU.mult))
            step.sync()
            step(tt(s32[7], s32[3], psv(7, 128, 32), ALU.mult))
            step.sync()
            step(tt(s32[4], s32[4], s32[7], ALU.add))
            step.sync()
            tt(s32[5], s32[4], s32[4], ALU.mult).then_inc(delta_ready, 1)
            dve.wait_ge(oroot.sem, oroot.at(1))
            step(v.reciprocal(s32[6], s32[6]))
            step.sync()
            step(tt(odn[:, :, NP:NC], s48[4], s48[6], ALU.mult))
            dve.wait_ge(proj_used, 30)
            step.sync()
            for h in range(DH):
                step(stt(odn[:, h, T0:NC], odn[:, h, T0:NC], pc("dn_norm"), zs[h], ALU.mult, ALU.mult))
            dve.wait_ge(syt_used.sem, syt_used.at(1))
            for f in range(4):
                step(ts(orw[:, f, T0:NC], orw[:, f, T0:NC], pc("gn_w", f), pc("gn_b", f), ALU.mult, ALU.add))
            step.sync()
            step(tt(orw[:, :, T0:NC], orw[:, :, T0:NC], bonus[:, :, T0:NC], ALU.add))
            step.sync()
            tt(orw[:, :, T0:NC], orw[:, :, T0:NC], gate[:, :, T0:NC], ALU.mult).then_inc(branches_ready, 1)
            dve.wait_ge(tokd_ready.sem, tokd_ready.at(1))

            def new_states(n):
                h, half = n // 2, n % 2
                if half == 0:
                    if h > 0:
                        dve.wait_ge(outer, n)
                    tt(spread[0:NS], stok[0:NS, 0, 128 * h:128 * h + 128].unsqueeze(1).broadcast_to([NS, NS, 128]),
                       row(ident[0:NS, 0:NS], NS, NS, 128), ALU.mult).then_inc(spread_ready, 1)
                dve.wait_ge(outer, n + 1)
                for b in range(4):
                    m = 8 * h + 4 * half + b
                    ins = stt(st[:, m, :], st[:, m, :], s32[0][:, m:m + 1], psv(6 + n % 2, 128, 128, at=128 * b),
                              ALU.mult, ALU.add)
                    if b < 3:
                        step(ins)
                ins.then_inc(outer_used, 1)

            dve.wait_ge(proj_used, 46)
            for n in range(16):
                dve.wait_ge(up_ready, n + 1)
                f, p = n % 8, psv(n % 4, 128, NX)
                if n < 8:
                    tt(mm_[:, f, :], p, gates(f), ALU.mult).then_inc(up_used, 1)
                else:
                    tt(gates(n), p, gates(n), ALU.mult).then_inc(up_used, 1)
                    dve.wait_ge(up_used, n + 1)
                    tt(mm_[:, f, :], mm_[:, f, :], gates(n), ALU.add).then_inc(merged, 1)
            dve.wait_ge(x_again, 48)
            for n in range(6):
                half, i = n // 3, n % 3
                rows = 128 if i < 2 else NS
                if n < 4:
                    new_states(2 * n)
                    new_states(2 * n + 1)
                dve.wait_ge(h_ready, n + 1)
                h_ = htok[0:rows, i, 512 * half:512 * half + 512]
                tt(h_, h_, psv(n, rows, 512), ALU.add).then_inc(h_used, 1)
            dve.wait_ge(rows_in, 32)
            for i, n in enumerate((128, 128, NS)):
                dve.wait_ge(hroot, i + 1)
                step(v.reciprocal(rs[0:n, i:i + 1], rs[0:n, i:i + 1]))
                step.sync()
                stt(xn2[0:n, i, :], htok[0:n, i, :], rs[0:n, i:i + 1], ln2row[0:n], ALU.mult, ALU.mult).then_inc(xn2_ready, 1)
            dve.wait_ge(consts, 2)
            step(v.tensor_reduce(sel, selh.rearrange("p h b -> p b h"), AX, ALU.add))
            dve.wait_ge(strw_sent, 32)
            dve.sem_inc(u_free, 8)
            dve.wait_ge(score_used, 1)
            NTOP = 32

            def topk(u, p, src, early=0):
                k = Steps(dve, topk_step, u * NTOP)

                def sync():
                    held(dve, topk_step, k.base + k.n)

                if early == 1:
                    dve.wait_ge(gexp_ready, 1)
                if not early:
                    dve.wait_ge(score_used, 12)
                    dve.wait_ge(sc_sent, 16 * 16)
                    dve.wait_ge(v_free, 16 * u - 8)
                    dve.wait_ge(gexp_ready, u)
                k(v.tensor_copy(cur, src))
                sync()
                for x in range(2):
                    k(v.max(best[:, x, 0:8], cur[:, x, :]))
                sync()
                for x in range(2):
                    k(v.match_replace(curm[:, x, :], best[:, x, 0:8], cur[:, x, :], NEG))
                    k(v.max_index(key_i[:, PT * x:PT * x + 8], best[:, x, 0:8], cur[:, x, :]))
                sync()
                for x in range(2):
                    k(v.max(best[:, x, 8:16], curm[:, x, :]))
                sync()
                for x in range(2):
                    k(v.max_index(key_i[:, PT * x + 8:PT * x + 16], best[:, x, 8:16], curm[:, x, :]))
                at_ = 0
                for a, na, nb in PAIRS:
                    o = cand[:, at_:at_ + na * nb].rearrange("p (a b) -> p a b", a=na)
                    k(tt(o, row(best[:, 0, a:a + na], 128, na, nb),
                         best[:, 1, 0:nb].unsqueeze(1).broadcast_to([128, na, nb]), ALU.add))
                    at_ += na * nb
                sync()
                k(v.max(cv[:, 0:8], cand))
                k(ts(keyf[:, 0, :], key_i[:, 0:PT], float(PK), None, ALU.mult))
                k(ts(keyf[:, 1, :], key_i[:, PT:2 * PT], 1.0, None, ALU.mult))
                sync()
                k(v.match_replace(candm, cv[:, 0:8], cand, NEG))
                k(v.max_index(pos_i[:, 0:8], cv[:, 0:8], cand))
                at_ = 0
                for a, na, nb in PAIRS:
                    o = cidx[:, at_:at_ + na * nb].rearrange("p (a b) -> p a b", a=na)
                    k(tt(o, row(keyf[:, 0, a:a + na], 128, na, nb),
                         keyf[:, 1, 0:nb].unsqueeze(1).broadcast_to([128, na, nb]), ALU.add))
                    at_ += na * nb
                sync()
                k(v.max(cv[:, 8:16], candm))
                sync()
                k(v.max_index(pos_i[:, 8:16], cv[:, 8:16], candm))
                ts(ncv0, cv[:, 0:1], -1.0, None, ALU.mult).then_inc(cv_ready, 1)
                k.sync()
                k(v.tensor_copy(posf, pos_i[:, :]))
                k.sync()
                k(tt(onehot, iota.unsqueeze(1).broadcast_to([128, PT, NCAND]), row(posf, 128, PT, NCAND), ALU.is_equal))
                k.sync()
                k(tt(onehot, onehot, cidx.unsqueeze(1).broadcast_to([128, PT, NCAND]), ALU.mult))
                k.sync()
                k(v.tensor_reduce(eidf, onehot, AX, ALU.add))
                assert k.n == NTOP, k.n
                k.sync()
                v.tensor_copy(idx[:, PT * p:PT * p + PT], eidf).then_inc(idx_ready, 1)

            NGELU = 5

            def dots(u, p, x, n=128):
                for j in range(PT):
                    dve.wait_ge(u_in[j % 8], 32 * u + 16 * (j // 8 + 1))
                    v.tensor_tensor_reduce(uring[j % 8][0:n], uring[j % 8][0:n], x, 1.0, 0.0, ALU.mult, ALU.add,
                                           hdot[0:n, p, j:j + 1]).then_inc(u_free, 1)

            def weights(u, p, n=128):
                h = hdot[0:n, p, :]
                a, b = g1[0:n], g2[0:n]
                k = Steps(dve, gelu_step, u * NGELU)
                dve.wait_ge(u_free, 16 * u + (PT + 8))
                k(tt(a, h, h, ALU.mult))
                k.sync()
                k(ts(a, a, 0.044715, 1.0, ALU.mult, ALU.add))
                k.sync()
                tt(a, a, h, ALU.mult).then_inc(gelu_in, 1)
                dve.wait_ge(gexp_ready, u + 1)
                k(v.reciprocal(gsum[0:n, p, :], gsum[0:n, p, :]))
                dve.wait_ge(tanh_ready, u + 1)
                k(stt(b, b, 1.0, h, ALU.add, ALU.mult))
                k.sync()
                k(tt(b, b, gexp[0:n, p, :], ALU.mult))
                k.sync()
                ts(wgt[0:n, p, :], b, gsum[0:n, p, :], 0.5, ALU.mult, ALU.mult).then_inc(w_ready, 1)
                assert k.n == NGELU

            def experts(u, p, x, n=128):
                dots(u, p, x, n)
                weights(u, p, n)

            topk(0, 0, sc_all[:, 0, :].rearrange("p (x n) -> p x n", x=2), early=2)
            flat = sc_all.rearrange("p u n -> p (u n)")

            def unit(i, first, q, t):
                u, p = i * 2 + (first + q), (first + q) % 2
                experts(u, p, xn2[:, t, :])
                topk(u + 1, 1 - p, flat[:, bass.ds(i * 512 + (first + q + 1) * 256, 256)].rearrange("p (x n) -> p x n", x=2))

            def final(order):
                i = ORDER[order]
                n = 128 if i < 2 else NS
                dve.wait_ge(peer_done, order + 1)
                for half in range(2):
                    h_ = htok[0:n, i, 512 * half:512 * half + 512]
                    ins = tt(h_, h_, psv(2 * i + half, n, 512), ALU.add)
                    if half == 0:
                        step(ins)
                ins.then_inc(fsq, 1)
                dve.wait_ge(froot, order + 1)
                step(v.reciprocal(rs[0:n, i:i + 1], rs[0:n, i:i + 1]))
                step.sync()
                stt(xn2[0:n, i, :], htok[0:n, i, :], rs[0:n, i:i + 1], lnfrow[0:n], ALU.mult, ALU.mult).then_inc(y_ready, 1)

            dots(0, 0, xn2[:, 0, :])
            topk(1, 1, sc_all[:, 1, :].rearrange("p (x n) -> p x n", x=2), early=1)
            weights(0, 0)
            experts(1, 1, xn2[:, 0, :])
            topk(2, 0, sc_all[:, 2, :].rearrange("p (x n) -> p x n", x=2))
            with dve.Fori(0, 3) as i:
                for q in range(2):
                    unit(i, 2, q, 0)
            experts(8, 0, xsrep[0:NS * PH], NS * PH)
            topk(9, 1, sc_all[:, 9, :].rearrange("p (x n) -> p x n", x=2))
            final(0)
            with dve.Fori(0, 3) as i:
                for q in range(2):
                    unit(i, 9, q, 1)
            experts(15, 1, xn2[:, 1, :])
            topk(16, 0, sc_all[:, 16, :].rearrange("p (x n) -> p x n", x=2))
            experts(16, 0, xn2[:, 1, :])
            final(1)
            final(2)

        TILE_ROWS = [128, 128, NS + META]

        def ccols(c):
            return slice(c * TC, (c + 1) * TC)

        def wait_w(eng, name):
            _, _, slot, _, use = place[name]
            eng.wait_ge(w_landed[slot], 16 * (use + 1))
            return slot

        freed, tiles = {}, 0
        for name, _, _, width, _ in items:
            if name == "updn":
                break
            tiles += width // 128
            freed[name] = (proj_ready, tiles)
        freed.update(updn=(up_ready, 8), uprw=(up_ready, 16), out0=(h_ready, 3), out1=(h_ready, 6),
                     wq0=(query_ready, 4), wq1=(query_ready, 8), wq2=(query_ready, 12))

        FILL = [(name, f) for name in ("g1", "g2") for f in range(4)]

        block = ctx.enter_context(nc.Block())

        @block.sync
        def _(sp):
            sp.dma_start(xtok[:, 0, :], x_prompt[0, 0:128]).then_inc(x_in, 16)
            sp.dma_start(xtok[:, 1, :], x_prompt[0, 128:256]).then_inc(x_in, 16)
            sp.dma_start(xtok[0:NS, 2, :], x_sample[:, 0]).then_inc(x_in, 16)
            sp.dma_start(xtok[NS:NS + META, 2, :], meta_tokens).then_inc(x_in, 16)
            srcs = {"ln1": ln1, "mu": rw_mu, "w0": rw_w0, "a0": rw_a0, "k_k": rw_k_k, "k_a": rw_k_a, "gn_w": rw_gn_w,
                    "gn_b": rw_gn_b, "dn_norm": dn_norm_w}
            for name, n in PAR:
                if name == "conv":
                    src = dn_conv_w[0].rearrange("j (f p) -> (j f) p", p=128)
                elif name == "r_k":
                    src = rw_r_k[0].rearrange("(f a) n -> f (a n)", a=2)
                else:
                    src = srcs[name][0].rearrange("(f p) -> f p", p=128)
                sp.dma_start(parrow[PAR_AT[name]:PAR_AT[name] + n, :], src).then_inc(par_in, 16)
            sp.dma_start(cconv[0:24, :], cache_dn_conv[0].rearrange("b j n -> (b j) n")).then_inc(small_in, 16)
            sp.dma_start(cshift[0:8, :], cache_rw_shift[0, :, 0]).then_inc(small_in, 16)
            for n, (name, src, slot, width, use) in enumerate(items):
                if name == "updn":
                    emit_sample_rwkv_in(sp)
                    emit_sample_rwkv_out(sp)
                    sp.wait_ge(strw_sent, 32)
                    emit_states_in(sp, range(DH - 1))
                    sp.wait_ge(rw_y, 2 * NCH)
                    sp.wait_ge(rw_yt_used, NCH)
                    emit_states_in(sp, range(DH - 1, DH))
                if use > 0:
                    before = [i[0] for i in items if i[2] == slot][use - 1]
                    sp.wait_ge(*freed[before])
                if name in ("updn", "uprw"):
                    dst = wslot[slot].rearrange("p k n -> p (k n)").rearrange("p (k n) -> p k n", k=4)
                else:
                    dst = wslot[slot][:, :, 0:width]
                sp.dma_start(dst, src).then_inc(w_landed[slot], 16)
                if n == 0:
                    sp.dma_start(lora[0:64, :], rw_w2[0]).then_inc(small_in, 16)
                    sp.dma_start(lora[64:128, :], rw_a2[0]).then_inc(small_in, 16)
                    sp.dma_start(g2w, rw_g2[0]).then_inc(small_in, 16)
                    sp.dma_start(dtb, dn_dt_bias.broadcast_to([128, 4])).then_inc(small_in, 16)
                    sp.dma_start(alog, dn_a_log.broadcast_to([128, 4])).then_inc(small_in, 16)
                    sp.dma_start(wba, wcols(w_in, OBETA, 8)).then_inc(small_in, 16)
                if name == "v":
                    sp.wait_ge(shift_ready.sem, shift_ready.at(4))
                    sp.dma_start(p_shift[0], shift_out[0:1, :]).then_inc(shift_sent, 16)
                    sp.dma_start(s_shift[0, :, 0], shift_out[1:9, :]).then_inc(shift_sent, 16)
                    sp.dma_start(s_conv[0, :, 0:2], cache_dn_conv[0, :, 1:3]).then_inc(out_dma, 16)
                    sp.wait_ge(conv_ready.sem, conv_ready.at(3))
                    sp.dma_start(p_conv[0, 0], conv_out[0:3, :]).then_inc(conv_sent, 16)
                    sp.dma_start(s_conv[0, :, 2], conv_out[3:11, :]).then_inc(conv_sent, 16)
                if name == "updn":
                    emit_x_again(sp)
                if name == "uprw":
                    emit_state_outputs(sp)
                if name == "out0":
                    sp.dma_start(keysT, peer_keys[0].rearrange("h s n c -> n (h s) c")).then_inc(keys_in, 16)
                if name == "out1":
                    emit_norm_rows(sp)
                if name == "wq1":
                    emit_sample_states(sp)
            emit_peer_io(sp)

        @block.gpsimd
        def _(pool):
            step = Steps(pool, pool_step)
            for t, v in ((ones, 1.0), (ident, 0.0), (halves, 0.0), (incl, 1.0), (strict, 1.0),
                         (level, 0.0), (reset, 1.0), (ba, 0.0), (prw[:, :, 0:1 + PAD], 0.0),
                         (pre[:, :, 0:3 + PAD], 0.0), (xnT[:, :, 0:PAD], 0.0)):
                step(nc.gpsimd.memset(t, v))
            step(nc.gpsimd.memset(eps[:, 0:1], 1e-6))
            step(nc.gpsimd.memset(eps[:, 1:2], DK * 1e-6))
            step(nc.gpsimd.memset(eps[:, 2:3], 64e-5))
            step.sync()
            step(nc.gpsimd.affine_select(out=ident, in_=ident, pattern=[[-1, 128]], compare_op=ALU.not_equal,
                                         fill=1.0, base=0, channel_multiplier=1))
            step.sync()
            step(nc.gpsimd.memset(halves[0:64, 0:64], 1.0))
            step.sync()
            step(nc.gpsimd.memset(halves[64:128, 64:128], 1.0))
            step.sync()
            step(nc.gpsimd.affine_select(out=incl, in_=incl, pattern=[[1, TC]], compare_op=ALU.is_ge, fill=0.0,
                                         base=0, channel_multiplier=-1))
            step(nc.gpsimd.affine_select(out=strict, in_=strict, pattern=[[1, TC]], compare_op=ALU.is_gt, fill=0.0,
                                         base=0, channel_multiplier=-1))
            for c in range(NCH):
                step(nc.gpsimd.memset(reset[:, c * TC:c * TC + 1], 0.0))
            odd = []
            for l in range(LEVELS + 1):
                b = 1 << l
                if TC % (2 * b) == 0:
                    odd.append((level[:, l, :].rearrange("p (m s r) -> p m s r", s=2, r=b)[:, :, 1, :], b, TC // (2 * b)))
                else:
                    n = min(b, TC - b)
                    odd.append((level[:, l, b:b + n].rearrange("p (m r) -> p m r", m=1), b, 1))
            for v, b, m in odd:
                step(nc.gpsimd.memset(v, 1.0))
            step.sync()
            for v, b, m in odd:
                step(nc.gpsimd.affine_select(out=v, in_=v, pattern=[[-2 * b, m], [0, v.shape[2]]],
                                             compare_op=ALU.is_ge, fill=0.0, base=0, channel_multiplier=1))
            step.sync()
            for v, b, m in odd:
                step(nc.gpsimd.affine_select(out=v, in_=v, pattern=[[2 * b, m], [0, v.shape[2]]],
                                             compare_op=ALU.is_ge, fill=0.0, base=b - 1, channel_multiplier=-1))
            step.sync()
            nc.gpsimd.memset(gtmp, 0.0).then_inc(consts, 1)
            sample_rwkv(pool, step)
            pool_peer(pool, step)

        @block.tensor
        def _(pe):
            def mm(out, lhsT, rhs, start=True, stop=True, **kw):
                return nc.tensor.matmul(out, lhsT, rhs, start=start, stop=stop, **kw)

            pe.wait_ge(consts, 1)
            for i, n in enumerate(TILE_ROWS):
                pe.wait_ge(xs_ready, i + 1)
                for half in range(2):
                    for q in range(4):
                        k = 4 * half + q
                        ins = nc.tensor.transpose(psv(2 * i + half, 128, 4, 128)[:, q, 0:n],
                                                  xs[0:n, i, k * 128:(k + 1) * 128], ident[0:n, 0:n])
                    ins.then_inc(xT_t, 1)
                if i == 0:
                    pe.wait_ge(par_in, 16 * len(PAR))
                    nc.tensor.transpose(psv(6, 128, PAR_ROWS), parrow[0:PAR_ROWS, :],
                                        ident[0:PAR_ROWS, 0:PAR_ROWS]).then_inc(par_t.sem, 1)
                    pe.wait_ge(small_in, 16 * 8)
                    for f in range(12):
                        nc.tensor.transpose(psv(7, 128, 24, at=24 * f), cconv[0:24, f * 128:(f + 1) * 128],
                                            ident[0:24, 0:24])
                    for f in range(14):
                        ins = nc.tensor.transpose(psv(7, 128, 8, at=288 + 8 * f), cshift[0:8, f * 128:(f + 1) * 128],
                                                  ident[0:8, 0:8])
                    ins.then_inc(cache_t.sem, 1)

            tile = [0]

            def project(name, first=PAD, banks=0, part=(0, 4)):
                slot = wait_w(pe, name)
                for f in range(part[0], min(part[1], place[name][3] // 128)):
                    b = banks + tile[0] % 4
                    if tile[0] >= 4:
                        pe.wait_ge(proj_used, tile[0] - 3)
                    for k in range(KT):
                        ins = mm(psv(b, 128, NC - first), wslot[slot][:, k, f * 128:(f + 1) * 128], xnT[:, k, first:NC],
                                 start=k == 0, stop=k == KT - 1)
                    ins.then_inc(proj_ready, 1)
                    tile[0] += 1

            pe.wait_ge(xT_done, 8)
            for name in ("r", "kr", "vr", "wag"):
                project(name)
            for c in range(NCH + 1):
                cols, n = (ccols(c), TC) if c < NCH else (slice(NP, NC), NS)
                for k in range(KT):
                    ins = mm(psv(4, n, 8, at=8 * c), xnT[:, k, cols], wba[:, k, :], start=k == 0, stop=k == KT - 1)
            ins.then_inc(ba_ready.sem, 1)
            pe.wait_ge(ba_used.sem, ba_used.at(1))
            pe.wait_ge(proj_used, 14)
            for f in range(14):
                ins = nc.tensor.transpose(psv(4 + f // 4, 9, 128, at=128 * (f % 4)), prw[:, f, NP:NP + 9], ident)
                if f % 4 == 3 or f == 13:
                    ins.then_inc(shift_t.sem, 1)
            project("q")
            pe.wait_ge(shift_ready.sem, shift_ready.at(4))
            pe.wait_ge(wag_act.sem, wag_act.at(2))
            for n in range(12):
                if n >= 4:
                    pe.wait_ge(lora_used.sem, lora_used.at(n - 3))
                f = n % 4
                w = (lora[0:64], lora[64:128], g2w)[n // 4][:, f * 128:(f + 1) * 128]
                x = (mix[0:64, 12, :], mix[64:128, 12, :], mix[:, 13, :])[n // 4]
                mm(psv(4 + f, 128, NC), w, x).then_inc(lora_ready.sem, 1)
            project("k")
            pe.wait_ge(lora_used.sem, lora_used.at(12))
            for f in range(4):
                pe.wait_ge(kksq_ready.sem, kksq_ready.at(1))
                mm(psv(4 + f, 128, NC), halves, t0[:, f, :]).then_inc(norm_ready.sem, 1)
            for f in range(4):
                pe.wait_ge(norm_used.sem, norm_used.at(f + 1))
                pe.wait_ge(bonus_in, 1)
                mm(psv(4 + f, 128, NC), halves, t2[:, f, :]).then_inc(bonus_sum.sem, 1)
            project("v")
            pe.wait_ge(bonus_done, 4)
            pe.wait_ge(proj_used, 26)
            for f in range(12):
                ins = nc.tensor.transpose(psv(4 + f // 4, 11, 128, at=128 * (f % 4)), pre[:, f, NP:NP + 11], ident)
                if f % 4 == 3:
                    ins.then_inc(conv_t.sem, 1)
            for c in range(NCH):
                for f in range(4):
                    ins = nc.tensor.transpose(psv(c, TC, 128, at=128 * f), mix[:, 8 + f, ccols(c)], ident)
                ins.then_inc(vtok_t.sem, 1)
            pe.wait_ge(conv_ready.sem, conv_ready.at(3))
            pe.wait_ge(vtok_ready.sem, vtok_ready.at(3))
            project("z", T0, banks=4)
            pe.wait_ge(qk_sq.sem, qk_sq.at(1))
            for f in range(8):
                if f == 4:
                    pe.wait_ge(proj_used, 30)
                mm(psv(f, 128, NC), ones, sqb[:, f, :]).then_inc(qk_sum.sem, 1)
            pe.wait_ge(g_ready, 1)
            pe.wait_ge(qk_root.sem, qk_root.at(8))
            gcols = gt[0:TC, 0:3, :]
            mm(psv(0, TC, 3, 4), incl[0:TC, :], gcols)
            mm(psv(0, 128, 3, 4, at=16), ones[0:TC, :], gcols).then_inc(gsum_ready.sem, 1)
            project("g0", T0, banks=4, part=(0, 2))
            pe.wait_ge(gb_in, 1)
            for c in range(NCH):
                for h in range(DH):
                    ins = mm(psv(1 + c, 128, TC, at=TC * h), gbc[0:TC, 4 * c + h, :], incl[0:TC, :])
                ins.then_inc(gb_ready.sem, 1)
            project("g0", T0, banks=4, part=(2, 4))
            pe.wait_ge(proj_used, 34)
            pe.wait_ge(qk_done, 1)
            pe.wait_ge(dec_exp.sem, dec_exp.at(2 * NCH))
            for n in range(6):
                c, hp = n // 2, n % 2
                for s in range(2):
                    h = 2 * hp + s
                    ins = mm(psv(n, TC, 2, TC, at=2 * TC * s), qkv[:, 4 + h, ccols(c)], qkv[:, h:h + 5:4, ccols(c)])
                ins.then_inc(kq_ready.sem, 1)
            for n in range(6):
                if n >= 2:
                    pe.wait_ge(tok_ready.sem, tok_ready.at(n - 1))
                c, kv = n // 2, n % 2
                for f in range(4):
                    ins = nc.tensor.transpose(psv(6 + kv, TC, 128, at=128 * f), qkv[:, 4 + 4 * kv + f, ccols(c)], ident)
                ins.then_inc(tok_t.sem, 1)
            pe.wait_ge(tok_ready.sem, tok_ready.at(6))
            pe.wait_ge(rw_vec_ready, 1)
            for n in range(6):
                if n >= 2:
                    pe.wait_ge(prw_ready.sem, prw_ready.at(n - 1))
                c, src = n // 2, (bb, kb)[n % 2]
                for f in range(4):
                    ins = nc.tensor.transpose(psv(6 + n % 2, TC, 128, at=128 * f), src[:, f, ccols(c)], ident)
                ins.then_inc(prw_t.sem, 1)

            def rw_matrix(b, src, g, c, par):
                for s in range(2):
                    f = 2 * g + s
                    rows = slice(64 * par, 64 * par + 64)
                    ins = mm(psv(b, TC, 2, TC, at=2 * TC * s), src[rows, f, ccols(c)], ar[rows, f, :, ccols(c)])
                return ins

            pe.wait_ge(kq_used, 6)
            for n in range(12):
                if n >= 6:
                    pe.wait_ge(rwm_used, n - 5)
                rw_matrix(n % 6, kb, n // 6, n % 6 // 2, n % 2).then_inc(rwm_ready.sem, 1)
            pe.wait_ge(rwm_used, 12)
            pe.wait_ge(prw_ready.sem, prw_ready.at(6))
            fill = FILL[:]

            def fill_half(half):
                if not fill:
                    return
                name, f = fill[0]
                slot = wait_w(pe, name)
                t = tile[0]
                if half == 0:
                    pe.wait_ge(proj_used, t - 1)
                for k in range(4 * half, 4 * half + 4):
                    ins = mm(psv(6 + t % 2, 128, NX), wslot[slot][:, k, f * 128:(f + 1) * 128], xnT[:, k, T0:NC],
                             start=k == 0, stop=k == KT - 1)
                if half == 1:
                    ins.then_inc(proj_ready, 1)
                    tile[0] += 1
                    fill.pop(0)

            for g in range(3):
                if g > 0:
                    for n in range(6):
                        pe.wait_ge(inv_z_used, 18 * g)
                        rw_matrix(n, bb, g - 1, n // 2, n % 2).then_inc(rwb_ready, 1)
                    pe.wait_ge(rwb_used, 6 * g)
                for l in range(LEVELS + 1):
                    for s in range(3):
                        n = (g * LEVELS + l - 1) * 3 + s
                        if l >= 1:
                            pe.wait_ge(inv_c, g * LEVELS + l)
                            pe.wait_ge(inv_x_used, (g * LEVELS + l - 1) * 3 + s + 1)
                            for q in range(4):
                                m = 4 * s + q
                                ins = mm(psv(s, TC, TC, at=TC * q), ct[0:TC, m, :], xx[0:TC, m, :])
                            ins.then_inc(inv_y, 1)
                    for s in range(3):
                        n = (g * LEVELS + l - 1) * 3 + s
                        if l >= 1:
                            pe.wait_ge(inv_y_used, n + 1)
                            for q in range(4):
                                m = 4 * s + q
                                ins = mm(psv(3 + s, TC, TC, at=TC * q), yy[0:TC, m, :], xT[0:TC, 12 * g + m, :])
                            ins.then_inc(inv_z, 1)
                    if 1 <= l < LEVELS:
                        fill_half(0)
                    for s in range(3):
                        n = (g * LEVELS + l - 1) * 3 + s
                        if l < LEVELS:
                            nx = (g * LEVELS + l) * 3 + s
                            if l == 0:
                                pe.wait_ge(inv_first, g + 1)
                            else:
                                pe.wait_ge(inv_z_used, n + 1)
                            for q in range(4):
                                ins = nc.tensor.transpose(psv(s, TC, TC, at=TC * q),
                                                          xT[0:TC, 12 * g + 4 * s + q, :], ident[0:TC, 0:TC])
                            ins.then_inc(inv_x, 1)
                    if 1 <= l < LEVELS:
                        fill_half(1)
            assert not fill
            pe.wait_ge(proj_used, 42)
            for x in range(6):
                if x >= 2:
                    pe.wait_ge(svt_ready.sem, svt_ready.at(x - 1))
                for f in range(4):
                    ins = nc.tensor.transpose(psv(6 + x % 2, NS, 128, at=128 * f), sv[:, x, f, :], ident)
                ins.then_inc(svt_t, 1)
            pe.wait_ge(inv_z_used, 18 * 3)
            pe.wait_ge(svt_ready.sem, svt_ready.at(6))

            for c in range(NCH):
                def xTm(m):
                    return xT[0:TC, m, :]
                if c > 0:
                    pe.wait_ge(dn_s_done, c)
                    for h in range(DH):
                        ins = mm(psv(0, TC, 128, at=128 * h), qkh[:, 4 + h, ccols(c)], s_dn_p[:, 128 * h:128 * h + 128])
                    ins.then_inc(dn_r, 1)
                    pe.wait_ge(rw_s_done, c)
                    pe.wait_ge(rw_yt_used, c)
                for h in range(RH):
                    rows, f, m = slice(64 * (h % 2), 64 * (h % 2) + 64), h // 2, 12 * (h // 4) + 4 * c + h % 4
                    out = psv(4 + h % 2, TC, 64, at=64 * f)
                    if c > 0:
                        mm(out, ar[rows, f, 0, ccols(c)], s_rw_p[rows, f, :], stop=False)
                    ins = mm(out, akT[0:TC, m, :], v_rw[0:TC, c, 64 * h:64 * h + 64], start=c == 0)
                ins.then_inc(rw_r, 1)
                pe.wait_ge(dn_r_done, c + 1)
                for h in range(DH):
                    ins = mm(psv(1, TC, 128, at=128 * h), xTm(4 * c + h), r_buf[0:TC, 128 * h:128 * h + 128])
                ins.then_inc(dn_u, 1)
                pe.wait_ge(rw_r_done, 2 * c + 2)
                if c > 0:
                    pe.wait_ge(rw_u_done, c)
                for h in range(RH):
                    m = 12 + 12 * (h // 4) + 4 * c + h % 4
                    ins = mm(psv(6, TC, 64, at=64 * h), xTm(m), r_bufw[0:TC, 64 * h:64 * h + 64])
                ins.then_inc(rw_u, 1)
                pe.wait_ge(dn_u_done, c + 1)
                for h in range(DH):
                    ins = mm(psv(3, 128, 128, at=128 * h), k_dn[0:TC, c, 128 * h:128 * h + 128],
                             u_buf[0:TC, 128 * h:128 * h + 128])
                ins.then_inc(dn_s, 1)
                if c > 0:
                    pe.wait_ge(dn_ot_used, c)
                for h in range(DH):
                    out = psv(2, TC, 128, at=128 * h)
                    if c > 0:
                        mm(out, qkh[:, h, ccols(c)], s_dn_p[:, 128 * h:128 * h + 128], stop=False)
                    ins = mm(out, qkd[0:TC, 4 * c + h, :], u_buf[0:TC, 128 * h:128 * h + 128], start=c == 0)
                ins.then_inc(dn_o, 1)
                pe.wait_ge(rw_u_done, c + 1)
                for h in range(RH):
                    hs = slice(64 * h, 64 * h + 64)
                    out = psv(7, 128, 64, at=64 * (h // 2))[64 * (h % 2):64 * (h % 2) + 64, :]
                    mm(out, b_rw[0:TC, c, hs], u_bufw[0:TC, hs], stop=False)
                    ins = mm(out, k_rw[0:TC, c, hs], v_rw[0:TC, c, hs], start=False)
                ins.then_inc(rw_s, 1)
                for par in range(2):
                    for h in range(par, RH, 2):
                        hs = slice(64 * h, 64 * h + 64)
                        rows, f, m = slice(64 * par, 64 * par + 64), h // 2, 12 * (h // 4) + 4 * c + h % 4
                        out = psv(4 + par, TC, 64, at=64 * f)
                        if c > 0:
                            mm(out, ar[rows, f, 1, ccols(c)], s_rw_p[rows, f, :], stop=False)
                        mm(out, rbT[0:TC, m, :], u_bufw[0:TC, hs], start=c == 0, stop=False)
                        ins = mm(out, rkT[0:TC, m, :], v_rw[0:TC, c, hs], start=False)
                    ins.then_inc(rw_y, 1)
                pe.wait_ge(dn_on, c + 1)
                for h in range(DH):
                    ins = nc.tensor.transpose(psv(2, 128, TC, at=TC * h), on_o[0:TC, 128 * h:128 * h + 128],
                                              ident[0:TC, 0:TC])
                ins.then_inc(dn_ot, 1)
                pe.wait_ge(rw_yn, c + 1)
                for f in range(4):
                    ins = nc.tensor.transpose(psv(4, 128, TC, at=TC * f), yw_o[0:TC, 128 * f:128 * f + 128],
                                              ident[0:TC, 0:TC])
                ins.then_inc(rw_yt, 1)
            pe_rest(pe, mm, project)

        @block.scalar
        def _(act):
            step = Steps(act, act_step)

            def fn(out, in_, func=ACT.Copy, **kw):
                return nc.scalar.activation(out, in_, func, **kw)

            act.wait_ge(x_in, 64)
            act.wait_ge(consts, 1)
            for i, n in enumerate(TILE_ROWS):
                step(fn(xs[0:n, i, :], xtok[0:n, i, :], ACT.Square, accum_out=ss[0:n, i:i + 1]))
            for i, n in enumerate(TILE_ROWS):
                step.sync(2 - i)
                fn(rs[0:n, i:i + 1], ss[0:n, i:i + 1], ACT.Sqrt, scale=1.0 / D,
                   bias=eps[0:n, 0:1]).then_inc(rs_ready, 1)
            act.wait_ge(par_t.sem, par_t.at(1))
            fn(par, psv(6, 128, PAR_ROWS)).then_inc(par_ready.sem, 1)
            act.wait_ge(cache_t.sem, cache_t.at(1))
            fn(cconvT.rearrange("p f c -> p (f c)"), psv(7, 128, 288)).then_inc(cache_ready.sem, 1)
            fn(cshiftT.rearrange("p f c -> p (f c)"), psv(7, 128, 112, at=288)).then_inc(cache_ready.sem, 1)
            tile = [0]

            def evacuate(dests, func=ACT.Copy, n=NC - PAD, banks=0):
                for d in dests:
                    act.wait_ge(proj_ready, tile[0] + 1)
                    fn(d, psv(banks + tile[0] % 4, 128, n), func).then_inc(proj_used, 1)
                    tile[0] += 1

            evacuate([prw[:, f, 1 + PAD:1 + NC] for f in range(14)])
            act.wait_ge(ba_ready.sem, ba_ready.at(1))
            step(fn(ba[0:TC, 0:3, :], psv(4, TC, 3, 8)))
            fn(ba[0:NS, 3, :], psv(4, NS, 8, at=24)).then_inc(ba_used.sem, 1)
            act.wait_ge(par2_ready, 1)
            act.wait_ge(proj_used, 14)
            for f in range(14):
                fn(mix[:, f, 0:NP], prw[:, f, 1:1 + NP], scale=omu[:, f:f + 1]).then_inc(mix_part.sem, 1)
            for b in range(4):
                act.wait_ge(shift_t.sem, shift_t.at(b + 1))
                n = 512 if b < 3 else 256
                fn(shift_out[0:9, 512 * b:512 * b + n], psv(4 + b, 9, n)).then_inc(shift_ready.sem, 1)
            act.wait_ge(mix_ready, 1)
            fn(mix[0:64, 12, :], mix[0:64, 12, :], ACT.Tanh).then_inc(wag_act.sem, 1)
            fn(mix[:, 13, :], mix[:, 13, :], ACT.Sigmoid).then_inc(wag_act.sem, 1)
            evacuate([pre[:, f, 3 + PAD:3 + NC] for f in range(4)])
            for n in range(12):
                f = n % 4
                act.wait_ge(lora_ready.sem, lora_ready.at(n + 1))
                p = psv(4 + f, 128, NC)
                if n < 4:
                    ins = fn(ld[:, f, :], p, ACT.Sigmoid, bias=par[:, PAR_AT["w0"] + f:PAR_AT["w0"] + f + 1])
                elif n < 8:
                    ins = fn(aa[:, f, :], p, ACT.Sigmoid, bias=par[:, PAR_AT["a0"] + f:PAR_AT["a0"] + f + 1])
                else:
                    ins = fn(gate[:, f, :], p)
                ins.then_inc(lora_used.sem, 1)
            act.wait_ge(kk0_ready, 1)
            act.wait_ge(shift_t.sem, shift_t.at(4))
            fn(t0, kk, ACT.Square).then_inc(kksq_ready.sem, 1)
            evacuate([pre[:, 4 + f, 3 + PAD:3 + NC] for f in range(4)])
            for f in range(4):
                act.wait_ge(norm_ready.sem, norm_ready.at(f + 1))
                fn(t1[:, f, :], psv(4 + f, 128, NC), ACT.Sqrt, bias=eps[:, 0:1]).then_inc(norm_used.sem, 1)
            act.wait_ge(cum_ready, 2)
            act.wait_ge(norm_ready.sem, norm_ready.at(4))
            fn(t0[:, :, 0:NP], cum[:, :, 0:NP], ACT.Exp).then_inc(exp_ready.sem, 1)
            fn(t1[:, :, 0:NP], cum[:, :, 0:NP], ACT.Exp, scale=-1.0).then_inc(exp_ready.sem, 1)
            fn(t2[:, :, 0:NP], t2[:, :, 0:NP], ACT.Exp).then_inc(exp_ready.sem, 1)
            fn(sv[:, 1, :, :], ld[:, :, NP:NC], ACT.Exp).then_inc(exp_ready.sem, 1)
            evacuate([pre[:, 8 + f, 3 + PAD:3 + NC] for f in range(4)])
            act.wait_ge(proj_used, 26)
            act.wait_ge(par_t.sem, par_t.at(1))
            for b in range(3):
                act.wait_ge(conv_t.sem, conv_t.at(b + 1))
                fn(conv_out[0:11, 512 * b:512 * b + 512], psv(4 + b, 11, 512)).then_inc(conv_ready.sem, 1)
            act.wait_ge(rw_vec_ready, 1)
            for c in range(NCH):
                act.wait_ge(vtok_t.sem, vtok_t.at(c + 1))
                fn(v_rw[0:TC, c, :], psv(c, TC, 512)).then_inc(vtok_ready.sem, 1)
            act.wait_ge(vtok_ready.sem, vtok_ready.at(3))
            for f in range(12):
                w = par[:, PAR_AT["conv"] + 36 + f:PAR_AT["conv"] + 37 + f]
                fn(qkv[:, f, 0:NP], pre[:, f, 3:3 + NP], scale=w).then_inc(tap_ready.sem, 1)
            act.wait_ge(conv_done, 1)
            for i in range(3):
                fn(qkv[:, 4 * i:4 * i + 4, :], qkv[:, 4 * i:4 * i + 4, :], ACT.Silu).then_inc(silu_done.sem, 1)
            act.wait_ge(silu_done.sem, silu_done.at(2))
            fn(sqb, qkv[:, 0:8, :], ACT.Square).then_inc(qk_sq.sem, 1)
            evacuate(zs, ACT.Silu, NX, banks=4)
            for f in range(8):
                act.wait_ge(qk_sum.sem, qk_sum.at(f + 1))
                fn(rnb[:, f, :], psv(f, 128, NC), ACT.Sqrt, scale=float(DK) if f < 4 else 1.0,
                   bias=eps[:, 1:2] if f < 4 else eps[:, 0:1]).then_inc(qk_root.sem, 1)
            act.wait_ge(ln_done, 1)
            step(fn(gtmp, gtmp, ACT.Exp, scale=-1.0))
            step.sync()
            step(fn(gtmp, gtmp, ACT.Ln, bias=1.0))
            step(fn(bt, ba[:, :, 0:4], ACT.Exp, scale=-1.0))
            fn(alog, alog, ACT.Exp).then_inc(ln_done, 1)
            act.wait_ge(gb_in, 1)
            step(fn(gend, psv(0, 128, 3, 4, at=16), ACT.Exp))
            fn(gout[0:TC], gout[0:TC], ACT.Exp).then_inc(gexp_done.sem, 1)
            for c in range(NCH):
                act.wait_ge(gb_ready.sem, gb_ready.at(c + 1))
                act.wait_ge(dec_in, c + 1)
                fn(edec[:, 4 * c:4 * c + 4, :], psv(1 + c, 128, 4, TC), ACT.Exp).then_inc(dec_exp.sem, 1)
                fn(dec[0:TC, 4 * c:4 * c + 4, :], dec[0:TC, 4 * c:4 * c + 4, :], ACT.Exp).then_inc(dec_exp.sem, 1)
            evacuate([gates(f) for f in range(4)], ACT.Sigmoid, NX, banks=4)
            act.wait_ge(gexp_done.sem, gexp_done.at(1))
            act.wait_ge(dec_ready, 1)
            for n in range(6):
                act.wait_ge(tok_t.sem, tok_t.at(n + 1))
                c = n // 2
                if n % 2 == 0:
                    for h in range(DH):
                        ins = fn(k_dn[0:TC, c, 128 * h:128 * h + 128], psv(6, TC, 128, at=128 * h),
                                 scale=gout[0:TC, c, h:h + 1])
                        if h < DH - 1:
                            step(ins)
                else:
                    ins = fn(v_dn[0:TC, c, :], psv(7, TC, 512))
                ins.then_inc(tok_ready.sem, 1)
            act.wait_ge(shift_sent, 32)
            for n in range(6):
                act.wait_ge(prw_t.sem, prw_t.at(n + 1))
                fn((b_rw, k_rw)[n % 2][0:TC, n // 2, :], psv(6 + n % 2, TC, 512)).then_inc(prw_ready.sem, 1)
            for g in range(3):
                for l in range(LEVELS + 1):
                    for s in range(3):
                        if l >= 1:
                            act.wait_ge(inv_y, (g * LEVELS + l - 1) * 3 + s + 1)
                            fn(yy[0:TC, 4 * s:4 * s + 4, :], psv(s, TC, 4, TC)).then_inc(inv_y_used, 1)
                    for s in range(3):
                        if l < LEVELS:
                            nx = (g * LEVELS + l) * 3 + s
                            act.wait_ge(inv_x, nx + 1)
                            fn(xx[0:TC, 4 * s:4 * s + 4, :], psv(s, TC, 4, TC)).then_inc(inv_x_used, 1)
                    if 1 <= l < LEVELS and tile[0] < 34 + len(FILL):
                        act.wait_ge(proj_ready, tile[0] + 1)
                        fn(gates(tile[0] - 30), psv(6 + tile[0] % 2, 128, NX), ACT.Sigmoid).then_inc(proj_used, 1)
                        tile[0] += 1
            act.wait_ge(inv_z, 18 * 3)
            act.wait_ge(inv_c, 18)
            for x in range(6):
                act.wait_ge(svt_t, x + 1)
                fn(svt[0:NS, :, x, :], psv(6 + x % 2, NS, RH, RN)).then_inc(svt_ready.sem, 1)
            for c in range(NCH):
                for par_ in range(2):
                    act.wait_ge(rw_r, c + 1)
                    src = psv(4 + par_, TC, 4, 64)
                    fn(r_bufw[0:TC].rearrange("p (f s v) -> p f s v", f=4, s=2)[:, :, par_, :], src).then_inc(rw_r_done, 1)
                act.wait_ge(rw_u, c + 1)
                fn(u_bufw[0:TC], psv(6, TC, 512), scale=-1.0).then_inc(rw_u_done, 1)
                act.wait_ge(dn_o, c + 1)
                step(fn(o_buf[0:TC], psv(2, TC, 512)))
                if c > 0:
                    act.wait_ge(dn_on, c)
                fn(sq_o[0:TC], psv(2, TC, 512), ACT.Square).then_inc(dn_o_used, 1)
                act.wait_ge(dn_ss, c + 1)
                fn(stat[0:TC, 4:8], stat[0:TC, 0:4], ACT.Sqrt, scale=1.0 / DK, bias=eps[0:TC, 0:1]).then_inc(dn_root, 1)
                act.wait_ge(rw_c, c + 1)
                fn(sqw_o[0:TC], yw_o[0:TC], ACT.Square).then_inc(rw_sq, 1)
                act.wait_ge(rw_var, c + 1)
                fn(stat[0:TC, 24:32], stat[0:TC, 16:24], ACT.Sqrt, scale=1.0 / RN, bias=eps[0:TC, 2:3]).then_inc(rw_root, 1)
                act.wait_ge(dn_ot, c + 1)
                fn(odn[:, :, ccols(c)], psv(2, 128, 4, TC)).then_inc(dn_ot_used, 1)
                act.wait_ge(rw_yt, c + 1)
                fn(orw[:, :, ccols(c)], psv(4, 128, 4, TC)).then_inc(rw_yt_used, 1)
            act.wait_ge(ssq_ready, 1)
            fn(stat[0:NS, 40:48], stat[0:NS, 32:40], ACT.Sqrt, scale=1.0 / RN, bias=eps[0:NS, 2:3]).then_inc(sroot.sem, 1)
            act_rest(act, step, fn, evacuate)

        @block.vector
        def _(dve):
            step = Steps(dve, vec_step)
            v = nc.vector
            tt, ts, stt = v.tensor_tensor, v.tensor_scalar, v.scalar_tensor_tensor

            def pc(name, f=0, n=1):
                return par[:, PAR_AT[name] + f:PAR_AT[name] + f + n]

            for i, n in enumerate(TILE_ROWS):
                dve.wait_ge(rs_ready, i + 1)
                step(v.reciprocal(rs[0:n, i:i + 1], rs[0:n, i:i + 1]))
                step.sync()
                ts(xs[0:n, i, :], xtok[0:n, i, :], rs[0:n, i:i + 1], None, ALU.mult).then_inc(xs_ready, 1)
            dve.wait_ge(par_ready.sem, par_ready.at(1))
            step(ts(omu, pc("mu", 0, 14), -1.0, 1.0, ALU.mult, ALU.add))
            ts(omka, pc("k_a", 0, 4), -1.0, 1.0, ALU.mult, ALU.add).then_inc(par2_ready, 1)
            for i in range(3):
                for half in range(2):
                    dve.wait_ge(xT_t, 2 * i + half + 1)
                    ks = slice(4 * half, 4 * half + 4)
                    moves = ([(slice(0, 128), slice(T0 + 128 * i, T0 + 128 * i + 128))] if i < 2 else
                             [(slice(0, NS), slice(NP, NC)), (slice(NS, NS + META), slice(PAD, T0))])
                    for a, b in moves:
                        src = psv(2 * i + half, 128, 4, 128)[:, :, a]
                        n = a.stop - a.start
                        tt(xnT[:, ks, b], src, row(pc("ln1", 4 * half, 4), 128, 4, n), ALU.mult).then_inc(xT_done, 1)
            dve.wait_ge(par2_ready, 1)
            for f in range(14):
                dve.wait_ge(mix_part.sem, mix_part.at(f + 1))
                step(stt(mix[:, f, 0:NP], prw[:, f, 0:NP], pc("mu", f), mix[:, f, 0:NP], ALU.mult, ALU.add))
            dve.wait_ge(cache_ready.sem, cache_ready.at(2))
            step(tt(dmix, cshiftT, prw[:, :, 1 + NP:1 + NC], ALU.subtract))
            step.sync()
            step(tt(dmix, dmix, row(pc("mu", 0, 14), 128, 14, 8), ALU.mult))
            step.sync()
            tt(mix[:, :, NP:NC], dmix, prw[:, :, 1 + NP:1 + NC], ALU.add).then_inc(mix_ready, 1)
            mr, mk, mv = mix[:, 0:4, :], mix[:, 4:8, :], mix[:, 8:12, :]
            dve.wait_ge(mix_ready, 1)
            for f in range(4):
                ins = ts(kk[:, f, :], mk[:, f, :], pc("k_k", f), None, ALU.mult)
                if f < 3:
                    step(ins)
            ins.then_inc(kk0_ready, 1)
            dve.wait_ge(lora_used.sem, lora_used.at(4))
            step(ts(ld, ld, -EDEC, None, ALU.mult))
            step.sync()
            for f in range(4):
                step(v.tensor_tensor_scan(cum[:, f, 0:NP], reset, ld[:, f, 0:NP], 0.0, ALU.mult, ALU.add))
            step.sync()
            v.tensor_copy(sv[:, 3], mv[:, :, NP:NC]).then_inc(cum_ready, 1)
            dve.wait_ge(lora_used.sem, lora_used.at(8))
            for f in range(4):
                step(ts(t2[:, f, :], aa[:, f, :], pc("k_a", f), omka[:, f:f + 1], ALU.mult, ALU.add))
            step.sync()
            step(tt(mk, mk, t2, ALU.mult))
            step.sync()
            for f in range(4):
                ins = stt(t2[:, f, :], mk[:, f, :], pc("r_k", f), mr[:, f, :], ALU.mult, ALU.mult)
                if f < 3:
                    step(ins)
            ins.then_inc(bonus_in, 1)
            dve.wait_ge(norm_used.sem, norm_used.at(4))
            step(v.reciprocal(t1, t1))
            step.sync()
            step(tt(kk, kk, t1, ALU.mult))
            for f in range(4):
                dve.wait_ge(bonus_sum.sem, bonus_sum.at(f + 1))
                tt(bonus[:, f, :], psv(4 + f, 128, NC), mv[:, f, :], ALU.mult).then_inc(bonus_done, 1)
            step.sync()
            step(tt(aa, aa, kk, ALU.mult))
            step(tt(t2[:, :, 0:NP], cum[:, :, 0:NP], ld[:, :, 0:NP], ALU.subtract))
            step.sync()
            v.tensor_copy(sv[:, 5], aa[:, :, NP:NC]).then_inc(cum_ready, 1)
            step(v.tensor_copy(sv[:, 0], mr[:, :, NP:NC]))
            step(v.tensor_copy(sv[:, 2], mk[:, :, NP:NC]))
            step(v.tensor_copy(sv[:, 4], kk[:, :, NP:NC]))
            dve.wait_ge(shift_sent, 32)
            dve.wait_ge(exp_ready.sem, exp_ready.at(1))
            step(v.tensor_copy(wc, t0[:, :, TC - 1:NP:TC]))
            step(tt(ar[:, :, 1, :], mr[:, :, 0:NP], t0[:, :, 0:NP], ALU.mult))
            dve.wait_ge(exp_ready.sem, exp_ready.at(2))
            step(tt(bb, aa[:, :, 0:NP], t1[:, :, 0:NP], ALU.mult))
            step(tt(kb, mk[:, :, 0:NP], t1[:, :, 0:NP], ALU.mult))
            dve.wait_ge(exp_ready.sem, exp_ready.at(3))
            tt(ar[:, :, 0, :], kk[:, :, 0:NP], t2[:, :, 0:NP], ALU.mult).then_inc(rw_vec_ready, 1)
            dve.wait_ge(vtok_ready.sem, vtok_ready.at(3))
            cw = [row(pc("conv", 12 * j, 12), 128, 12, 8) for j in range(4)]
            cc = cconvT.rearrange("p f (b j) -> p f b j", j=3)
            dve.wait_ge(proj_used, 26)
            qs = qkv[:, :, NP:NC]
            step(tt(qs, pre[:, :, 3 + NP:3 + NC], cw[3], ALU.mult))
            for j in range(3):
                step.sync()
                step(tt(cst, cc[:, :, :, j], cw[j], ALU.mult))
                step.sync()
                step(tt(qs, qs, cst, ALU.add))
            for j in range(3):
                for f in range(12):
                    if j == 0:
                        dve.wait_ge(tap_ready.sem, tap_ready.at(f + 1))
                    else:
                        step.sync(11)
                    ins = stt(qkv[:, f, 0:NP], pre[:, f, j:j + NP], pc("conv", 12 * j + f), qkv[:, f, 0:NP],
                              ALU.mult, ALU.add)
                    if j == 2 and f == 11:
                        ins.then_inc(conv_done, 1)
                    else:
                        step(ins)
            step(tt(gt, ba[:, :, 4:8], dtb.unsqueeze(1).broadcast_to([128, 4, 4]), ALU.add))
            step.sync()
            step(ts(gtmp, gt, -1.0, None, ALU.mult))
            step.sync()
            tt(gtmp, gtmp, gt, ALU.max).then_inc(ln_done, 1)
            dve.wait_ge(ln_done, 2)
            step(stt(gt, gt, 0.0, gtmp, ALU.max, ALU.add))
            step(ts(bt, bt, 1.0, None, ALU.add))
            step.sync()
            step(v.reciprocal(bt, bt))
            stt(gt, gt, -1.0, alog.unsqueeze(1).broadcast_to([128, 4, 4]), ALU.mult, ALU.mult).then_inc(g_ready, 1)
            dve.wait_ge(qk_root.sem, qk_root.at(8))
            step(v.reciprocal(rnb, rnb))
            step.sync()
            step(tt(qkv[:, 0:8, :], qkv[:, 0:8, :], rnb, ALU.mult))
            dve.wait_ge(silu_done.sem, silu_done.at(3))
            step.sync()
            v.tensor_copy(sd, qkv[:, :, NP:NC]).then_inc(qk_done, 1)
            dve.wait_ge(g_ready, 1)
            dve.wait_ge(gsum_ready.sem, gsum_ready.at(1))
            step(v.tensor_copy(gcum[0:TC], psv(0, TC, 3, 4)))
            step.sync()
            step(v.tensor_copy(gbc[0:TC], gt[0:TC, 0:3, :].rearrange("p c h -> p (c h)").unsqueeze(2).broadcast_to([TC, 12, 128])))
            tt(gout[0:TC], psv(0, TC, 3, 4, at=16), gcum[0:TC], ALU.subtract).then_inc(gb_in, 1)
            gc12 = gcum[0:TC].rearrange("p c h -> p (c h)")
            for c in range(NCH):
                dve.wait_ge(gb_ready.sem, gb_ready.at(c + 1))
                g4 = slice(4 * c, 4 * c + 4)
                step(tt(dec[0:TC, g4, :], psv(1 + c, TC, 4, TC), row(gc12[:, g4], TC, 4, TC), ALU.subtract))
                step.sync()
                ts(dec[0:TC, g4, :], dec[0:TC, g4, :], 0.0, None, ALU.min).then_inc(dec_in, 1)
            dve.wait_ge(dec_exp.sem, dec_exp.at(6))
            dve.wait_ge(conv_sent, 32)
            for c in range(NCH):
                e = edec[:, 4 * c:4 * c + 4, :]
                step(tt(qkh[:, 0:4, ccols(c)], qkv[:, 0:4, ccols(c)], e, ALU.mult))
                step(tt(qkh[:, 4:8, ccols(c)], qkv[:, 4:8, ccols(c)], e, ALU.mult))
            step(tt(dst[0:TC], dec[0:TC], strict[0:TC].unsqueeze(1).broadcast_to([TC, 12, TC]), ALU.mult))
            step.sync()
            tt(dec[0:TC], dec[0:TC], incl[0:TC].unsqueeze(1).broadcast_to([TC, 12, TC]), ALU.mult).then_inc(dec_ready, 1)
            dve.wait_ge(dec_ready, 1)
            for n in range(6):
                dve.wait_ge(kq_ready.sem, kq_ready.at(n + 1))
                c, hp = n // 2, n % 2
                p = psv(n, TC, 2, 2, TC)
                for s in range(2):
                    h = 2 * hp + s
                    step(stt(bT[0:TC, 4 * c + h, :], p[:, s, 1, :], bt[0:TC, c, h:h + 1], dst[0:TC, 4 * c + h, :],
                             ALU.mult, ALU.mult))
                hs = slice(4 * c + 2 * hp, 4 * c + 2 * hp + 2)
                tt(qkd[0:TC, hs, :], p[:, :, 0, :], dec[0:TC, hs, :], ALU.mult).then_inc(kq_used, 1)

            def pair(base, g, n):
                m = 12 * g + 4 * (n // 2) + n % 2
                return base[0:TC, m:m + 3:2, :]

            m_incl = incl[0:TC].unsqueeze(1).broadcast_to([TC, 2, TC])
            m_strict = strict[0:TC].unsqueeze(1).broadcast_to([TC, 2, TC])
            for n in range(12):
                dve.wait_ge(rwm_ready.sem, rwm_ready.at(n + 1))
                p = psv(n % 6, TC, 2, 2, TC)
                step(tt(pair(akT, n // 6, n % 6), p[:, :, 0, :], m_strict, ALU.mult))
                tt(pair(rkT, n // 6, n % 6), p[:, :, 1, :], m_incl, ALU.mult).then_inc(rwm_used, 1)
            for g in range(3):
                if g > 0:
                    for n in range(6):
                        dve.wait_ge(rwb_ready, 6 * (g - 1) + n + 1)
                        p = psv(n, TC, 2, 2, TC)
                        step(tt(pair(bT, 0, n), p[:, :, 0, :], m_strict, ALU.mult))
                        tt(pair(rbT, g - 1, n), p[:, :, 1, :], m_incl, ALU.mult).then_inc(rwb_used, 1)
                xg = xT[0:TC, 12 * g:12 * g + 12, :]
                for l in range(LEVELS + 1):
                    mask = level[0:TC, l, :].unsqueeze(1).broadcast_to([TC, 12, TC])
                    if l == 0:
                        step.sync()
                        step(tt(xg, bT[0:TC], mask, ALU.mult))
                        step.sync()
                        tt(xg, ident[0:TC, 0:TC].unsqueeze(1).broadcast_to([TC, 12, TC]), xg,
                           ALU.subtract).then_inc(inv_first, 1)
                    else:
                        n = (g * LEVELS + l - 1) * 3
                        if n > 0:
                            dve.wait_ge(inv_y, n)
                        tt(ct[0:TC], bT[0:TC], mask, ALU.mult).then_inc(inv_c, 1)
                        for s in range(3):
                            dve.wait_ge(inv_z, n + s + 1)
                            xs4 = xT[0:TC, 12 * g + 4 * s:12 * g + 4 * s + 4, :]
                            tt(xs4, xs4, psv(3 + s, TC, 4, TC), ALU.subtract).then_inc(inv_z_used, 1)
                        if l == 1:
                            dve.wait_ge(inv_first, g + 1)

            for c in range(NCH):
                if c == 0:
                    dve.wait_ge(tok_ready.sem, tok_ready.at(6))
                    v.tensor_copy(r_buf[0:TC], v_dn[0:TC, 0, :]).then_inc(dn_r_done, 1)
                else:
                    dve.wait_ge(dn_r, c)
                    tt(r_buf[0:TC], v_dn[0:TC, c, :], psv(0, TC, 512), ALU.subtract).then_inc(dn_r_done, 1)
                dve.wait_ge(dn_u, c + 1)
                tt(u_buf[0:TC].rearrange("p (h v) -> p h v", h=4), psv(1, TC, 4, 128), row(bt[0:TC, c, :], TC, 4, 128),
                   ALU.mult).then_inc(dn_u_done, 1)
                dve.wait_ge(dn_o, c + 1)
                dve.wait_ge(dn_s, c + 1)
                sp4 = s_dn_p.rearrange("p (h v) -> p h v", h=4)
                if c == 0:
                    v.tensor_copy(s_dn_p, psv(3, 128, 512)).then_inc(dn_s_done, 1)
                else:
                    step(tt(sp4, sp4, row(gend[:, c, :], 128, 4, 128), ALU.mult))
                    step.sync()
                    tt(s_dn_p, s_dn_p, psv(3, 128, 512), ALU.add).then_inc(dn_s_done, 1)
                dve.wait_ge(rw_s, c + 1)
                dve.wait_ge(rw_y, 2 * c + 2)
                if c > 0:
                    step(tt(s_rw_p, s_rw_p, psv(7, 128, 4, 64), ALU.add))
                    step.sync()
                tt(s_rw_p, s_rw_p if c > 0 else psv(7, 128, 4, 64), row(wc[:, :, c], 128, 4, 64),
                   ALU.mult).then_inc(rw_s_done, 1)
                dve.wait_ge(dn_o_used, c + 1)
                v.tensor_reduce(stat[0:TC, 0:4], sq_o[0:TC].rearrange("p (h v) -> p h v", h=4), AX,
                                ALU.add).then_inc(dn_ss, 1)
                for par_ in range(2):
                    step(v.tensor_reduce(stat[0:TC, 8 + par_:16:2], psv(4 + par_, TC, 4, 64), AX, ALU.add))
                step.sync()
                step(ts(stat[0:TC, 8:16], stat[0:TC, 8:16], 1.0 / RN, None, ALU.mult))
                step.sync()
                if c > 0:
                    dve.wait_ge(rw_yt, c)
                yw = yw_o[0:TC].rearrange("p (f s v) -> p f s v", f=4, s=2)
                for par_ in range(2):
                    ins = tt(yw[:, :, par_, :], psv(4 + par_, TC, 4, 64), row(stat[0:TC, 8 + par_:16:2], TC, 4, 64),
                             ALU.subtract)
                    if par_ == 0:
                        step(ins)
                ins.then_inc(rw_c, 1)
                dve.wait_ge(dn_root, c + 1)
                step(v.reciprocal(stat[0:TC, 4:8], stat[0:TC, 4:8]))
                step.sync()
                if c > 0:
                    dve.wait_ge(dn_ot, c)
                tt(on_o[0:TC].rearrange("p (h v) -> p h v", h=4), o_buf[0:TC].rearrange("p (h v) -> p h v", h=4),
                   row(stat[0:TC, 4:8], TC, 4, 128), ALU.mult).then_inc(dn_on, 1)
                dve.wait_ge(rw_sq, c + 1)
                v.tensor_reduce(stat[0:TC, 16:24], sqw_o[0:TC].rearrange("p (h v) -> p h v", h=8), AX,
                                ALU.add).then_inc(rw_var, 1)
                dve.wait_ge(rw_root, c + 1)
                step(v.reciprocal(stat[0:TC, 24:32], stat[0:TC, 24:32]))
                step.sync()
                y8 = yw_o[0:TC].rearrange("p (h v) -> p h v", h=8)
                tt(y8, y8, row(stat[0:TC, 24:32], TC, 8, 64), ALU.mult).then_inc(rw_yn, 1)
            dve.wait_ge(ytok_in, 16 * 16)
            ys = ytok[0:NS].rearrange("p (h v) -> p h v", h=8)
            sq8 = view(I3 + 512, 512)[0:NS].rearrange("p (h v) -> p h v", h=8)
            step(v.tensor_reduce(stat[0:NS, 32:40], ys, AX, ALU.add))
            step.sync()
            step(ts(stat[0:NS, 32:40], stat[0:NS, 32:40], 1.0 / RN, None, ALU.mult))
            step.sync()
            step(tt(ys, ys, row(stat[0:NS, 32:40], NS, 8, 64), ALU.subtract))
            step.sync()
            step(tt(sq8, ys, ys, ALU.mult))
            step.sync()
            v.tensor_reduce(stat[0:NS, 32:40], sq8, AX, ALU.add).then_inc(ssq_ready, 1)
            dve.wait_ge(sroot.sem, sroot.at(1))
            step(v.reciprocal(stat[0:NS, 40:48], stat[0:NS, 40:48]))
            step.sync()
            tt(ys, ys, row(stat[0:NS, 40:48], NS, 8, 64), ALU.mult).then_inc(syt_ready, 1)
            vec_rest(dve, step, v, tt, ts, stt, pc)


_INS = ["x_prompt", "x_sample", "cache_dn_conv", "state_dn", "cache_rw_shift", "state_rw", "meta_tokens", "ln1", "w_in",
        "dn_conv_w", "dn_a_log", "dn_dt_bias", "dn_norm_w", "rw_mu", "rw_w0", "rw_w2", "rw_a0", "rw_a2", "rw_g2",
        "rw_k_k", "rw_k_a", "rw_r_k", "rw_gn_w", "rw_gn_b", "w_up_dn", "w_up_rw", "w_out", "ln2", "peer_wq",
        "peer_keys", "peer_u", "peer_v", "ln_f"]
_OUTS = [(1, 256, 1024), (8, 1, 1024), (1, 1, 3, 1536), (1, 1, 4, 128, 128), (1, 1, 1, 1792), (1, 1, 8, 64, 64),
         (1, 8, 3, 1536), (1, 8, 4, 128, 128), (1, 8, 1, 1792), (1, 8, 8, 64, 64)]


def kernel(**inputs):
    import numpy as _np
    import concourse.bacc as _bacc
    from concourse import mybir as _mybir
    from concourse.bass_utils import run_bass_kernel_spmd as _run

    nc = _bacc.Bacc("TRN2", target_bir_lowering=False, num_devices=1)
    arrays, args = {}, []
    for name in _INS:
        a = _np.ascontiguousarray(inputs[name])
        arrays[f"in_{name}"] = a
        args.append(nc.dram_tensor(f"in_{name}", a.shape, _mybir.dt.from_np(a.dtype), kind="ExternalInput").ap())
    for i, shape in enumerate(_OUTS):
        args.append(nc.dram_tensor(f"out_{i}", shape, _mybir.dt.float32, kind="ExternalOutput").ap())
    hybrid_step(nc, *args)
    r = _run(nc, [arrays], core_ids=[0])
    return tuple(r.results[0][f"out_{i}"] for i in range(len(_OUTS)))
```
